# Optimizing a Trainium2 kernel written in Bass

```python
import math
import jax, jax.numpy as jnp
from jax import lax
import numpy as np

D_MODEL = 1024
BATCH = 1
SEQ = 512
DEPTH = 1

HEAD_DIM = 64
FOX_HEADS = 8
NSA_HEADS = 8
NSA_KV_GROUPS = 2
NSA_REP = NSA_HEADS // NSA_KV_GROUPS
CMP_BLOCK = 32
CMP_STRIDE = 16
CMP_HIDDEN = 256
SLC_BLOCK = 64
SLC_TOPK = 16
WINDOW = 512
Q_BLOCK = 128
REL_BUCKETS = 32
REL_MAX_DIST = 128
D_FF = 4 * D_MODEL
RMS_EPS = 1e-6
NEG_INF = -1e30
FORCED_SCORE = 1e4
SCALE = HEAD_DIM ** -0.5

FOX_W = FOX_HEADS * HEAD_DIM
NSA_W = NSA_HEADS * HEAD_DIM
KV_W = NSA_KV_GROUPS * HEAD_DIM
IN_SPLITS = (FOX_W, FOX_W, FOX_W, FOX_HEADS,
             NSA_W, KV_W, KV_W, KV_W, KV_W, KV_W, KV_W, 3 * NSA_HEADS,
             D_MODEL, D_MODEL)
IN_WIDTH = sum(IN_SPLITS)


def rms_norm(x, g):
    xf = x.astype(jnp.float32)
    y = xf * lax.rsqrt(jnp.mean(xf * xf, axis=-1, keepdims=True) + RMS_EPS)
    return (y * g.astype(jnp.float32)).astype(x.dtype)

def masked_softmax(s, mask):
    p = jax.nn.softmax(jnp.where(mask, s, NEG_INF), axis=-1)
    return jnp.where(mask, p, 0.0)

def rel_bucket(dist):
    n = jnp.maximum(dist, 0)
    exact = REL_BUCKETS // 2
    nf = jnp.maximum(n, exact).astype(jnp.float32)
    log_b = exact + (jnp.log(nf / exact) / math.log(REL_MAX_DIST / exact)
                     * (REL_BUCKETS - exact)).astype(jnp.int32)
    return jnp.where(n < exact, n, jnp.minimum(log_b, REL_BUCKETS - 1))

def fox_attention(q, k, v, f_logit, b_f):
    B, T, H, DH = q.shape
    nb = T // Q_BLOCK
    log_f = jax.nn.log_sigmoid(f_logit.astype(jnp.float32) + b_f.astype(jnp.float32))
    c = jnp.cumsum(log_f, axis=1).transpose(0, 2, 1)
    qb = q.reshape(B, nb, Q_BLOCK, H, DH).transpose(1, 0, 3, 2, 4)
    cqb = c.reshape(B, H, nb, Q_BLOCK).transpose(2, 0, 1, 3)
    kpos = jnp.arange(T)

    def block(args):
        i, qi, ci = args
        qpos = i * Q_BLOCK + jnp.arange(Q_BLOCK)
        s = jnp.einsum('bhqd,bkhd->bhqk', qi, k).astype(jnp.float32) * SCALE
        s = s + ci[..., None] - c[:, :, None, :]
        p = masked_softmax(s, kpos[None, :] <= qpos[:, None])
        return jnp.einsum('bhqk,bkhd->bqhd', p.astype(v.dtype), v)

    o = lax.map(block, (jnp.arange(nb), qb, cqb))
    return o.transpose(1, 0, 2, 3, 4).reshape(B, T, H * DH)

def compress_blocks(kv, pe, w1, w2):
    B, T, G, DH = kv.shape
    nc = (T - CMP_BLOCK) // CMP_STRIDE + 1
    idx = np.arange(nc)[:, None] * CMP_STRIDE + np.arange(CMP_BLOCK)[None, :]
    blk = kv[:, idx] + pe[:, None, :]
    blk = blk.transpose(0, 3, 1, 2, 4).reshape(B, G, nc, CMP_BLOCK * DH)
    return jax.nn.silu(blk @ w1) @ w2

def nsa_attention(q, k_cmp, v_cmp, k_slc, v_slc, k_win, v_win, gate_logit, rel_table,
                  pe_k, w1_k, w2_k, pe_v, w1_v, w2_v):
    B, T, H, DH = q.shape
    G, R = NSA_KV_GROUPS, NSA_REP
    nb = T // Q_BLOCK
    nc = (T - CMP_BLOCK) // CMP_STRIDE + 1
    ns = T // SLC_BLOCK
    n_sel = min(SLC_TOPK, ns)

    kc = compress_blocks(k_cmp, pe_k, w1_k, w2_k)
    vc = compress_blocks(v_cmp, pe_v, w1_v, w2_v)
    cmp_start = np.arange(nc) * CMP_STRIDE
    cmp_end = jnp.asarray(cmp_start + CMP_BLOCK - 1, dtype=jnp.int32)
    slc_start = np.arange(ns) * SLC_BLOCK
    overlap = jnp.asarray(((cmp_start[:, None] < slc_start[None, :] + SLC_BLOCK)
                           & (cmp_start[:, None] + CMP_BLOCK > slc_start[None, :])).astype(np.float32))

    tbl_heads = rel_table.T
    tbl_grp = tbl_heads.reshape(G, R, REL_BUCKETS)
    g_idx = jnp.arange(G)[None, :, None, None, None]
    r_idx = jnp.arange(R)[None, None, :, None, None]

    ks = k_slc.transpose(0, 2, 1, 3).reshape(B, G, ns, SLC_BLOCK, DH)
    vs = v_slc.transpose(0, 2, 1, 3).reshape(B, G, ns, SLC_BLOCK, DH)
    pad = ((0, 0), (0, 0), (WINDOW, 0), (0, 0))
    kwp = jnp.pad(k_win.transpose(0, 2, 1, 3), pad)
    vwp = jnp.pad(v_win.transpose(0, 2, 1, 3), pad)
    win_dist = jnp.asarray(np.arange(Q_BLOCK)[:, None] + WINDOW - np.arange(Q_BLOCK + WINDOW)[None, :],
                           dtype=jnp.int32)
    bias_win = tbl_heads[:, rel_bucket(win_dist)].reshape(G, R, Q_BLOCK, Q_BLOCK + WINDOW)

    qb = q.reshape(B, nb, Q_BLOCK, G, R, DH).transpose(1, 0, 3, 4, 2, 5)
    b_idx = jnp.arange(B)[:, None, None, None]
    gk_idx = jnp.arange(G)[None, :, None, None]
    j = jnp.arange(ns)

    def block(args):
        i, qi = args
        qpos = i * Q_BLOCK + jnp.arange(Q_BLOCK)
        s = jnp.einsum('bgrqd,bgcd->bgrqc', qi, kc).astype(jnp.float32) * SCALE
        bias = tbl_heads[:, rel_bucket(qpos[:, None] - cmp_end[None, :])].reshape(G, R, Q_BLOCK, nc)
        p_cmp = masked_softmax(s + bias, cmp_end[None, :] <= qpos[:, None])
        o_cmp = jnp.einsum('bgrqc,bgcd->bgrqd', p_cmp.astype(vc.dtype), vc)
        imp = jnp.einsum('bgrqc,cs->bgqs', p_cmp, overlap)
        cur = qpos // SLC_BLOCK
        forced = (j[None, :] == 0) | (j[None, :] == cur[:, None]) | (j[None, :] == cur[:, None] - 1)
        valid = j[None, :] * SLC_BLOCK <= qpos[:, None]
        imp = jnp.where(forced, FORCED_SCORE, jnp.where(valid, imp, -1.0))
        _, sel = lax.top_k(imp, n_sel)
        k_sel = ks[b_idx, gk_idx, sel].reshape(B, G, Q_BLOCK, n_sel * SLC_BLOCK, DH)
        v_sel = vs[b_idx, gk_idx, sel].reshape(B, G, Q_BLOCK, n_sel * SLC_BLOCK, DH)
        pos = (sel[..., None] * SLC_BLOCK + jnp.arange(SLC_BLOCK)).reshape(B, G, Q_BLOCK, n_sel * SLC_BLOCK)
        s = jnp.einsum('bgrqd,bgqkd->bgrqk', qi, k_sel).astype(jnp.float32) * SCALE
        bias = tbl_grp[g_idx, r_idx, rel_bucket(qpos[:, None] - pos)[:, :, None]]
        p = masked_softmax(s + bias, (pos <= qpos[:, None])[:, :, None])
        o_slc = jnp.einsum('bgrqk,bgqkd->bgrqd', p.astype(v_sel.dtype), v_sel)
        kw = lax.dynamic_slice_in_dim(kwp, i * Q_BLOCK, Q_BLOCK + WINDOW, axis=2)
        vw = lax.dynamic_slice_in_dim(vwp, i * Q_BLOCK, Q_BLOCK + WINDOW, axis=2)
        kpos = i * Q_BLOCK - WINDOW + jnp.arange(Q_BLOCK + WINDOW)
        wmask = ((kpos[None, :] >= 0) & (kpos[None, :] <= qpos[:, None])
                 & (qpos[:, None] - kpos[None, :] < WINDOW))
        s = jnp.einsum('bgrqd,bgkd->bgrqk', qi, kw).astype(jnp.float32) * SCALE + bias_win
        p = masked_softmax(s, wmask)
        o_win = jnp.einsum('bgrqk,bgkd->bgrqd', p.astype(vw.dtype), vw)
        return jnp.stack([o_cmp, o_slc, o_win], axis=-2)

    o = lax.map(block, (jnp.arange(nb), qb))
    o = o.transpose(1, 0, 4, 2, 3, 5, 6).reshape(B, T, H, 3, DH)
    gates = jax.nn.sigmoid(gate_logit)[..., None]
    return jnp.sum(gates * o, axis=3).reshape(B, T, H * DH)

def first_inputs(seed: int = 0) -> dict:
    key = jax.random.key(seed)
    ks = jax.random.split(key, 20)

    def w(k, shape, fan_in):
        return jax.random.normal(k, shape, jnp.float32) * fan_in ** -0.5

    def gain(k, shape):
        return 1.0 + 0.05 * jax.random.normal(k, shape, jnp.float32)

    nrm = lambda k, shape: jax.random.normal(k, shape, jnp.float32)
    L = DEPTH
    return {
        "x": nrm(ks[0], (BATCH, SEQ, D_MODEL)),
        "rel_bias_table": 0.5 * nrm(ks[1], (REL_BUCKETS, NSA_HEADS)),
        "g_attn": gain(ks[2], (L, D_MODEL)),
        "w_in": w(ks[3], (L, D_MODEL, IN_WIDTH), D_MODEL),
        "b_forget": 3.0 + 0.5 * nrm(ks[4], (L, FOX_HEADS)),
        "cmp_pe_k": 0.5 * nrm(ks[5], (L, CMP_BLOCK, HEAD_DIM)),
        "cmp_w1_k": w(ks[6], (L, CMP_BLOCK * HEAD_DIM, CMP_HIDDEN), CMP_BLOCK * HEAD_DIM),
        "cmp_w2_k": w(ks[7], (L, CMP_HIDDEN, HEAD_DIM), CMP_HIDDEN),
        "cmp_pe_v": 0.5 * nrm(ks[8], (L, CMP_BLOCK, HEAD_DIM)),
        "cmp_w1_v": w(ks[9], (L, CMP_BLOCK * HEAD_DIM, CMP_HIDDEN), CMP_BLOCK * HEAD_DIM),
        "cmp_w2_v": w(ks[10], (L, CMP_HIDDEN, HEAD_DIM), CMP_HIDDEN),
        "w_br_fox": w(ks[11], (L, FOX_W, D_MODEL), FOX_W),
        "w_br_nsa": w(ks[12], (L, NSA_W, D_MODEL), NSA_W),
        "w_out": w(ks[13], (L, D_MODEL, D_MODEL), D_MODEL),
        "g_mlp": gain(ks[14], (L, D_MODEL)),
        "w_ff1": w(ks[15], (L, D_MODEL, D_FF), D_MODEL),
        "w_ff2": w(ks[16], (L, D_FF, D_MODEL), D_FF),
        "g_final": gain(ks[17], (D_MODEL,)),
    }

def first_block(x, rel_bias_table, g_attn, w_in, b_forget, cmp_pe_k, cmp_w1_k, cmp_w2_k,
              cmp_pe_v, cmp_w1_v, cmp_w2_v, w_br_fox, w_br_nsa, w_out, g_mlp, w_ff1, w_ff2,
              g_final):
    B, T, _ = x.shape
    offsets = np.cumsum(IN_SPLITS)[:-1].tolist()
    for l in range(DEPTH):
        h = rms_norm(x, g_attn[l])
        z = h @ w_in[l]
        (fq, fk, fv, f_logit, nq, kc, vc, ksl, vsl, kwn, vwn, n_gate, g_a, g_b) = jnp.split(z, offsets, axis=-1)
        fox_h = lambda t: t.reshape(B, T, FOX_HEADS, HEAD_DIM)
        kv_h = lambda t: t.reshape(B, T, NSA_KV_GROUPS, HEAD_DIM)
        o_fox = fox_attention(fox_h(fq), fox_h(fk), fox_h(fv), f_logit, b_forget[l])
        o_nsa = nsa_attention(nq.reshape(B, T, NSA_HEADS, HEAD_DIM), kv_h(kc), kv_h(vc), kv_h(ksl), kv_h(vsl),
                              kv_h(kwn), kv_h(vwn), n_gate.reshape(B, T, NSA_HEADS, 3), rel_bias_table,
                              cmp_pe_k[l], cmp_w1_k[l], cmp_w2_k[l], cmp_pe_v[l], cmp_w1_v[l], cmp_w2_v[l])
        merged = jax.nn.sigmoid(g_a) * (o_fox @ w_br_fox[l]) + jax.nn.sigmoid(g_b) * (o_nsa @ w_br_nsa[l])
        x = x + merged @ w_out[l]
        h = rms_norm(x, g_mlp[l])
        x = x + jnp.square(jax.nn.relu(h @ w_ff1[l])) @ w_ff2[l]
    return rms_norm(x, g_final)


GRID_W = 64
CTX_LEN = 256
N_HEADS = 8
N_KV_HEADS = 2
HEAD_DIM_2 = 128
ROPE_THETA = 10000.0
CONV_DIM = 512
CONV_WIDTH = 31
FFN_DIM = 2816
FFN_CONV_WIDTH = 3
EPS = 1e-6
Q_DIM = N_HEADS * HEAD_DIM_2
KV_DIM = N_KV_HEADS * HEAD_DIM_2
IN_DIM = Q_DIM + 2 * KV_DIM + 2 * CONV_DIM + 2 * D_MODEL
SPLITS = (Q_DIM, Q_DIM + KV_DIM, Q_DIM + 2 * KV_DIM, Q_DIM + 2 * KV_DIM + 2 * CONV_DIM)


def rms_norm_2(x, g):
    xf = x.astype(jnp.float32)
    y = xf * lax.rsqrt(jnp.mean(xf * xf, axis=-1, keepdims=True) + EPS)
    return (y * g.astype(jnp.float32)).astype(x.dtype)

def layer_norm(x, g, b):
    xf = x.astype(jnp.float32)
    mu = jnp.mean(xf, axis=-1, keepdims=True)
    var = jnp.mean(jnp.square(xf - mu), axis=-1, keepdims=True)
    y = (xf - mu) * lax.rsqrt(var + EPS)
    return (y * g.astype(jnp.float32) + b.astype(jnp.float32)).astype(x.dtype)

def depthwise_conv(x, w, b):
    C = x.shape[-1]
    y = lax.conv_general_dilated(x, w[:, None, :], window_strides=(1,), padding='SAME',
                                 dimension_numbers=('NWC', 'WIO', 'NWC'), feature_group_count=C)
    return y + b

def modulation(cvec, w_mod, b_mod):
    m = jax.nn.silu(cvec) @ w_mod + b_mod
    return jnp.split(m[:, None, :], 6, axis=-1)

def modulate(h, shift, scale):
    return h * (1.0 + scale) + shift

def axial_rope(rows):
    half = HEAD_DIM_2 // 2
    inv_freq = ROPE_THETA ** (-jnp.arange(0, half, 2, dtype=jnp.float32) / half)
    r = jnp.repeat(jnp.arange(rows, dtype=jnp.float32), GRID_W)
    col = jnp.tile(jnp.arange(GRID_W, dtype=jnp.float32), rows)
    ang = jnp.concatenate([r[:, None] * inv_freq, col[:, None] * inv_freq], axis=-1)
    return jnp.cos(ang), jnp.sin(ang)

def apply_rope(x, cos, sin):
    xf = x.astype(jnp.float32).reshape(x.shape[:-1] + (HEAD_DIM_2 // 2, 2))
    x0, x1 = xf[..., 0], xf[..., 1]
    c = cos[None, :, None, :]
    s = sin[None, :, None, :]
    out = jnp.stack([x0 * c - x1 * s, x0 * s + x1 * c], axis=-1)
    return out.reshape(x.shape).astype(x.dtype)

def head_rms(t, n_heads, g):
    B, L, _ = t.shape
    return rms_norm_2(t.reshape(B, L, n_heads, HEAD_DIM_2), g)

def project(h, w_in, q_g, k_g):
    p = h @ w_in
    q, k, v, u, g = jnp.split(p, SPLITS, axis=-1)
    B, L, _ = h.shape
    q = head_rms(q, N_HEADS, q_g)
    k = head_rms(k, N_KV_HEADS, k_g)
    v = v.reshape(B, L, N_KV_HEADS, HEAD_DIM_2)
    return q, k, v, u, g

def context_kv(hc, w_in, k_g):
    p = hc @ w_in[:, Q_DIM:Q_DIM + 2 * KV_DIM]
    k, v = jnp.split(p, 2, axis=-1)
    B, L, _ = hc.shape
    return head_rms(k, N_KV_HEADS, k_g), v.reshape(B, L, N_KV_HEADS, HEAD_DIM_2)

def block_attention(q, k, v):
    B, Lq, H, d = q.shape
    G = H // N_KV_HEADS
    nblk = Lq // Q_BLOCK
    qb = q.reshape(B, nblk, Q_BLOCK, N_KV_HEADS, G, d).transpose(1, 0, 2, 3, 4, 5)
    scale = HEAD_DIM_2 ** -0.5

    def one_block(qblk):
        s = jnp.einsum('bqkgd,bskd->bkgqs', qblk, k, preferred_element_type=jnp.float32) * scale
        p = jax.nn.softmax(s, axis=-1)
        return jnp.einsum('bkgqs,bskd->bqkgd', p.astype(v.dtype), v)

    o = lax.map(one_block, qb)
    return o.transpose(1, 0, 2, 3, 4, 5).reshape(B, Lq, H * d)

def conformer_conv(u, dw_w, dw_b, ln_g, ln_b, w_conv_out):
    a, b = jnp.split(u, 2, axis=-1)
    h = a * jax.nn.sigmoid(b)
    h = depthwise_conv(h, dw_w, dw_b)
    h = jax.nn.silu(layer_norm(h, ln_g, ln_b))
    return h @ w_conv_out

def merge_branches(attn, u, g, w_attn_out, dw_w, dw_b, ln_g, ln_b, w_conv_out, w_out):
    y_a = attn @ w_attn_out
    y_b = conformer_conv(u, dw_w, dw_b, ln_g, ln_b, w_conv_out)
    g_a, g_b = jnp.split(g, 2, axis=-1)
    return (jax.nn.sigmoid(g_a) * y_a + jax.nn.sigmoid(g_b) * y_b) @ w_out

def conv_glu_ffn(h, w_up, dw_w, dw_b, w_down):
    up = h @ w_up
    a, b = jnp.split(up, 2, axis=-1)
    a = depthwise_conv(a, dw_w, dw_b)
    return (jax.nn.gelu(a, approximate=True) * b) @ w_down

def second_inputs(seed: int = 0) -> dict:
    key = jax.random.key(seed)
    ks = jax.random.split(key, 24)

    def nrm(k, shape, scale):
        return jax.random.normal(k, shape, jnp.float32) * scale

    return {
        'x': nrm(ks[0], (BATCH, SEQ, D_MODEL), 1.0),
        'c': nrm(ks[1], (BATCH, D_MODEL), 1.0),
        'ctx': nrm(ks[2], (BATCH, CTX_LEN, D_MODEL), 1.0),
        'c_ctx': nrm(ks[3], (D_MODEL,), 1.0),
        'w_mod': nrm(ks[4], (DEPTH, D_MODEL, 6 * D_MODEL), 0.5 * D_MODEL ** -0.5),
        'b_mod': nrm(ks[5], (DEPTH, 6 * D_MODEL), 0.02),
        'norm1_g': 1.0 + nrm(ks[6], (DEPTH, D_MODEL), 0.02),
        'w_in': nrm(ks[7], (DEPTH, D_MODEL, IN_DIM), D_MODEL ** -0.5),
        'q_norm_g': 1.0 + nrm(ks[8], (DEPTH, HEAD_DIM_2), 0.02),
        'k_norm_g': 1.0 + nrm(ks[9], (DEPTH, HEAD_DIM_2), 0.02),
        'w_attn_out': nrm(ks[10], (DEPTH, Q_DIM, D_MODEL), Q_DIM ** -0.5),
        'conv_dw_w': nrm(ks[11], (DEPTH, CONV_WIDTH, CONV_DIM), CONV_WIDTH ** -0.5),
        'conv_dw_b': nrm(ks[12], (DEPTH, CONV_DIM), 0.02),
        'conv_ln_g': 1.0 + nrm(ks[13], (DEPTH, CONV_DIM), 0.02),
        'conv_ln_b': nrm(ks[14], (DEPTH, CONV_DIM), 0.02),
        'w_conv_out': nrm(ks[15], (DEPTH, CONV_DIM, D_MODEL), CONV_DIM ** -0.5),
        'w_out': nrm(ks[16], (DEPTH, D_MODEL, D_MODEL), D_MODEL ** -0.5),
        'norm2_g': 1.0 + nrm(ks[17], (DEPTH, D_MODEL), 0.02),
        'w_up': nrm(ks[18], (DEPTH, D_MODEL, 2 * FFN_DIM), D_MODEL ** -0.5),
        'ffn_dw_w': nrm(ks[19], (DEPTH, FFN_CONV_WIDTH, FFN_DIM), FFN_CONV_WIDTH ** -0.5),
        'ffn_dw_b': nrm(ks[20], (DEPTH, FFN_DIM), 0.02),
        'w_down': nrm(ks[21], (DEPTH, FFN_DIM, D_MODEL), FFN_DIM ** -0.5),
        'final_g': 1.0 + nrm(ks[22], (D_MODEL,), 0.02),
    }

def second_block(x, c, ctx, c_ctx, w_mod, b_mod, norm1_g, w_in, q_norm_g, k_norm_g, w_attn_out,
              conv_dw_w, conv_dw_b, conv_ln_g, conv_ln_b, w_conv_out, w_out, norm2_g,
              w_up, ffn_dw_w, ffn_dw_b, w_down, final_g):
    B, L, _ = x.shape
    rows = L // GRID_W
    cos, sin = axial_rope(rows)
    for i in range(DEPTH):
        sh1, sc1, g1, sh2, sc2, g2 = modulation(c, w_mod[i], b_mod[i])
        csh1, csc1, cg1, csh2, csc2, cg2 = modulation(c_ctx[None], w_mod[i], b_mod[i])

        hx = modulate(rms_norm_2(x, norm1_g[i]), sh1, sc1)
        hc = modulate(rms_norm_2(ctx, norm1_g[i]), csh1, csc1)
        qx, kx, vx, ux, gx = project(hx, w_in[i], q_norm_g[i], k_norm_g[i])
        qx = apply_rope(qx, cos, sin)
        kx = apply_rope(kx, cos, sin)
        last = i == DEPTH - 1
        if last:
            kc, vc = context_kv(hc, w_in[i], k_norm_g[i])
        else:
            qc, kc, vc, uc, gc = project(hc, w_in[i], q_norm_g[i], k_norm_g[i])
        attn_x = block_attention(qx, jnp.concatenate([kc, kx], axis=1), jnp.concatenate([vc, vx], axis=1))
        mix_x = merge_branches(attn_x, ux, gx, w_attn_out[i], conv_dw_w[i], conv_dw_b[i],
                               conv_ln_g[i], conv_ln_b[i], w_conv_out[i], w_out[i])
        x = x + g1 * mix_x
        hx2 = modulate(rms_norm_2(x, norm2_g[i]), sh2, sc2)
        x = x + g2 * conv_glu_ffn(hx2, w_up[i], ffn_dw_w[i], ffn_dw_b[i], w_down[i])

        if not last:
            attn_c = block_attention(qc, kc, vc)
            mix_c = merge_branches(attn_c, uc, gc, w_attn_out[i], conv_dw_w[i], conv_dw_b[i],
                                   conv_ln_g[i], conv_ln_b[i], w_conv_out[i], w_out[i])
            ctx = ctx + cg1 * mix_c
            hc2 = modulate(rms_norm_2(ctx, norm2_g[i]), csh2, csc2)
            ctx = ctx + cg2 * conv_glu_ffn(hc2, w_up[i], ffn_dw_w[i], ffn_dw_b[i], w_down[i])
    return rms_norm_2(x, final_g)


def setup_inputs(seed=0):
    out = dict(first_inputs(seed))
    for name, value in second_inputs(seed + 1).items():
        if name != "x":
            out[name + "_2"] = value
    return out


def reference(
    x, rel_bias_table, g_attn, w_in, b_forget, cmp_pe_k, cmp_w1_k, cmp_w2_k, cmp_pe_v, cmp_w1_v,
    cmp_w2_v, w_br_fox, w_br_nsa, w_out, g_mlp, w_ff1, w_ff2, g_final, c_2, ctx_2, c_ctx_2,
    w_mod_2, b_mod_2, norm1_g_2, w_in_2, q_norm_g_2, k_norm_g_2, w_attn_out_2, conv_dw_w_2,
    conv_dw_b_2, conv_ln_g_2, conv_ln_b_2, w_conv_out_2, w_out_2, norm2_g_2, w_up_2, ffn_dw_w_2,
    ffn_dw_b_2, w_down_2, final_g_2,
):
    x = first_block(
        x, rel_bias_table, g_attn, w_in, b_forget, cmp_pe_k, cmp_w1_k, cmp_w2_k, cmp_pe_v,
        cmp_w1_v, cmp_w2_v, w_br_fox, w_br_nsa, w_out, g_mlp, w_ff1, w_ff2, g_final,
    )
    return second_block(
        x, c_2, ctx_2, c_ctx_2, w_mod_2, b_mod_2, norm1_g_2, w_in_2, q_norm_g_2, k_norm_g_2,
        w_attn_out_2, conv_dw_w_2, conv_dw_b_2, conv_ln_g_2, conv_ln_b_2, w_conv_out_2, w_out_2,
        norm2_g_2, w_up_2, ffn_dw_w_2, ffn_dw_b_2, w_down_2, final_g_2,
    )


_drawn_inputs = setup_inputs


def setup_inputs(seed=0):
    import zlib

    import numpy as np

    out = dict(_drawn_inputs(seed))
    spreads = {}
    factors = {'g_attn': 3.253,
     'cmp_pe_k': 6.225,
     'ctx_2': 8.0,
     'c_ctx_2': 3.549,
     'b_mod_2': 2.823,
     'norm1_g_2': 8.0,
     'q_norm_g_2': 8.0,
     'k_norm_g_2': 8.0,
     'conv_dw_b_2': 22.118,
     'conv_ln_g_2': 34.257,
     'conv_ln_b_2': 33.24,
     'norm2_g_2': 8.0,
     'ffn_dw_b_2': 23.131,
     'final_g_2': 9.161}
    for name, (base, spread) in spreads.items():
        noise = np.random.default_rng([zlib.crc32(name.encode()), seed]).standard_normal(out[name].shape)
        drawn = base * np.exp(spread * noise) if base else spread * noise
        out[name] = __import__('jax').numpy.asarray(drawn.astype(out[name].dtype))
    for name, factor in factors.items():
        out[name] = (out[name] * factor).astype(out[name].dtype)
    return out
```

```python
from contextlib import ExitStack

import numpy as np

import concourse.bass as bass
from concourse import mybir

F32 = mybir.dt.float32
F32R = mybir.dt.float32r
ALU = mybir.AluOpType
ACT = mybir.ActivationFunctionType
AX = mybir.AxisListType.X

P = 128
T = 512
D = 1024
KT = D // P
NT = T // P
FOX_PAIRS = 4
NSA_PAIRS = 4
NSA_HEADS = 8
CMP_STRIDE, CMP_BLOCK = 16, 32
NCB = (T - CMP_BLOCK) // CMP_STRIDE + 1
CW = 32
FF = 4 * D
CTX = 256
H2, KV2 = 8, 2
KEYS2 = CTX + T
CONV_T = 4
TAPS = 31
FFN_T = 22
EPS = 1e-6
NEG = -1e30
S8 = 8.0
SC2 = 128.0 ** -0.5
RING = 4
AHEAD = 2
REL_W = 639

C_ID, C_ONE, C_ROT, C_COS, C_SIN, C_MASK, C_ROW, C_EPS = 0, 128, 256, 384, 896, 1408, 1536, 1537
C_ALL = 1539
V_SPEC = [("g_attn", 8), ("g_mlp", 8), ("g_final", 8), ("norm1", 8), ("norm2", 8), ("final2", 8), ("ln_g", 4),
          ("ln_b", 4), ("dw_b", 4), ("dw_w", 4 * TAPS), ("ffn_w", FFN_T * 3), ("ffn_b", FFN_T), ("q_g", 1),
          ("k_g", 1), ("c", 8), ("c_ctx", 8), ("b_mod", 48), ("pe_k", 16), ("pe_v", 16)]
V_AT, V_ALL = {}, 0
for _n, _w in V_SPEC:
    V_AT[_n] = V_ALL
    V_ALL += _w

GROUPS = [("fox_qk", 8), ("fox_v", 4), ("nsa_kv", 8), ("nsa_q", 4), ("cmp", 8), ("gate", 16), ("branch", 8),
          ("out", 8)]
for _c in range(4):
    GROUPS += [(f"ff1_{_c}", 8), (f"ff2_{_c}", 8)]
GROUPS += [("kv2", 4), ("glu", 8), ("q2", 8), ("gate2", 16), ("conv_out", 4), ("attn_out", 8), ("out2", 8)]
HID = [8, 8, 6]
for _c in range(3):
    GROUPS += [(f"up_{_c}", 2 * HID[_c]), (f"down_{_c}", 8)]
BASE, PANELS = {}, 0
for _n, _w in GROUPS:
    BASE[_n] = PANELS
    PANELS += _w
COUNT = dict(GROUPS)
STAGES = ["norm1", "fox_qk", "fox_v", "nsa_kv", "nsa_q", "cmp", "attn1", "gate", "branch", "out", "norm_mlp", "ff",
          "final1", "mod", "norm2", "kv2", "glu", "q2", "conv_ln", "attn2", "gate2", "conv_out", "attn_out", "out2", "norm_ffn",
          "ffn", "final2"]


def build(nc, a, out, upto="final2"):
    stages = STAGES[:STAGES.index(upto) + 1]
    ctx = ExitStack()
    base0 = (nc.sbuf_base + 63) // 64 * 64
    room = (nc.sbuf_usable_end - base0) // 4
    mark = {"at": 0}

    def place(name, shape, dt, at=None):
        n = int(np.prod(shape[1:]))
        n = (n + 7) // 8 * 8
        if at is None:
            at = mark["at"]
            mark["at"] += n
        assert at + n <= room, (name, at, n, room)
        return nc.alloc_sbuf_tensor_at(name, list(shape), dt, offset=base0 + 4 * at)

    raw = place("raw", [P, RING, 8, P], F32)
    w_hi = place("w_hi", [P, RING, 8, P], F32R)
    w_lo = place("w_lo", [P, RING, 8, P], F32R)
    h_hi = place("h_hi", [P, KT, T], F32R)
    h_lo = place("h_lo", [P, KT, T], F32R)
    x_at = mark["at"]
    X = place("X", [P, KT, T], F32)
    cst = place("cst", [P, C_ALL], F32)
    vec = place("vec", [P, V_ALL], F32)
    cst_r = place("cst_r", [P, 2 * P], F32R)
    rstd_at = mark["at"]
    rstd = place("rstd", [P, T], F32)
    sq_acc = place("sq_acc", [P, T], F32)
    tmp_at = mark["at"]
    tmp_v = place("tmp_v", [P, 2, T], F32)
    tmp_s = place("tmp_s", [P, 2, T], F32)
    small_at = mark["at"]
    small = place("small", [P, 736], F32)
    pool = mark["at"]

    eps, eps128 = cst[:, C_EPS:C_EPS + 1], cst[:, C_EPS + 1:C_EPS + 2]

    def vcol(name, k=0):
        return vec[:, V_AT[name] + k:V_AT[name] + k + 1]

    q_hi = place("q_hi", [P, 8, T], F32R, pool)
    q_lo = place("q_lo", [P, 8, T], F32R, pool + 4096)
    v_hi = place("v_hi", [P, NT, 512], F32R, pool + 8192)
    v_lo = place("v_lo", [P, NT, 512], F32R, pool + 10240)
    kn_hi = place("kn_hi", [P, 2, T], F32R, pool + 12800)
    kn_lo = place("kn_lo", [P, 2, T], F32R, pool + 13824)
    vn_hi = place("vn_hi", [P, 2, NT, P], F32R, pool + 14848)
    vn_lo = place("vn_lo", [P, 2, NT, P], F32R, pool + 15872)
    cmp_at = pool + 16896
    pt_hi = place("pt_hi", [P, 1280], F32R, cmp_at)
    pt_lo = place("pt_lo", [P, 1280], F32R, cmp_at + 1280)
    bias = place("bias", [P, 2, T], F32, cmp_at + 2560)
    sb = place("sb", [P, 2, 1280], F32, rstd_at)
    nq_hi = place("nq_hi", [P, 4, T], F32R, x_at)
    nq_lo = place("nq_lo", [P, 4, T], F32R, x_at + 2048)
    blk_f = place("blk_f", [P, 16, 64], F32, cmp_at)
    blk_hi = [place(f"blk_hi{j}", [P, 16, 64], F32R, cmp_at + 1024 + 2048 * j) for j in range(2)]
    blk_lo = [place(f"blk_lo{j}", [P, 16, 64], F32R, cmp_at + 2048 + 2048 * j) for j in range(2)]
    sig_n = place("sig_n", [24, T], F32, cmp_at + 3072)
    w2k = place("w2k", [P, 2, P], F32, tmp_at)
    w2v = place("w2v", [P, 2, 64], F32, tmp_at + 256)
    lf_a = place("lf_a", [8, T], F32, rstd_at)
    cum = place("cum", [8, T], F32, rstd_at + 512)
    zf = place("zf", [8, T], F32, tmp_at + 512)
    hot = place("hot", [32, 640], F32, pool)
    r8 = place("r8", [8, 640], F32, pool + 640)
    r_mask = place("r_mask", [8, 640], F32, pool + 1280)
    sm = {"at": small_at}

    def sml(name, shape, dt=F32):
        t = place(name, shape, dt, sm["at"])
        sm["at"] += (int(np.prod(shape[1:])) + 7) // 8 * 8
        assert sm["at"] <= small_at + 632, (name, sm["at"] - small_at)
        return t

    vc_hi = place("vc_hi", [CW, P], F32R, cmp_at + 5120)
    vc_lo = place("vc_lo", [CW, P], F32R, cmp_at + 5248)
    kc_hi = sml("kc_hi", [P, CW], F32R)
    kc_lo = sml("kc_lo", [P, CW], F32R)
    gate_t = sml("gate_t", [P, NT, 24])
    c_q8 = sml("c_q8", [P, NT, 8])
    row_max = sml("row_max", [P, 2, 4])
    neg_max = sml("neg_max", [P, 2, 4])
    row_sum = sml("row_sum", [P, 2, 4])
    factor = sml("factor", [P, 2, 4])
    factor2 = sml("factor2", [P, 2, 4])
    p_cmp = sml("p_cmp", [P, 2, NT, CW])
    hid_c = sml("hid_c", [P, 2, 64])
    tab = sml("tab", [32, 8])
    bf = sml("bf", [8, 1])
    silu_c = place("silu_c", [P, 16], F32, small_at + 632)
    mod = place("mod", [P, 64], F32, small_at + 648)
    gains = place("gains", [P, 24], F32, small_at + 712)
    gates = place("gates", [P, 16, T], F32, pool + 8192)
    f_hi = place("f_hi", [P, 8, T], F32R, pool)
    f_lo = place("f_lo", [P, 8, T], F32R, pool + 4096)
    mod_a = place("mod_a", [P, 6 * D], F32, pool + 8192)
    mod_x = place("mod_x", [P, 2 * D], F32, pool + 14336)
    wm = place("wm", [P, 2, 3 * D], F32, pool + 16384)
    x_ctx = place("x_ctx", [P, KT, CTX], F32, pool)
    q2_hi = place("q2_hi", [P, H2, T], F32R, pool)
    q2_lo = place("q2_lo", [P, H2, T], F32R, pool + 4096)
    k2_hi = place("k2_hi", [P, KV2, KEYS2], F32R, pool + 8192)
    k2_lo = place("k2_lo", [P, KV2, KEYS2], F32R, pool + 9728)
    v2_hi = place("v2_hi", [P, 6, KV2 * P], F32R, pool + 11264)
    v2_lo = place("v2_lo", [P, 6, KV2 * P], F32R, pool + 12800)
    hc_hi = place("hc_hi", [P, KT, CTX], F32R, pool + 14336)
    hc_lo = place("hc_lo", [P, KT, CTX], F32R, pool + 16384)
    VP = T + TAPS - 1
    u_pad = place("u_pad", [P, CONV_T, VP], F32, pool + 14336)
    conv = place("conv", [P, CONV_T, T], F32, pool + 16504)
    yc_hi = place("yc_hi", [P, CONV_T, T], F32R, pool + 18552)
    yc_lo = place("yc_lo", [P, CONV_T, T], F32R, pool + 20600)
    qg = place("qg", [P, 2, T], F32, pool + 18552)
    probs = place("probs", [P, NT, KEYS2], F32, pool + 14336)
    pt2_hi = place("pt2_hi", [P, 2, T], F32R, tmp_at)
    pt2_lo = place("pt2_lo", [P, 2, T], F32R, tmp_at + 1024)

    ps = nc.alloc_psum_tensor("ps", [P, 8, T], F32)
    scratch_c = nc.dram_tensor("scratch_c", (8, T), F32).ap()
    scratch_r = nc.dram_tensor("scratch_r", (8, P, 640), F32).ap()

    total = max([BASE[g] + COUNT[g] for g in BASE if g.split("_")[0] in ("ff1", "ff2") and "ff" in stages
                 or g.split("_")[0] in ("up", "down") and "ffn" in stages or g in stages], default=0)
    sems = {}

    def sem(name):
        if name not in sems:
            sems[name] = nc.alloc_semaphore(name)
        return sems[name]

    landed = [sem(f"panel_landed_{s}") for s in range(RING)]
    hi_ready = sem("panel_hi_ready")
    lo_ready = sem("panel_lo_ready")
    used = sem("panel_used")
    bank_free = sem("bank_free")
    in_x, in_c, in_v, in_small = sem("x_loaded"), sem("constants_loaded"), sem("vectors_loaded"), sem("small_loaded")
    n_sq, n_acc, n_sum, n_rms = (sem("norm_" + s) for s in ("square", "sum", "column_sum", "rms"))
    n_val, n_hi, n_lo = sem("norm_value"), sem("norm_hi"), sem("norm_lo")
    setup = sem("setup_done")
    x_new = sem("x_updated")
    chain_v, chain_s = sem("vector_step"), sem("scalar_step")

    def done(n):
        return n + 1 + RING

    split_norm = {"norm1": 0, "norm_mlp": 1, "norm2": 2, "norm2c": 3, "norm_ffn": 4}
    NORMS = {"norm1": 0, "norm_mlp": 1, "final1": 2, "norm2": 3, "norm2c": 4, "norm_ffn": 5, "final2": 6}
    X_STEP = {"norm_mlp": 8, "final1": 8 + 32, "norm2": 48, "norm_ffn": 56, "final2": 56 + 24}
    conv_sum = 2
    n_sum_at = {"norm1": 1, "norm_mlp": 2, "final1": 3, "norm2": 4, "norm2c": 5, "norm_ffn": 6, "final2": 7}

    inst = [("fox", p, h, None) for p in range(FOX_PAIRS) for h in range(2)]
    for p in range(NSA_PAIRS):
        for h in range(2):
            inst += [("cmp", p, h, 0), ("slc", p, h, 1), ("win", p, h, 2)]
    NI = len(inst)
    big_of, turn_of, first_turn, n_turn, n_big, n_small = [], [], [], 0, 0, 0
    for k, p, h, b in inst:
        first_turn.append(n_turn)
        n_turn += 1 if k == "cmp" else NT
        big_of.append(n_small % 2 if k == "cmp" else n_big % 2)
        n_small += k == "cmp"
        n_big += k != "cmp"
    PT_AT = [0, 512, 896, 1152]

    def pair_of(s):
        return inst[s][1] + (0 if inst[s][0] == "fox" else FOX_PAIRS)

    def head_of(s):
        return 2 * pair_of(s) + inst[s][2]

    def head_end(s):
        return s + 1 == NI or head_of(s + 1) != head_of(s)

    def head_start(s):
        return s == 0 or head_of(s - 1) != head_of(s)

    def load_of(s):
        return s if s < 8 else 8 + (s - 8) // 3

    def turns(s):
        return [0] if inst[s][0] == "cmp" else list(range(NT))

    SB_AT = [0, P, 3 * P, 6 * P]

    def scores_of(s, t):
        if inst[s][0] == "cmp":
            w = 8 * t + 7
            return p_cmp[:, big_of[s], t, 0:w], w
        w = (t + 1) * P
        return sb[:, big_of[s], SB_AT[t]:SB_AT[t] + w], w

    def pt_shape(s, j):
        return (CW, 0, T) if inst[s][0] == "cmp" else (P, PT_AT[j], T - j * P)

    pt_wait, seen = {}, {}
    for s in range(NI):
        for j in turns(s):
            if j in seen:
                pt_wait[first_turn[s] + j] = seen[j] + 1
            seen[j] = first_turn[s] + j

    def s2(t):
        b = 2 if t % 2 == 0 else 0
        return ps[:, b:b + 2, :].rearrange("p b n -> p (b n)")

    block = ctx.enter_context(nc.Block())

    def loop(eng, group, body):
        last = BASE[group] + COUNT[group] == total
        n = COUNT[group] // RING - last
        if n == 1:
            for u in range(RING):
                body(0, u, True)
        elif n > 1:
            with eng.Fori(0, n) as i:
                for u in range(RING):
                    body(i, u, True)
        if last:
            for u in range(RING):
                body(n, u, u + AHEAD < RING)

    def has(stage):
        return stage in stages

    @block.sync
    def _(sp):
        for u in range(RING if total else 0):
            sp.dma_start(raw[:, u], a["panels"][u]).then_inc(landed[u], 16)
            if u == 0:
                sp.dma_start(X[:], a["x"]).then_inc(in_x, 16)
                sp.dma_start(cst[:], a["consts"]).then_inc(in_c, 16)
                sp.dma_start(vec[:], a["vectors"]).then_inc(in_v, 16)
        if total > RING:
            with sp.Fori(1, total // RING) as i:
                for u in range(RING):
                    sp.wait_ge(lo_ready, i * RING + (u - RING + 1))
                    sp.dma_start(raw[:, u], a["panels"][bass.ds(i * RING + u, 1)].rearrange("o p k n -> p (o k) n"))\
                      .then_inc(landed[u], 16)
        if not has("final2"):
            return
        for f in range(KT):
            sp.wait_ge(sem("final2_tile"), f + 1)
            sp.dma_start(out[:, f, :], X[:, f, :]).then_inc(sem("out_stored"), 16)
        sp.wait_ge(sem("out_stored"), 16 * KT)

    @block.gpsimd
    def _(gp):
        gp.dma_start(hot[:], a["onehot"]).then_inc(in_small, 16)
        gp.dma_start(tab[:], a["table"]).then_inc(in_small, 16)
        gp.dma_start(bf[:], a["b_forget"]).then_inc(in_small, 16)
        gp.dma_start(r_mask[:], a["r_mask"]).then_inc(in_small, 16)
        gp.wait_ge(sem("rel_rows"), 2)
        gp.dma_start(scratch_r, r8[:].unsqueeze(1).to_broadcast([8, P, 640])).then_inc(sem("rel_stored"), 16)
        if not has("cmp"):
            gp.wait_ge(sem("rel_stored"), 16)
            return
        gp.wait_ge(sem("v_turned"), 5)
        gp.dma_start(w2k[:], a["w2k"]).then_inc(sem("w2_loaded"), 16)
        gp.dma_start(w2v[:], a["w2v"]).then_inc(sem("w2_loaded"), 16)
        gp.wait_ge(sem("c_summed"), 1)
        gp.dma_start(scratch_c, cum[:]).then_inc(sem("c_stored"), 16)
        gp.wait_ge(sem("c_stored"), 16)
        gp.wait_ge(sem("rel_stored"), 16)
        if not has("attn1"):
            return
        gp.wait_ge(sem("cmp_v_done"), 1)
        for n in range(16):
            s_prev = None
            if n >= 2:
                m = n - 2
                if m < 8:
                    gp.wait_ge(sem("fox_bias"), 4 * (m + 1))
                else:
                    gp.wait_ge(sem("scored"), 4 * (8 + 3 * (m - 8) + 3))
            if n < 8:
                src = bass.AP(tensor=scratch_c.tensor, offset=n * T, ap=[[0, P], [1, T]])
            else:
                head = (n - 8) // 2 + 4 * ((n - 8) % 2)
                src = bass.AP(tensor=scratch_r.tensor, offset=head * P * 640 + 127, ap=[[639, P], [1, T]])
            gp.dma_start(bias[:, n % 2, :], src).then_inc(sem(f"bias_loaded_{n % 2}"), 16)
        if not has("out"):
            return
        gp.wait_ge(used, done(BASE["branch"] + 7))
        gp.dma_start(X[:], a["x"]).then_inc(sem("x_reloaded"), 16)
        if not has("ff"):
            return
        for n in range(16):
            c, part, i = n // 4, n // 2 % 2, n % 2
            if n == 0:
                gp.wait_ge(used, done(BASE["out"] - 1))
            if i == 1:
                gp.wait_ge(sem("mod_step"), n + 1)
            elif n >= 4:
                gp.wait_ge(sem("mod_step"), n - 1)
            gp.dma_start(wm[:, part], a["w_mod"][2 * c + i, :, part * 3 * D:(part + 1) * 3 * D])\
              .then_inc(sem(f"w_mod_loaded_{part}"), 16)
        if not has("norm2"):
            return
        gp.wait_ge(sem("mod_summed"), 1)
        gp.dma_start(x_ctx[:], a["ctx"]).then_inc(sem("ctx_loaded"), 16)
        gp.wait_ge(sem("ctx_loaded"), 16)

    @block.scalar
    def _(act):
        step = {"n": 0}

        def split_hi(i, u, group):
            if isinstance(i, int) and BASE[group] + RING * i + u + AHEAD >= total:
                return
            slot, turn = (u + AHEAD) % RING, (u + AHEAD) // RING
            act.wait_ge(landed[slot], (i + (BASE[group] // RING + turn + 1)) * 16)
            act.wait_ge(used, i * RING + (BASE[group] + u + AHEAD + 1))
            act.activation(w_hi[:, slot], raw[:, slot], ACT.Copy).then_inc(hi_ready, 1)

        def chain(ins):
            ins.then_inc(chain_s, 1)
            step["n"] += 1
            act.wait_ge(chain_s, step["n"])

        def norm(name, src, N, dst_hi, shift):
            k = NORMS[name]
            if name in X_STEP:
                act.wait_ge(x_new, X_STEP[name])
            for f in range(KT):
                act.wait_ge(n_acc, 8 * k + f - 1) if 8 * k + f > 1 else None
                act.activation(tmp_s[:, f % 2, :N], src[:, f, :], ACT.Square).then_inc(n_sq, 1)
            act.wait_ge(n_sum, n_sum_at[name])
            act.activation(rstd[:, :N], ps[:, 4, :N], ACT.Sqrt, scale=1.0 / D, bias=eps).then_inc(n_rms, 1)
            if dst_hi is not None:
                for f in range(KT):
                    act.wait_ge(n_val, 8 * split_norm[name] + f + 1)
                    if shift is None:
                        act.activation(dst_hi[:, f, :], tmp_v[:, f % 2, :N], ACT.Copy).then_inc(n_hi, 1)
                    else:
                        act.activation(dst_hi[:, f, :], tmp_v[:, f % 2, :N], ACT.Identity,
                                       bias=mod[:, shift + f:shift + f + 1]).then_inc(n_hi, 1)

        def split_out(group, dst):
            def body(i, u, ahead):
                split_hi(i, u, group) if ahead else None
                act.wait_ge(used, i * RING + done(BASE[group] + u))
                act.activation(dst[:, bass.ds(i * RING + u, 1), :], ps[:, u % 2:u % 2 + 1, :], ACT.Copy)\
                   .then_inc(sem(group + "_hi"), 1)
            loop(act, group, body)

        def only_split(group):
            loop(act, group, lambda i, u, ahead: split_hi(i, u, group) if ahead else None)

        def hi_of_tmp(group, dst, total_f, part="_val"):
            def body(i, u, ahead):
                split_hi(i, u, group) if ahead else None
                act.wait_ge(sem(group + part), i * RING + (u + 1))
                act.activation(dst[:, bass.ds(i * RING + u, 1), :], tmp_v[:, u % 2:u % 2 + 1, :], ACT.Copy)\
                   .then_inc(sem(group + "_hi"), 1)
            loop(act, group, body)

        act.wait_ge(in_c, 16)
        act.activation(cst_r[:, 0:P], cst[:, C_ID:C_ID + P], ACT.Copy).then_inc(setup, 1)
        act.activation(cst_r[:, P:2 * P], cst[:, C_MASK:C_MASK + P], ACT.Copy).then_inc(setup, 1)
        act.wait_ge(in_v, 16)
        act.activation(silu_c[:, :], vec[:, V_AT["c"]:V_AT["c"] + 16], ACT.Silu).then_inc(sem("silu_c_ready"), 1)
        for m in range(AHEAD if total else 0):
            act.wait_ge(landed[m], 16)
            act.activation(w_hi[:, m], raw[:, m], ACT.Copy).then_inc(hi_ready, 1)
        act.wait_ge(in_x, 16)
        norm("norm1", X, T, h_hi, None)
        if not has("fox_qk"):
            return
        act.wait_ge(sem("rel_stored"), 16)
        split_out("fox_qk", q_hi)
        if not has("fox_v"):
            return

        def v_out(t_sem, at, views):
            for j, dst in views:
                act.wait_ge(sem(t_sem), j + 1)
                act.activation(dst, ps[:, 4 + j % 2, :].rearrange("p (t n) -> p t n", n=P), ACT.Copy)\
                   .then_inc(sem("v_hi_done"), 1)

        for u in range(RING):
            split_hi(0, u, "fox_v")
            v_out("v_turned", 0, [(u, v_hi[:, :, u * P:(u + 1) * P])])
        if not has("nsa_kv"):
            return
        for m in range(8):
            i, u = divmod(m, RING)
            split_hi(i, u, "nsa_kv")
            if m == 0:
                act.wait_ge(sem("forget_z"), 1)
                chain(act.activation(lf_a[:], zf[:], ACT.Abs))
                chain(act.activation(lf_a[:], lf_a[:], ACT.Exp, scale=-1.0))
                act.activation(lf_a[:], lf_a[:], ACT.Ln, bias=cst[0:8, C_ONE:C_ONE + 1]).then_inc(sem("forget_ln"), 1)
            if m == 1:
                act.wait_ge(used, done(BASE["nsa_kv"] + 1))
                act.activation(sig_n[:], ps[0:24, 1, :], ACT.Sigmoid).then_inc(sem("gate_n"), 1)
            if m in (2, 3):
                act.wait_ge(used, done(BASE["nsa_kv"] + m))
                act.activation(kn_hi[:, m - 2, :], ps[:, m % 2, :], ACT.Copy).then_inc(sem("kn_hi_done"), 1)
            if m in (4, 5):
                act.wait_ge(sem("blk_ready"), m - 3)
                act.activation(blk_hi[m - 4][:], blk_f[:], ACT.Copy).then_inc(sem("blk_hi_done"), 1)
            if m in (6, 7):
                v_out("v_turned", 0, [(m - 2, vn_hi[:, m - 6])])
        if not has("nsa_q"):
            return
        split_out("nsa_q", nq_hi)
        if not has("cmp"):
            return
        for m in range(8):
            i, u = divmod(m, RING)
            split_hi(i, u, "cmp")
            if m == 3:
                act.wait_ge(used, done(BASE["cmp"] + 3))
                act.activation(hid_c[:], ps[:, 0, 0:P].rearrange("p (f n) -> p f n", f=2), ACT.Silu)\
                   .then_inc(sem("cmp_hidden"), 1)
                act.wait_ge(sem("cmp_k_out"), 1)
                for g in range(2):
                    act.activation(kc_hi[64 * g:64 * g + 64, :], ps[64 * g:64 * g + 64, 4, CW * g:CW * g + CW], ACT.Copy)\
                       .then_inc(sem("kc_hi_done"), 1)
            if m == 7:
                act.wait_ge(used, done(BASE["cmp"] + 7))
                act.wait_ge(sem("cmp_k_out"), 1)
                act.activation(hid_c[:], ps[:, 1, 0:P].rearrange("p (f n) -> p f n", f=2), ACT.Silu)\
                   .then_inc(sem("cmp_hidden"), 1)
                act.wait_ge(sem("cmp_v_out"), 1)
                act.activation(vc_hi[:], ps[0:CW, 5, 0:P], ACT.Copy).then_inc(sem("vc_hi_done"), 1)
        if not has("attn1"):
            return

        def fox_bias(s):
            act.wait_ge(sem(f"bias_loaded_{s % 2}"), 16 * (s // 2 + 1))
            if s >= 2:
                act.wait_ge(sem("turned"), first_turn[s - 2] + NT)
            for t in range(NT):
                w = (t + 1) * P
                act.activation(sb[:, big_of[s], SB_AT[t]:SB_AT[t] + w], bias[:, s % 2, 0:w], ACT.Identity,
                               bias=c_q8[:, t, s:s + 1]).then_inc(sem("fox_bias"), 1)

        def exps(s):
            act.wait_ge(sem("neg_max_ready"), s + 1)
            for t in range(NT):
                buf, w = scores_of(s, t)
                act.activation(buf, buf, ACT.Exp, bias=neg_max[:, s % 2, t:t + 1],
                               accum_out=row_sum[:, s % 2, t:t + 1]).then_inc(sem("exp_done"), 1)

        def hi_turn(s, j):
            r = first_turn[s] + j
            act.wait_ge(sem("turned"), r + 1)
            if r in pt_wait:
                act.wait_ge(sem("pv_done"), pt_wait[r])
            rows, at, w = pt_shape(s, j)
            act.activation(pt_hi[0:rows, at:at + w], ps[0:rows, 4 + r % 2, 0:w], ACT.Copy).then_inc(sem("pt_hi_done"), 1)

        def o_hi(s):
            p, half = pair_of(s), inst[s][2]
            r = slice(64 * half, 64 * half + 64)
            act.wait_ge(sem("pv_done"), first_turn[s] + len(turns(s)))
            dst = q_hi[r, p, :] if p < FOX_PAIRS else nq_hi[r, p - FOX_PAIRS, :]
            act.activation(dst, ps[r, 6 + half, :], ACT.Copy).then_inc(sem("o_hi_done"), 1)

        act.wait_ge(sem("c_q_ready"), 1)
        act.wait_ge(sem("cmp_v_done"), 1)
        fox_bias(0)
        for s in range(NI + 2):
            if s >= 2 and head_end(s - 2):
                o_hi(s - 2)
            js = turns(s - 1) if 1 <= s <= NI else []
            for j in js[:2]:
                hi_turn(s - 1, j)
            if s < NI:
                exps(s)
            for j in js[2:]:
                hi_turn(s - 1, j)
            if s + 1 < FOX_PAIRS * 2:
                fox_bias(s + 1)
        if not has("gate"):
            return

        def sigmoids(group):
            act.wait_ge(bank_free, BASE[group] + 2)
            def body(i, u, ahead):
                split_hi(i, u, group) if ahead else None
                act.wait_ge(used, i * RING + done(BASE[group] + u))
                act.activation(gates[:, bass.ds(i * RING + u, 1), :], ps[:, u % 2:u % 2 + 1, :], ACT.Sigmoid)\
                   .then_inc(bank_free, 1)
            loop(act, group, body)

        sigmoids("gate")
        if not has("branch"):
            return
        hi_of_tmp("branch", h_hi, 8)
        if not has("out"):
            return
        only_split("out")
        if not has("norm_mlp"):
            return
        norm("norm_mlp", X, T, h_hi, None)
        if not has("ff"):
            return
        for c in range(4):
            g = f"ff1_{c}"

            def body(i, u, ahead):
                split_hi(i, u, g) if ahead else None
                act.wait_ge(used, i * RING + done(BASE[g] + u))
                act.activation(tmp_s[:, u % 2, :], ps[:, u % 2, :], ACT.Relu).then_inc(sem("relu_done"), 1)
                act.wait_ge(sem("relu_squared"), i * RING + (8 * c + u + 1))
                act.activation(f_hi[:, bass.ds(i * RING + u, 1), :], tmp_v[:, u % 2:u % 2 + 1, :], ACT.Copy)\
                   .then_inc(sem("f_hi_done"), 1)
            loop(act, g, body)
            only_split(f"ff2_{c}")
        if not has("final1"):
            return
        norm("final1", X, T, None, None)
        if not has("norm2"):
            return
        norm("norm2", X, T, h_hi, 0)
        act.wait_ge(sem("ctx_loaded"), 16)
        norm("norm2c", x_ctx, CTX, hc_hi, 48)
        if not has("kv2"):
            return

        def head_norm(n, bank, N, m, g):
            act.activation(tmp_s[:, m, :N], ps[:, bank, :N], ACT.Square).then_inc(sem("h_sq"), 1)
            act.activation(qg[:, m, :N], ps[:, bank, :N], ACT.Copy, scale=g).then_inc(sem("h_gained"), 1)

        for u in range(RING):
            split_hi(0, u, "kv2")
            act.wait_ge(used, done(BASE["kv2"] + u))
            if u < 2:
                if u == 1:
                    act.wait_ge(sem("h_lo_done"), 2)
                head_norm(0, u, T, 0, vcol("k_g"))
                head_norm(0, 2 + u, CTX, 1, vcol("k_g"))
                for m, (dst, N) in enumerate([(k2_hi[:, u, CTX:KEYS2], T), (k2_hi[:, u, 0:CTX], CTX)]):
                    act.wait_ge(sem("h_aux"), 2 * u + m + 1)
                    act.activation(rstd[:, :N], ps[:, 4, :N], ACT.Sqrt, scale=1.0 / P, bias=eps).then_inc(sem("h_rms"), 1)
                    act.wait_ge(sem("h_val"), 2 * u + m + 1)
                    act.activation(dst, tmp_v[:, 0, :N], ACT.Copy).then_inc(sem("h_hi_done"), 1)
            else:
                g = u - 2
                act.wait_ge(sem("v2_turned"), 2 * g + 1)
                act.activation(v2_hi[:, 2:6, g * P:(g + 1) * P], ps[:, 4, :].rearrange("p (t n) -> p t n", n=P),
                               ACT.Copy).then_inc(sem("v2_hi_done"), 1)
                act.wait_ge(sem("v2_turned"), 2 * g + 2)
                act.activation(v2_hi[:, 0:2, g * P:(g + 1) * P], ps[:, 5, 0:CTX].rearrange("p (t n) -> p t n", n=P),
                               ACT.Copy).then_inc(sem("v2_hi_done"), 1)
        if not has("glu"):
            return

        def glu(i, u, ahead):
            split_hi(i, u, "glu") if ahead else None
            act.wait_ge(used, i * RING + done(BASE["glu"] + u))
            if u % 2:
                act.activation(tmp_s[:, u // 2, :], ps[:, 1, :], ACT.Sigmoid).then_inc(sem("glu_sig"), 1)
        loop(act, "glu", glu)
        if not has("q2"):
            return

        def q2(i, u, ahead):
            split_hi(i, u, "q2") if ahead else None
            act.wait_ge(used, i * RING + done(BASE["q2"] + u))
            act.activation(tmp_s[:, u % 2, :], ps[:, u % 2, :], ACT.Square).then_inc(sem("q_sq"), 1)
            act.activation(qg[:, u % 2, :], ps[:, u % 2, :], ACT.Copy, scale=vcol("q_g")).then_inc(sem("q_gained"), 1)
            if u:
                q2_hi_part(i, u - 1)
            if u == RING - 1:
                q2_hi_part(i, u)

        def q2_hi_part(i, u):
            act.wait_ge(sem("q_aux"), i * RING + (u + 1))
            act.activation(rstd[:], ps[:, 4, :], ACT.Sqrt, bias=eps128).then_inc(sem("q_rms"), 1)
            act.wait_ge(sem("q_val"), i * RING + (u + 1))
            act.activation(q2_hi[:, bass.ds(i * RING + u, 1), :], tmp_v[:, 0:1, :], ACT.Copy).then_inc(sem("q_hi_done"), 1)

        loop(act, "q2", q2)
        if not has("conv_ln"):
            return
        for f in range(CONV_T):
            act.wait_ge(sem("ln_centered"), f + 1)
            act.wait_ge(sem("ln_sq_summed"), f - 1) if f > 1 else None
            act.activation(tmp_s[:, f % 2, :], conv[:, f, :], ACT.Square).then_inc(sem("ln_sq"), 1)
        act.wait_ge(sem("ln_column"), 2)
        act.activation(rstd[:], ps[:, 4, :], ACT.Sqrt, scale=1.0 / (CONV_T * P), bias=eps).then_inc(sem("ln_rms"), 1)
        for f in range(CONV_T):
            act.wait_ge(sem("ln_scaled"), f + 1)
            act.wait_ge(sem("yc_lo_done"), f - 1) if f > 1 else None
            chain(act.activation(tmp_s[:, f % 2, :], tmp_v[:, f % 2, :], ACT.Silu, scale=vcol("ln_g", f),
                                 bias=vcol("ln_b", f)))
            act.activation(yc_hi[:, f, :], tmp_s[:, f % 2, :], ACT.Copy).then_inc(sem("yc_hi_done"), 1)
        if not has("attn2"):
            return

        def exps2(h):
            for t in range(NT):
                act.wait_ge(sem("neg_max2"), NT * h + t + 1)
                act.wait_ge(sem("turned2"), 6 * h) if h else None
                act.activation(probs[:, t, :], s2(t)[:, 0:KEYS2], ACT.Exp, bias=neg_max[:, h % 2, t:t + 1],
                               accum_out=row_sum[:, h % 2, t:t + 1]).then_inc(sem("exp2_done"), 1)

        def o2_hi(h):
            act.wait_ge(sem("pv2_done"), 6 * (h + 1))
            act.activation(q2_hi[:, h, :], ps[:, 6 + h % 2, :], ACT.Copy).then_inc(sem("o2_hi_done"), 1)

        for h in range(H2 + 1):
            if h < H2:
                if h:
                    for j in range(6):
                        r = 6 * (h - 1) + j
                        act.wait_ge(sem("turned2"), r + 1)
                        act.wait_ge(sem("pv2_done"), r - 1) if r > 1 else None
                        act.activation(pt2_hi[:, r % 2, :], ps[:, 4 + r % 2, :], ACT.Copy).then_inc(sem("pt2_hi_done"), 1)
                    o2_hi(h - 1)
                exps2(h)
            else:
                for j in range(6):
                    r = 6 * (h - 1) + j
                    act.wait_ge(sem("turned2"), r + 1)
                    act.wait_ge(sem("pv2_done"), r - 1)
                    act.activation(pt2_hi[:, r % 2, :], ps[:, 4 + r % 2, :], ACT.Copy).then_inc(sem("pt2_hi_done"), 1)
                o2_hi(h - 1)
        if not has("gate2"):
            return
        sigmoids("gate2")
        if not has("conv_out"):
            return
        only_split("conv_out")
        if not has("attn_out"):
            return
        hi_of_tmp("attn_out", h_hi, 8)
        if not has("out2"):
            return
        only_split("out2")
        if not has("norm_ffn"):
            return
        norm("norm_ffn", X, T, h_hi, 24)
        if not has("ffn"):
            return
        at = 0
        for c in range(3):
            g = f"up_{c}"

            def up(i, u, ahead):
                split_hi(i, u, g) if ahead else None
                act.wait_ge(used, i * RING + done(BASE[g] + u))
                b, f = u // 2, i * 2 + (8 * c + u // 2)
                if u % 2 == 0:
                    act.activation(tmp_s[:, b, :], ps[:, 0, :], ACT.Identity,
                                   scale=vec[:, bass.ds(f + (V_AT["ffn_w"] + FFN_T), 1)],
                                   bias=vec[:, bass.ds(f + V_AT["ffn_b"], 1)]).then_inc(sem("tap_mid"), 1)
                else:
                    act.wait_ge(sem("taps_done"), i * 2 + (8 * c + b + 1))
                    act.activation(tmp_s[:, b, :], tmp_s[:, b, :], ACT.Gelu_apprx_tanh).then_inc(sem("gelu_done"), 1)
                    act.wait_ge(sem("hidden_val"), i * 2 + (8 * c + b + 1))
                    act.activation(f_hi[:, bass.ds(i * 2 + b, 1), :], tmp_v[:, b:b + 1, :], ACT.Copy)\
                       .then_inc(sem("hidden_hi"), 1)
            loop(act, g, up)
            only_split(f"down_{c}")
        if not has("final2"):
            return
        norm("final2", X, T, None, None)

    @block.vector
    def _(dve):
        step = {"n": 0}

        def chain(ins):
            ins.then_inc(chain_v, 1)
            step["n"] += 1
            dve.wait_ge(chain_v, step["n"])

        def split_lo(i, u, group):
            if isinstance(i, int) and BASE[group] + RING * i + u + AHEAD >= total:
                return
            slot = (u + AHEAD) % RING
            dve.wait_ge(hi_ready, i * RING + (BASE[group] + u + AHEAD + 1))
            dve.tensor_tensor(w_lo[:, slot], raw[:, slot], w_hi[:, slot].bitcast(F32), ALU.subtract).then_inc(lo_ready, 1)

        def norm(name, src, N, dst_hi, dst_lo, gain, shift):
            k = NORMS[name]
            for f in range(KT):
                dve.wait_ge(n_sq, 8 * k + f + 1)
                if f == 0:
                    dve.tensor_copy(sq_acc[:, :N], tmp_s[:, 0, :N]).then_inc(n_acc, 1)
                else:
                    dve.wait_ge(n_acc, 8 * k + f)
                    dve.tensor_tensor(sq_acc[:, :N], sq_acc[:, :N], tmp_s[:, f % 2, :N], ALU.add).then_inc(n_acc, 1)
            dve.wait_ge(n_rms, n_sum_at[name])
            chain(dve.reciprocal(rstd[:, :N], rstd[:, :N]))
            if dst_hi is None:
                for f in range(KT):
                    dve.scalar_tensor_tensor(src[:, f, :], src[:, f, :], gain(f), rstd[:, :N], ALU.mult, ALU.mult)\
                       .then_inc(sem(name + "_tile"), 1)
                dve.wait_ge(sem(name + "_tile"), KT)
                return

            def value(f):
                if f >= 2:
                    dve.wait_ge(n_lo, 8 * split_norm[name] + f - 1)
                dve.scalar_tensor_tensor(tmp_v[:, f % 2, :N], src[:, f, :], gain(f), rstd[:, :N], ALU.mult, ALU.mult)\
                   .then_inc(n_val, 1)

            value(0)
            for f in range(KT):
                if f + 1 < KT:
                    value(f + 1)
                dve.wait_ge(n_hi, 8 * split_norm[name] + f + 1)
                if shift is None:
                    dve.tensor_tensor(dst_lo[:, f, :], tmp_v[:, f % 2, :N], dst_hi[:, f, :].bitcast(F32), ALU.subtract)\
                       .then_inc(n_lo, 1)
                else:
                    dve.scalar_tensor_tensor(dst_lo[:, f, :], tmp_v[:, f % 2, :N], mod[:, shift + f:shift + f + 1],
                                             dst_hi[:, f, :].bitcast(F32), ALU.add, ALU.subtract).then_inc(n_lo, 1)

        def gain_of(name):
            return lambda f: vcol(name, f)

        def split_out(group, hi, lo):
            def body(i, u, ahead):
                split_lo(i, u, group) if ahead else None
                dve.wait_ge(sem(group + "_hi"), i * RING + (u + 1))
                f = bass.ds(i * RING + u, 1)
                dve.tensor_tensor(lo[:, f, :], ps[:, u % 2:u % 2 + 1, :], hi[:, f, :].bitcast(F32), ALU.subtract)\
                   .then_inc(bank_free, 1)
            loop(dve, group, body)

        def only_split(group):
            loop(dve, group, lambda i, u, ahead: split_lo(i, u, group) if ahead else None)

        dve.sem_inc(used, RING)
        dve.sem_inc(bank_free, 2)
        dve.memset(p_cmp[:], 0.0)
        dve.memset(blk_f[:].rearrange("p j (g c) -> p (j g) c", c=CW)[:, :, NCB:CW], 0.0).then_inc(setup, 1)
        for m in range(AHEAD if total else 0):
            dve.wait_ge(hi_ready, m + 1)
            dve.tensor_tensor(w_lo[:, m], raw[:, m], w_hi[:, m].bitcast(F32), ALU.subtract).then_inc(lo_ready, 1)
        dve.wait_ge(in_small, 64)
        dve.wait_ge(sem("rel_out"), 1)
        dve.scalar_tensor_tensor(r8[:, 0:T], ps[0:8, 5, :], S8, r_mask[:, 0:T], ALU.mult, ALU.add).then_inc(sem("rel_rows"), 1)
        dve.scalar_tensor_tensor(r8[:, T:640], ps[0:8, 6, 0:P], S8, r_mask[:, T:640], ALU.mult, ALU.add)\
           .then_inc(sem("rel_rows"), 1)
        norm("norm1", X, T, h_hi, h_lo, gain_of("g_attn"), None)
        if not has("fox_qk"):
            return
        dve.wait_ge(sem("rel_stored"), 16)
        split_out("fox_qk", q_hi, q_lo)
        if not has("fox_v"):
            return

        def v_copy(j, group, m):
            dve.wait_ge(used, done(BASE[group] + m))
            if j >= 2:
                dve.wait_ge(sem("v_turned"), j - 1)
            dve.tensor_copy(tmp_v[:, j % 2, :], ps[:, m % 2, :]).then_inc(bank_free, 1)

        def v_out(j, hi, lo):
            dve.wait_ge(sem("v_hi_done"), j + 1)
            dve.tensor_tensor(lo, ps[:, 4 + j % 2, :].rearrange("p (t n) -> p t n", n=P), hi.bitcast(F32), ALU.subtract)\
               .then_inc(sem("v_lo_done"), 1)

        def v_dst(v, j):
            return v[:, :, j * P:(j + 1) * P] if j < 4 else v[:, j - 4]

        for u in range(RING):
            split_lo(0, u, "fox_v")
            v_copy(u, "fox_v", u)
            v_out(u, v_dst(v_hi, u), v_dst(v_lo, u))
        if not has("nsa_kv"):
            return
        for m in range(8):
            i, u = divmod(m, RING)
            split_lo(i, u, "nsa_kv")
            dve.wait_ge(used, done(BASE["nsa_kv"] + m))
            if m == 0:
                dve.tensor_scalar(zf[:], ps[0:8, 0, :], bf[:, 0:1], None, ALU.add).then_inc(sem("forget_z"), 1)
                dve.wait_ge(sem("forget_z"), 1)
                dve.wait_ge(sem("forget_ln"), 1)
                chain(dve.scalar_tensor_tensor(zf[:], zf[:], 0.0, lf_a[:], ALU.min, ALU.subtract))
                chain(dve.tensor_scalar(zf[:], zf[:], -S8, None, ALU.mult))
                chain(dve.memset(lf_a[:], 1.0))
                dve.tensor_tensor_scan(cum[:], lf_a[:], zf[:], 0.0, ALU.mult, ALU.add).then_inc(sem("c_summed"), 1)
                dve.wait_ge(sem("c_summed"), 1)
                dve.wait_ge(sem("c_turned"), 1)
                dve.tensor_scalar(c_q8[:], ps[:, 4, 0:32].rearrange("p (t h) -> p t h", h=8), -1.0, None, ALU.mult)\
                   .then_inc(sem("c_q_ready"), 1)
                dve.wait_ge(sem("c_q_ready"), 1)
                dve.sem_inc(bank_free, 1)
            if m == 1:
                dve.wait_ge(sem("gate_turned"), 1)
                dve.tensor_copy(gate_t[:], ps[:, 5, 0:96].rearrange("p (t h) -> p t h", h=24)).then_inc(bank_free, 1)
            if m in (2, 3):
                dve.wait_ge(sem("kn_hi_done"), m - 1)
                dve.tensor_tensor(kn_lo[:, m - 2, :], ps[:, m % 2, :], kn_hi[:, m - 2, :].bitcast(F32), ALU.subtract)\
                   .then_inc(bank_free, 1)
            if m in (4, 5):
                pe = vec[:, V_AT["pe_k" if m == 4 else "pe_v"]:V_AT["pe_k" if m == 4 else "pe_v"] + 16]
                for par in range(2):
                    for g in range(2):
                        src = bass.AP(tensor=ps[:].tensor, offset=64 * g * 8 * T + (m % 2) * T + par,
                                      ap=[[8 * T, 64], [2, 16], [CMP_STRIDE, NCB]])
                        dst = blk_f[64 * par:64 * par + 64, :, CW * g:CW * g + NCB]
                        pe_b = pe[64 * par:64 * par + 64, :].unsqueeze(2).to_broadcast([64, 16, NCB])
                        last = dve.tensor_tensor(dst, src, pe_b, ALU.add)
                last.then_inc(sem("blk_ready"), 1)
                dve.wait_ge(sem("blk_ready"), m - 3)
                dve.wait_ge(sem("blk_hi_done"), m - 3)
                dve.tensor_tensor(blk_lo[m - 4][:], blk_f[:], blk_hi[m - 4][:].bitcast(F32), ALU.subtract)\
                   .then_inc(sem("blk_lo_done"), 1)
                dve.wait_ge(sem("blk_lo_done"), m - 3)
                dve.sem_inc(bank_free, 1)
            if m in (6, 7):
                v_copy(m - 2, "nsa_kv", m)
                v_out(m - 2, v_dst(vn_hi, m - 2), v_dst(vn_lo, m - 2))
        if not has("nsa_q"):
            return
        split_out("nsa_q", nq_hi, nq_lo)
        if not has("cmp"):
            return
        for m in range(8):
            i, u = divmod(m, RING)
            split_lo(i, u, "cmp")
            if m == 3:
                dve.wait_ge(sem("kc_hi_done"), 2)
                for g in range(2):
                    last = dve.tensor_tensor(kc_lo[64 * g:64 * g + 64, :], ps[64 * g:64 * g + 64, 4, CW * g:CW * g + CW],
                                             kc_hi[64 * g:64 * g + 64, :].bitcast(F32), ALU.subtract)
                last.then_inc(bank_free, 4)
        dve.wait_ge(sem("vc_hi_done"), 1)
        dve.tensor_tensor(vc_lo[:], ps[0:CW, 5, 0:P], vc_hi[:].bitcast(F32), ALU.subtract)\
           .then_inc(bank_free, 4)
        dve.wait_ge(bank_free, BASE["cmp"] + 8 + 2)
        dve.sem_inc(sem("cmp_v_done"), 1)
        if not has("attn1"):
            return

        def score(s):
            kind, p, half, b = inst[s]
            if kind == "fox":
                dve.wait_ge(sem("fox_bias"), NT * (s + 1))
            else:
                n = load_of(s)
                dve.wait_ge(sem(f"bias_loaded_{n % 2}"), 16 * (n // 2 + 1))
                prev = [r for r in range(s) if (inst[r][0] == "cmp") == (kind == "cmp")]
                if len(prev) >= 2:
                    dve.wait_ge(sem("turned"), first_turn[prev[-2]] + len(turns(prev[-2])))
            for t in range(NT):
                buf, w = scores_of(s, t)
                dve.wait_ge(sem("qk_done"), NT * s + t + 1)
                if kind == "fox":
                    add = buf
                elif kind == "cmp":
                    c0 = T - P - t * P + CMP_BLOCK - 1
                    add = bias[:, load_of(s) % 2, c0:c0 + CMP_STRIDE * (w - 1) + 1:CMP_STRIDE]
                else:
                    add = bias[:, load_of(s) % 2, T - w:T]
                dve.tensor_tensor_reduce(out=buf, in0=ps[:, 2 + t % 2, 0:w], in1=add, scale=1.0 / S8, scalar=-3e38,
                                         op0=ALU.add, op1=ALU.max, accum_out=row_max[:, s % 2, t:t + 1])\
                   .then_inc(sem("scored"), 1)
            dve.wait_ge(sem("scored"), NT * (s + 1))
            dve.tensor_scalar(neg_max[:, s % 2, :], row_max[:, s % 2, :], -1.0, None, ALU.mult)\
               .then_inc(sem("neg_max_ready"), 1)

        def normalize(s):
            kind, p, half, b = inst[s]
            dve.wait_ge(sem("exp_done"), NT * (s + 1))
            f = factor[:, s % 2, :]
            chain(dve.reciprocal(f, row_sum[:, s % 2, :]))
            if b is not None:
                head = p + NSA_PAIRS * half
                f2 = factor2[:, s % 2, :]
                chain(dve.tensor_tensor(f2, f, gate_t[:, :, 3 * head + b], ALU.mult))
                f = f2
                if kind == "cmp":
                    chain(dve.tensor_tensor(f[:, 0:1], f[:, 0:1], cst[:, C_ROW:C_ROW + 1], ALU.mult))
            for t in range(NT):
                buf, w = scores_of(s, t)
                last = dve.tensor_scalar(buf, buf, f[:, t:t + 1], None, ALU.mult)
            last.then_inc(sem("normed"), 1)

        def o_lo(s):
            p, half = pair_of(s), inst[s][2]
            r = slice(64 * half, 64 * half + 64)
            hi, lo = (q_hi, q_lo) if p < FOX_PAIRS else (nq_hi, nq_lo)
            dve.wait_ge(sem("o_hi_done"), head_of(s) + 1)
            dve.tensor_tensor(lo[r, p % 4, :], ps[r, 6 + half, :], hi[r, p % 4, :].bitcast(F32), ALU.subtract)\
               .then_inc(sem("o_done"), 1)

        for s in range(NI + 2):
            if s >= 2 and head_end(s - 2):
                o_lo(s - 2)
            if s < NI:
                score(s)
            for j in (turns(s - 1) if 1 <= s <= NI else []):
                rows, at, w = pt_shape(s - 1, j)
                r = first_turn[s - 1] + j
                dve.wait_ge(sem("pt_hi_done"), r + 1)
                dve.tensor_tensor(pt_lo[0:rows, at:at + w], ps[0:rows, 4 + r % 2, 0:w],
                                  pt_hi[0:rows, at:at + w].bitcast(F32), ALU.subtract).then_inc(sem("pt_lo_done"), 1)
            if s < NI:
                normalize(s)
        if not has("gate"):
            return
        only_split("gate")
        if not has("branch"):
            return
        dve.wait_ge(bank_free, BASE["branch"] + 2)

        def branch(i, u, ahead):
            split_lo(i, u, "branch") if ahead else None
            b = 2 * (u % 2)
            f = i * RING + u
            dve.wait_ge(used, i * RING + done(BASE["branch"] + u))
            dve.tensor_tensor(tmp_s[:, 0:1, :], ps[:, b:b + 1, :], gates[:, bass.ds(f, 1), :], ALU.mult)
            dve.tensor_tensor(tmp_s[:, 1:2, :], ps[:, b + 1:b + 2, :], gates[:, bass.ds(f + 8, 1), :], ALU.mult)\
               .then_inc(sem("branch_gated"), 1)
            dve.wait_ge(sem("branch_gated"), f + 1)
            dve.tensor_tensor(tmp_v[:, u % 2, :], tmp_s[:, 0, :], tmp_s[:, 1, :], ALU.add).then_inc(sem("branch_val"), 1)
            dve.wait_ge(sem("branch_hi"), f + 1)
            dve.tensor_tensor(h_lo[:, bass.ds(f, 1), :], tmp_v[:, u % 2:u % 2 + 1, :], h_hi[:, bass.ds(f, 1), :].bitcast(F32),
                              ALU.subtract).then_inc(bank_free, 1)
        loop(dve, "branch", branch)
        if not has("out"):
            return
        dve.wait_ge(sem("x_reloaded"), 16)

        def add_to_x(group, gain=None):
            def body(i, u, ahead):
                split_lo(i, u, group) if ahead else None
                dve.wait_ge(used, i * RING + done(BASE[group] + u))
                x = X[:, bass.ds(i * RING + u, 1), :]
                if gain is None:
                    dve.tensor_tensor(x, ps[:, u % 2:u % 2 + 1, :], x, ALU.add).then_inc(bank_free, 1)
                else:
                    dve.scalar_tensor_tensor(x, ps[:, u % 2:u % 2 + 1, :], mod[:, bass.ds(i * RING + (gain + u), 1)], x,
                                             ALU.mult, ALU.add).then_inc(bank_free, 1)
            loop(dve, group, body)
            dve.wait_ge(bank_free, BASE[group] + COUNT[group] + 2)
            dve.sem_inc(x_new, 8)

        add_to_x("out")
        if not has("norm_mlp"):
            return
        norm("norm_mlp", X, T, h_hi, h_lo, gain_of("g_mlp"), None)
        if not has("ff"):
            return
        dve.memset(mod_a[:], 0.0)
        dve.memset(mod_x[:], 0.0).then_inc(sem("mod_step"), 1)
        dve.wait_ge(sem("silu_c_ready"), 1)

        def mod_sums(c, part, i, u):
            if u != 1:
                return
            n = 4 * c + 2 * part
            dve.wait_ge(sem(f"w_mod_loaded_{part}"), i * 16 + 16 * (2 * c + 1))
            dve.wait_ge(sem("mod_step"), i + (n + 1))
            k = bass.ds(i + 2 * c, 1)
            acc = mod_a[:, part * 3 * D:(part + 1) * 3 * D]
            ins = dve.scalar_tensor_tensor(acc, wm[:, part], silu_c[:, k], acc, ALU.mult, ALU.add)
            if part == 0:
                ins.then_inc(sem("mod_x_step"), 1)
                ins = dve.scalar_tensor_tensor(mod_x[:], wm[:, 0, 0:2 * D], silu_c[:, bass.ds(i + 2 * c + 8, 1)], mod_x[:],
                                               ALU.mult, ALU.add)
            ins.then_inc(sem("mod_step"), 1)

        for c in range(4):
            g = f"ff1_{c}"

            def ff1(i, u, ahead):
                split_lo(i, u, g) if ahead else None
                mod_sums(c, 0, i, u)
                dve.wait_ge(sem("relu_done"), i * RING + (8 * c + u + 1))
                dve.tensor_tensor(tmp_v[:, u % 2, :], tmp_s[:, u % 2, :], tmp_s[:, u % 2, :], ALU.mult)\
                   .then_inc(sem("relu_squared"), 1)
                dve.wait_ge(sem("f_hi_done"), i * RING + (8 * c + u + 1))
                f = bass.ds(i * RING + u, 1)
                dve.tensor_tensor(f_lo[:, f, :], tmp_v[:, u % 2:u % 2 + 1, :], f_hi[:, f, :].bitcast(F32), ALU.subtract)\
                   .then_inc(bank_free, 1)
            loop(dve, g, ff1)
            g2 = f"ff2_{c}"

            def ff2(i, u, ahead):
                split_lo(i, u, g2) if ahead else None
                mod_sums(c, 1, i, u)
                dve.wait_ge(used, i * RING + done(BASE[g2] + u))
                x = X[:, bass.ds(i * RING + u, 1), :]
                dve.tensor_tensor(x, ps[:, u % 2:u % 2 + 1, :], x, ALU.add).then_inc(bank_free, 1)
            loop(dve, g2, ff2)
            dve.wait_ge(bank_free, BASE[g2] + COUNT[g2] + 2)
            dve.sem_inc(x_new, 8)
        if not has("final1"):
            return
        norm("final1", X, T, None, None, gain_of("g_final"), None)
        if not has("mod"):
            return
        dve.wait_ge(sem("mod_out"), 1)
        b_mod = vec[:, V_AT["b_mod"]:V_AT["b_mod"] + 48]
        dve.tensor_tensor(mod[:, 0:48], ps[:, 5, 0:48], b_mod, ALU.add)
        chain(dve.tensor_tensor(mod[:, 48:64], ps[:, 5, 48:64], b_mod[:, 0:16], ALU.add))
        chain(dve.tensor_scalar(gains[:, 0:8], mod[:, 8:16], 1.0, None, ALU.add))
        chain(dve.tensor_scalar(gains[:, 8:16], mod[:, 56:64], 1.0, None, ALU.add))
        chain(dve.tensor_scalar(gains[:, 16:24], mod[:, 32:40], 1.0, None, ALU.add))
        for n, name in enumerate(("norm1", "norm1", "norm2")):
            g = gains[:, 8 * n:8 * n + 8]
            chain(dve.tensor_tensor(g, g, vec[:, V_AT[name]:V_AT[name] + 8], ALU.mult))
        dve.sem_inc(sem("mod_summed"), 1)
        if not has("norm2"):
            return
        dve.sem_inc(x_new, 8)
        norm("norm2", X, T, h_hi, h_lo, lambda f: gains[:, f:f + 1], 0)
        dve.wait_ge(sem("ctx_loaded"), 16)
        norm("norm2c", x_ctx, CTX, hc_hi, hc_lo, lambda f: gains[:, 8 + f:9 + f], 48)
        if not has("kv2"):
            return

        def inv_rms(N, m):
            dve.wait_ge(sem("h_rms"), m)
            chain(dve.reciprocal(rstd[:, :N], rstd[:, :N]))

        for u in range(RING):
            split_lo(0, u, "kv2")
            if u < 2:
                dve.wait_ge(sem("h_aux"), 2 * u + 1)
                inv_rms(T, 2 * u + 1)
                chain(dve.tensor_tensor(tmp_v[:, 1, :], ps[:, 5, :], cst[:, C_SIN:C_SIN + T], ALU.mult))
                chain(dve.tensor_tensor(tmp_v[:, 0, :], qg[:, 0, :], cst[:, C_COS:C_COS + T], ALU.mult))
                chain(dve.tensor_tensor(tmp_v[:, 0, :], tmp_v[:, 0, :], tmp_v[:, 1, :], ALU.add))
                dve.tensor_tensor(tmp_v[:, 0, :], tmp_v[:, 0, :], rstd[:], ALU.mult).then_inc(sem("h_val"), 1)
                dve.wait_ge(sem("h_hi_done"), 2 * u + 1)
                dve.tensor_tensor(k2_lo[:, u, CTX:KEYS2], tmp_v[:, 0, :], k2_hi[:, u, CTX:KEYS2].bitcast(F32), ALU.subtract)\
                   .then_inc(sem("h_lo_done"), 1)
                dve.wait_ge(sem("h_aux"), 2 * u + 2)
                inv_rms(CTX, 2 * u + 2)
                dve.tensor_tensor(tmp_v[:, 0, :CTX], qg[:, 1, :CTX], rstd[:, :CTX], ALU.mult).then_inc(sem("h_val"), 1)
                dve.wait_ge(sem("h_hi_done"), 2 * u + 2)
                dve.tensor_tensor(k2_lo[:, u, 0:CTX], tmp_v[:, 0, :CTX], k2_hi[:, u, 0:CTX].bitcast(F32), ALU.subtract)\
                   .then_inc(sem("h_lo_done"), 1)
                dve.wait_ge(sem("h_lo_done"), 2 * u + 2)
                dve.sem_inc(bank_free, 1)
            else:
                g = u - 2
                dve.wait_ge(used, done(BASE["kv2"] + u))
                if g:
                    dve.wait_ge(sem("v2_turned"), 2)
                dve.tensor_copy(tmp_v[:, 0, :], ps[:, u % 2, :])
                dve.tensor_copy(tmp_v[:, 1, 0:CTX], ps[:, 2 + u % 2, 0:CTX]).then_inc(bank_free, 1)
                v = v2_lo[:, 2:6, g * P:(g + 1) * P]
                vh = v2_hi[:, 2:6, g * P:(g + 1) * P]
                dve.wait_ge(sem("v2_hi_done"), 2 * g + 1)
                dve.tensor_tensor(v, ps[:, 4, :].rearrange("p (t n) -> p t n", n=P), vh.bitcast(F32), ALU.subtract)\
                   .then_inc(sem("v2_lo_done"), 1)
                dve.wait_ge(sem("v2_hi_done"), 2 * g + 2)
                dve.tensor_tensor(v2_lo[:, 0:2, g * P:(g + 1) * P], ps[:, 5, 0:CTX].rearrange("p (t n) -> p t n", n=P),
                                  v2_hi[:, 0:2, g * P:(g + 1) * P].bitcast(F32), ALU.subtract).then_inc(sem("v2_lo_done"), 1)
        if not has("glu"):
            return
        for e in (0, VP - TAPS // 2):
            dve.memset(u_pad[:, :, e:e + TAPS // 2], 0.0)

        def glu(i, u, ahead):
            split_lo(i, u, "glu") if ahead else None
            if u % 2:
                f = i * 2 + u // 2
                dve.wait_ge(sem("glu_sig"), f + 1)
                dve.tensor_tensor(u_pad[:, bass.ds(f, 1), TAPS // 2:TAPS // 2 + T], ps[:, 0:1, :], tmp_s[:, u // 2:u // 2 + 1, :],
                                  ALU.mult).then_inc(bank_free, 2)
        loop(dve, "glu", glu)
        dve.wait_ge(bank_free, BASE["glu"] + 8 + 2)
        if not has("q2"):
            return

        def conv_taps(i, u):
            f = i * 2 + u // 2
            acc = conv[:, bass.ds(f, 1), :]
            for tap in (range(16) if u % 2 == 0 else range(16, TAPS)):
                x = u_pad[:, bass.ds(f, 1), tap:tap + T]
                w = vec[:, bass.ds(f * TAPS + (V_AT["dw_w"] + tap), 1)]
                if tap == 0:
                    dve.tensor_scalar(acc, x, w, vec[:, bass.ds(f + V_AT["dw_b"], 1)], ALU.mult, ALU.add)\
                       .then_inc(sem("conv_step"), 1)
                else:
                    dve.wait_ge(sem("conv_step"), f * TAPS + tap)
                    dve.scalar_tensor_tensor(acc, x, w, acc, ALU.mult, ALU.add).then_inc(sem("conv_step"), 1)

        def q2_tail(i, u):
            n = i * RING + u
            dve.wait_ge(sem("q_aux"), n + 1)
            dve.tensor_tensor(tmp_v[:, 1, :], ps[:, 5, :], cst[:, C_SIN:C_SIN + T], ALU.mult)
            dve.wait_ge(sem("q_rms"), n + 1)
            dve.reciprocal(rstd[:], rstd[:]).then_inc(sem("q_inv"), 1)
            dve.tensor_tensor(tmp_v[:, 0, :], qg[:, u % 2, :], cst[:, C_COS:C_COS + T], ALU.mult).then_inc(sem("q_cos"), 1)
            dve.wait_ge(sem("q_cos"), n + 1)
            dve.tensor_tensor(tmp_v[:, 0, :], tmp_v[:, 0, :], tmp_v[:, 1, :], ALU.add).then_inc(sem("q_turned"), 1)
            dve.wait_ge(sem("q_turned"), n + 1)
            dve.wait_ge(sem("q_inv"), n + 1)
            dve.tensor_tensor(tmp_v[:, 0, :], tmp_v[:, 0, :], rstd[:], ALU.mult).then_inc(sem("q_val"), 1)
            dve.wait_ge(sem("q_hi_done"), n + 1)
            dve.tensor_tensor(q2_lo[:, bass.ds(n, 1), :], tmp_v[:, 0:1, :], q2_hi[:, bass.ds(n, 1), :].bitcast(F32), ALU.subtract)\
               .then_inc(bank_free, 1)

        def q2(i, u, ahead):
            split_lo(i, u, "q2") if ahead else None
            if u:
                q2_tail(i, u - 1)
            conv_taps(i, u)
            if u == RING - 1:
                q2_tail(i, u)
        loop(dve, "q2", q2)
        if not has("conv_ln"):
            return
        dve.wait_ge(sem("conv_step"), CONV_T * TAPS)
        chain(dve.tensor_tensor(sq_acc[:], conv[:, 0, :], conv[:, 1, :], ALU.add))
        chain(dve.tensor_tensor(sq_acc[:], sq_acc[:], conv[:, 2, :], ALU.add))
        dve.tensor_tensor(sq_acc[:], sq_acc[:], conv[:, 3, :], ALU.add).then_inc(sem("ln_summed"), 1)
        dve.wait_ge(sem("ln_column"), 1)
        chain(dve.tensor_scalar(rstd[:], ps[:, 4, :], 1.0 / (CONV_T * P), None, ALU.mult))
        for f in range(CONV_T):
            dve.tensor_tensor(conv[:, f, :], conv[:, f, :], rstd[:], ALU.subtract).then_inc(sem("ln_centered"), 1)
        for f in range(CONV_T):
            dve.wait_ge(sem("ln_sq"), f + 1)
            if f == 0:
                dve.tensor_copy(sq_acc[:], tmp_s[:, 0, :]).then_inc(sem("ln_sq_summed"), 1)
            else:
                dve.wait_ge(sem("ln_sq_summed"), f)
                dve.tensor_tensor(sq_acc[:], sq_acc[:], tmp_s[:, f % 2, :], ALU.add).then_inc(sem("ln_sq_summed"), 1)
        dve.wait_ge(sem("ln_rms"), 1)
        chain(dve.reciprocal(rstd[:], rstd[:]))
        for f in range(CONV_T):
            dve.wait_ge(sem("yc_hi_done"), f - 1) if f > 1 else None
            dve.tensor_tensor(tmp_v[:, f % 2, :], conv[:, f, :], rstd[:], ALU.mult).then_inc(sem("ln_scaled"), 1)
            if f:
                dve.wait_ge(sem("yc_hi_done"), f)
                dve.tensor_tensor(yc_lo[:, f - 1, :], tmp_s[:, (f - 1) % 2, :], yc_hi[:, f - 1, :].bitcast(F32), ALU.subtract)\
                   .then_inc(sem("yc_lo_done"), 1)
        dve.wait_ge(sem("yc_hi_done"), CONV_T)
        dve.tensor_tensor(yc_lo[:, 3, :], tmp_s[:, 1, :], yc_hi[:, 3, :].bitcast(F32), ALU.subtract)\
           .then_inc(sem("yc_lo_done"), 1)
        if not has("attn2"):
            return

        def row_max2(h, t):
            dve.wait_ge(sem("qk2_done"), NT * h + t + 1)
            dve.tensor_reduce(neg_max[:, h % 2, t:t + 1], s2(t)[:, 0:KEYS2], AX, ALU.max, negate=True)\
               .then_inc(sem("neg_max2"), 1)

        def normalize2(h):
            dve.wait_ge(sem("exp2_done"), NT * (h + 1))
            chain(dve.reciprocal(factor[:, h % 2, :], row_sum[:, h % 2, :]))
            for t in range(NT):
                last = dve.tensor_scalar(probs[:, t, :], probs[:, t, :], factor[:, h % 2, t:t + 1], None, ALU.mult)
            last.then_inc(sem("normed2"), 1)

        for h in range(H2 + 1):
            if h < H2:
                row_max2(h, 0)
                row_max2(h, 1)
            if h:
                for j in range(6):
                    r = 6 * (h - 1) + j
                    dve.wait_ge(sem("pt2_hi_done"), r + 1)
                    dve.tensor_tensor(pt2_lo[:, r % 2, :], ps[:, 4 + r % 2, :], pt2_hi[:, r % 2, :].bitcast(F32), ALU.subtract)\
                       .then_inc(sem("pt2_lo_done"), 1)
                dve.wait_ge(sem("o2_hi_done"), h)
                dve.tensor_tensor(q2_lo[:, h - 1, :], ps[:, 6 + (h - 1) % 2, :], q2_hi[:, h - 1, :].bitcast(F32), ALU.subtract)\
                   .then_inc(sem("o2_done"), 1)
            if h < H2:
                row_max2(h, 2)
                row_max2(h, 3)
                normalize2(h)
        if not has("gate2"):
            return
        only_split("gate2")
        if not has("conv_out"):
            return
        dve.wait_ge(bank_free, BASE["conv_out"] + 2)

        def conv_out(i, u, ahead):
            split_lo(i, u, "conv_out") if ahead else None
            dve.wait_ge(used, i * RING + done(BASE["conv_out"] + u))
            b, g = 2 * (u % 2), gates[:, 8 + 2 * u:10 + 2 * u, :]
            dve.tensor_tensor(g, ps[:, b:b + 2, :], g, ALU.mult).then_inc(bank_free, 1)
        loop(dve, "conv_out", conv_out)
        if not has("attn_out"):
            return
        dve.wait_ge(bank_free, BASE["conv_out"] + 4 + 2)

        def attn_out(i, u, ahead):
            split_lo(i, u, "attn_out") if ahead else None
            f = i * RING + u
            dve.wait_ge(used, i * RING + done(BASE["attn_out"] + u))
            dve.tensor_tensor(tmp_s[:, 0:1, :], ps[:, u % 2:u % 2 + 1, :], gates[:, bass.ds(f, 1), :], ALU.mult)\
               .then_inc(sem("attn_gated"), 1)
            dve.wait_ge(sem("attn_gated"), f + 1)
            dve.tensor_tensor(tmp_v[:, u % 2:u % 2 + 1, :], tmp_s[:, 0:1, :], gates[:, bass.ds(f + 8, 1), :], ALU.add)\
               .then_inc(sem("attn_out_val"), 1)
            dve.wait_ge(sem("attn_out_hi"), f + 1)
            dve.tensor_tensor(h_lo[:, bass.ds(f, 1), :], tmp_v[:, u % 2:u % 2 + 1, :], h_hi[:, bass.ds(f, 1), :].bitcast(F32),
                              ALU.subtract).then_inc(bank_free, 1)
        loop(dve, "attn_out", attn_out)
        if not has("out2"):
            return
        add_to_x("out2", gain=16)
        if not has("norm_ffn"):
            return
        norm("norm_ffn", X, T, h_hi, h_lo, lambda f: gains[:, 16 + f:17 + f], 24)
        if not has("ffn"):
            return
        for c in range(3):
            g = f"up_{c}"

            def up(i, u, ahead):
                split_lo(i, u, g) if ahead else None
                b, n, F = u // 2, i * 2 + (8 * c + u // 2), FFN_T
                if u % 2 == 0:
                    dve.wait_ge(sem("tap_mid"), n + 1)
                    dve.scalar_tensor_tensor(tmp_s[:, b, 1:T], ps[:, 0, 0:T - 1], vec[:, bass.ds(n + V_AT["ffn_w"], 1)],
                                             tmp_s[:, b, 1:T], ALU.mult, ALU.add).then_inc(sem("tap_left"), 1)
                    dve.wait_ge(sem("tap_left"), n + 1)
                    dve.scalar_tensor_tensor(tmp_s[:, b, 0:T - 1], ps[:, 0, 1:T],
                                             vec[:, bass.ds(n + (V_AT["ffn_w"] + 2 * F), 1)],
                                             tmp_s[:, b, 0:T - 1], ALU.mult, ALU.add).then_inc(sem("taps_done"), 1)
                    dve.wait_ge(sem("taps_done"), n + 1)
                    dve.sem_inc(bank_free, 1)
                else:
                    dve.wait_ge(sem("gelu_done"), n + 1)
                    dve.tensor_tensor(tmp_v[:, b, :], ps[:, 1, :], tmp_s[:, b, :], ALU.mult).then_inc(sem("hidden_val"), 1)
                    dve.wait_ge(sem("hidden_hi"), n + 1)
                    f = bass.ds(i * 2 + b, 1)
                    dve.tensor_tensor(f_lo[:, f, :], tmp_v[:, b:b + 1, :], f_hi[:, f, :].bitcast(F32), ALU.subtract)\
                       .then_inc(bank_free, 1)
            loop(dve, g, up)
            add_to_x(f"down_{c}", gain=40)
        if not has("final2"):
            return
        norm("final2", X, T, None, None, gain_of("final2"), None)

    @block.tensor
    def _(pe):
        ident, ones = cst[:, C_ID:C_ID + P], cst[:, C_ONE:C_ONE + P]

        def panel(i, u, group, out, blocks, hi, lo, N=T, ready=None, last=True, first=True):
            if first:
                pe.wait_ge(lo_ready, i * RING + (BASE[group] + u + 1))
                pe.wait_ge(bank_free, i * RING + (BASE[group] + u + 1))
            for b, k in blocks:
                if ready is not None and u == 0:
                    pe.wait_ge(*ready(k))
                start, stop = (b, k) == blocks[0], (b, k) == blocks[-1]
                pe.matmul(out, w_hi[:, u, b, :], hi[:, k, :N], start=start, stop=False)
                pe.matmul(out, w_hi[:, u, b, :], lo[:, k, :N], start=False, stop=False)
                ins = pe.matmul(out, w_lo[:, u, b, :], hi[:, k, :N], start=False, stop=stop)
            if last:
                ins.then_inc(used, 1)

        ALL = [(k, k) for k in range(KT)]

        def panels(group, ready=None, hi=h_hi, lo=h_lo, blocks=ALL):
            loop(pe, group, lambda i, u, ahead: panel(i, u, group, ps[:, u % 2, :], blocks, hi, lo, ready=ready))

        def column_sum(name, N):
            pe.wait_ge(n_acc, 8 * (NORMS[name] + 1))
            pe.matmul(ps[:, 4, :N], ones, sq_acc[:, :N], start=True, stop=True).then_inc(n_sum, 1)

        def normed(name):
            return lambda k: (n_lo, 8 * split_norm[name] + k + 1)

        def evacuated(group, per=1):
            return lambda k: (bank_free, BASE[group] + per * (k + 1) + 2)

        pe.wait_ge(in_c, 16)
        pe.wait_ge(in_small, 64)
        pe.matmul(ps[0:8, 5, :], tab[:], hot[:, 0:T], start=True, stop=True)
        pe.matmul(ps[0:8, 6, 0:P], tab[:], hot[:, T:640], start=True, stop=True).then_inc(sem("rel_out"), 1)
        column_sum("norm1", T)
        if not has("fox_qk"):
            return
        panels("fox_qk", normed("norm1"))
        if not has("fox_v"):
            return

        def turn_v(j, group, m):
            pe.wait_ge(bank_free, BASE[group] + m + 1 + 2)
            if j >= 2:
                pe.wait_ge(sem("v_lo_done"), j - 1)
            for t in range(NT):
                ins = pe.transpose(ps[:, 4 + j % 2, t * P:(t + 1) * P], tmp_v[:, j % 2, t * P:(t + 1) * P], ident)
            ins.then_inc(sem("v_turned"), 1)

        for u in range(RING):
            panel(0, u, "fox_v", ps[:, u % 2, :], ALL, h_hi, h_lo)
            if u:
                turn_v(u - 1, "fox_v", u - 1)
        turn_v(3, "fox_v", 3)
        if not has("nsa_kv"):
            return
        for m in range(8):
            i, u = divmod(m, RING)
            panel(i, u, "nsa_kv", ps[:, m % 2, :], ALL, h_hi, h_lo)
            if m == 0:
                pe.wait_ge(sem("v_lo_done"), 4)
                pe.wait_ge(sem("c_summed"), 1)
                for t in range(NT):
                    ins = pe.transpose(ps[:, 4, 8 * t:8 * t + 8], cum[:, t * P:(t + 1) * P], ident[0:8, 0:8])
                ins.then_inc(sem("c_turned"), 1)
            if m == 1:
                pe.wait_ge(sem("gate_n"), 1)
                for t in range(NT):
                    ins = pe.transpose(ps[:, 5, 24 * t:24 * t + 24], sig_n[:, t * P:(t + 1) * P], ident[0:24, 0:24])
                ins.then_inc(sem("gate_turned"), 1)
            if m == 7:
                turn_v(4, "nsa_kv", 6)
        turn_v(5, "nsa_kv", 7)
        if not has("nsa_q"):
            return
        panels("nsa_q")
        if not has("cmp"):
            return
        pe.wait_ge(bank_free, BASE["cmp"] + 2)
        pe.wait_ge(sem("blk_lo_done"), 2)
        pe.wait_ge(sem("v_lo_done"), 6)
        for m in range(8):
            i, u = divmod(m, RING)
            kv = m // 4
            pe.wait_ge(lo_ready, BASE["cmp"] + m + 1)
            for b in range(8):
                jp, f = 4 * u + b // 2, b % 2
                out = ps[:, kv, 64 * f:64 * f + 64]
                x_hi, x_lo = blk_hi[kv][:, jp, :], blk_lo[kv][:, jp, :]
                end = u == 3 and b >= 6
                pe.matmul(out, w_hi[:, u, b, :], x_hi, start=(u == 0 and b == 0), stop=False, skip_group_check=True)
                pe.matmul(out, w_hi[:, u, b, :], x_lo, start=False, stop=False, skip_group_check=True)
                ins = pe.matmul(out, w_lo[:, u, b, :], x_hi, start=False, stop=end, skip_group_check=True)
            ins.then_inc(used, 1)
            if m == 3:
                pe.wait_ge(sem("w2_loaded"), 32)
                pe.wait_ge(sem("cmp_hidden"), 1)
                for f in range(2):
                    ins = pe.matmul(ps[:, 4, 0:64], w2k[:, f, :], hid_c[:, f, :], start=f == 0, stop=f == 1)
                ins.then_inc(sem("cmp_k_out"), 1)
        pe.wait_ge(sem("cmp_hidden"), 2)
        for g in range(2):
            for f in range(2):
                ins = pe.matmul(ps[0:CW, 5, 64 * g:64 * g + 64], hid_c[:, f, CW * g:CW * g + CW], w2v[:, f, :],
                                start=f == 0, stop=f == 1)
        ins.then_inc(sem("cmp_v_out"), 1)
        if not has("attn1"):
            return

        def keys_of(s):
            kind, p, half, b = inst[s]
            r = slice(64 * half, 64 * half + 64)
            if kind == "fox":
                return q_hi[r, p, :], q_lo[r, p, :], q_hi[r, 4 + p, :], q_lo[r, 4 + p, :]
            if kind == "cmp":
                return nq_hi[r, p, :], nq_lo[r, p, :], kc_hi[r, :], kc_lo[r, :]
            n = 0 if kind == "slc" else 1
            return nq_hi[r, p, :], nq_lo[r, p, :], kn_hi[r, n, :], kn_lo[r, n, :]

        def qk(s):
            qh, ql, kh, kl = keys_of(s)
            for t in range(NT):
                n = NT * s + t
                if n >= 2:
                    pe.wait_ge(sem("scored"), n - 1)
                w = 8 * t + 8 if inst[s][0] == "cmp" else (t + 1) * P
                out = ps[:, 2 + t % 2, 0:w]
                c = slice(t * P, (t + 1) * P)
                pe.matmul(out, qh[:, c], kh[:, 0:w], start=True, stop=False, skip_group_check=True)
                pe.matmul(out, qh[:, c], kl[:, 0:w], start=False, stop=False, skip_group_check=True)
                fox = inst[s][0] == "fox"
                ins = pe.matmul(out, ql[:, c], kh[:, 0:w], start=False, stop=not fox, skip_group_check=True)
                if fox:
                    ins = pe.matmul(ps[:, 2 + t % 2, w - P:w], cst_r[:, 0:P], cst_r[:, P:2 * P], start=False, stop=True,
                                    skip_group_check=True)
                ins.then_inc(sem("qk_done"), 1)

        def turn_p(s, j):
            r = first_turn[s] + j
            if r >= 2:
                pe.wait_ge(sem("pt_lo_done"), r - 1)
            if inst[s][0] == "cmp":
                for t in range(NT):
                    ins = pe.transpose(ps[0:CW, 4 + r % 2, t * P:(t + 1) * P], p_cmp[:, big_of[s], t, :], ident)
            else:
                for t in range(j, NT):
                    ins = pe.transpose(ps[:, 4 + r % 2, (t - j) * P:(t - j + 1) * P],
                                       sb[:, big_of[s], SB_AT[t] + j * P:SB_AT[t] + (j + 1) * P], ident)
            ins.then_inc(sem("turned"), 1)

        def pv(s, j):
            kind, p, half, b = inst[s]
            r = first_turn[s] + j
            rows, at, w = pt_shape(s, j)
            if kind == "fox":
                vh, vl = v_hi[:, j, p * P:(p + 1) * P], v_lo[:, j, p * P:(p + 1) * P]
            elif kind == "cmp":
                vh, vl = vc_hi[:], vc_lo[:]
            else:
                n = 0 if kind == "slc" else 1
                vh, vl = vn_hi[:, n, j], vn_lo[:, n, j]
            out = ps[:, 6 + half, T - w:T]
            begin = head_start(s) and j == 0
            end = head_end(s) and j == turns(s)[-1]
            if begin and head_of(s) >= 2:
                pe.wait_ge(sem("o_done"), head_of(s) - 1)
            pe.wait_ge(sem("pt_lo_done"), r + 1)
            pe.matmul(out, vh, pt_hi[0:rows, at:at + w], start=begin, stop=False, skip_group_check=True)
            pe.matmul(out, vh, pt_lo[0:rows, at:at + w], start=False, stop=False, skip_group_check=True)
            pe.matmul(out, vl, pt_hi[0:rows, at:at + w], start=False, stop=end, skip_group_check=True)\
              .then_inc(sem("pv_done"), 1)

        pe.wait_ge(sem("cmp_v_done"), 1)
        pe.wait_ge(setup, 3)
        for s in range(NI + 1):
            if s < NI:
                qk(s)
            if s:
                pe.wait_ge(sem("normed"), s)
                js = turns(s - 1)
                for j in js:
                    turn_p(s - 1, j)
                    if j:
                        pv(s - 1, j - 1)
                pv(s - 1, js[-1])
        if not has("gate"):
            return
        pe.wait_ge(sem("o_done"), 16)
        panels("gate")
        if not has("branch"):
            return
        pe.wait_ge(bank_free, BASE["branch"] + 2)

        def branch(i, u, ahead):
            b = 2 * (u % 2)
            panel(i, u, "branch", ps[:, b, :], [(k, k) for k in range(4)], q_hi, q_lo, last=False)
            panel(i, u, "branch", ps[:, b + 1, :], [(4 + k, k) for k in range(4)], nq_hi, nq_lo, first=False)
        loop(pe, "branch", branch)
        if not has("out"):
            return
        panels("out", evacuated("branch"))
        if not has("norm_mlp"):
            return
        column_sum("norm_mlp", T)
        if not has("ff"):
            return
        for c in range(4):
            panels(f"ff1_{c}", normed("norm_mlp"))
            panels(f"ff2_{c}", evacuated(f"ff1_{c}"), f_hi, f_lo)
        if not has("final1"):
            return
        column_sum("final1", T)
        if not has("mod"):
            return
        pe.wait_ge(sem("mod_step"), 17)
        for f in range(64):
            src = mod_a[:, f * P:(f + 1) * P] if f < 48 else mod_x[:, (f - 48) * P:(f - 47) * P]
            ins = pe.matmul(ps[:, 5, f:f + 1], src, ones[:, 0:1], start=True, stop=True)
        ins.then_inc(sem("mod_out"), 1)
        if not has("norm2"):
            return
        column_sum("norm2", T)
        column_sum("norm2c", CTX)
        if not has("kv2"):
            return
        rot = cst[:, C_ROT:C_ROT + P]
        for u in range(RING):
            panel(0, u, "kv2", ps[:, u % 2, :], ALL, h_hi, h_lo, ready=normed("norm2"), last=False)
            panel(0, u, "kv2", ps[:, 2 + u % 2, 0:CTX], ALL, hc_hi, hc_lo, N=CTX, ready=normed("norm2c"), first=False)
            if u < 2:
                pe.wait_ge(sem("h_gained"), 2 * u + 2)
                pe.matmul(ps[:, 4, :], ones, tmp_s[:, 0, :], start=True, stop=True)
                pe.matmul(ps[:, 5, :], rot, qg[:, 0, :], start=True, stop=True).then_inc(sem("h_aux"), 1)
                pe.wait_ge(sem("h_lo_done"), 2 * u + 1)
                pe.matmul(ps[:, 4, :CTX], ones, tmp_s[:, 1, :CTX], start=True, stop=True).then_inc(sem("h_aux"), 1)
            else:
                g = u - 2
                pe.wait_ge(bank_free, BASE["kv2"] + u + 1 + 2)
                if g:
                    pe.wait_ge(sem("v2_lo_done"), 2)
                for t in range(NT):
                    ins = pe.transpose(ps[:, 4, t * P:(t + 1) * P], tmp_v[:, 0, t * P:(t + 1) * P], ident)
                ins.then_inc(sem("v2_turned"), 1)
                for t in range(CTX // P):
                    ins = pe.transpose(ps[:, 5, t * P:(t + 1) * P], tmp_v[:, 1, t * P:(t + 1) * P], ident)
                ins.then_inc(sem("v2_turned"), 1)
        if not has("glu"):
            return
        panels("glu")
        if not has("q2"):
            return
        pe.wait_ge(bank_free, BASE["q2"] + 2)
        pe.wait_ge(sem("v2_lo_done"), 4)

        def q_aux(i, u):
            n = i * RING + u
            pe.wait_ge(sem("q_gained"), n + 1)
            if u:
                pe.wait_ge(sem("q_val"), n)
            pe.matmul(ps[:, 4, :], ones, tmp_s[:, u % 2, :], start=True, stop=True)
            pe.matmul(ps[:, 5, :], rot, qg[:, u % 2, :], start=True, stop=True).then_inc(sem("q_aux"), 1)

        def q2(i, u, ahead):
            panel(i, u, "q2", ps[:, u % 2, :], ALL, h_hi, h_lo)
            if u:
                q_aux(i, u - 1)
            if u == RING - 1:
                q_aux(i, u)
        loop(pe, "q2", q2)
        if not has("conv_ln"):
            return
        pe.wait_ge(bank_free, BASE["q2"] + 8 + 2)
        pe.wait_ge(sem("ln_summed"), 1)
        pe.matmul(ps[:, 4, :], ones, sq_acc[:], start=True, stop=True).then_inc(sem("ln_column"), 1)
        pe.wait_ge(sem("ln_sq_summed"), CONV_T)
        pe.matmul(ps[:, 4, :], ones, sq_acc[:], start=True, stop=True).then_inc(sem("ln_column"), 1)
        if not has("attn2"):
            return

        def qk2(h, t):
            n = NT * h + t
            if n >= 2:
                pe.wait_ge(sem("exp2_done"), n - 1)
            g, c = h // (H2 // KV2), slice(t * P, (t + 1) * P)
            for k0, w in ((0, T), (T, KEYS2 - T)):
                out = s2(t)[:, k0:k0 + w]
                pe.matmul(out, q2_hi[:, h, c], k2_hi[:, g, k0:k0 + w], start=True, stop=False)
                pe.matmul(out, q2_hi[:, h, c], k2_lo[:, g, k0:k0 + w], start=False, stop=False)
                ins = pe.matmul(out, q2_lo[:, h, c], k2_hi[:, g, k0:k0 + w], start=False, stop=True)
            ins.then_inc(sem("qk2_done"), 1)

        def pv2(h, j):
            r, g = 6 * h + j, h // (H2 // KV2)
            out = ps[:, 6 + h % 2, :]
            pe.wait_ge(sem("pt2_lo_done"), r + 1)
            c = slice(g * P, (g + 1) * P)
            pe.matmul(out, v2_hi[:, j, c], pt2_hi[:, r % 2, :], start=j == 0, stop=False)
            pe.matmul(out, v2_hi[:, j, c], pt2_lo[:, r % 2, :], start=False, stop=False)
            pe.matmul(out, v2_lo[:, j, c], pt2_hi[:, r % 2, :], start=False, stop=j == 5).then_inc(sem("pv2_done"), 1)

        pe.wait_ge(sem("yc_lo_done"), CONV_T)
        for h in range(H2 + 1):
            if h < H2:
                qk2(h, 0)
                qk2(h, 1)
            if h:
                pe.wait_ge(sem("normed2"), h)
                if h >= 3:
                    pe.wait_ge(sem("o2_done"), h - 2)
                for j in range(6):
                    r = 6 * (h - 1) + j
                    if r >= 2:
                        pe.wait_ge(sem("pt2_lo_done"), r - 1)
                    for t in range(NT):
                        ins = pe.transpose(ps[:, 4 + r % 2, t * P:(t + 1) * P], probs[:, t, j * P:(j + 1) * P], ident)
                    ins.then_inc(sem("turned2"), 1)
                    if j:
                        pv2(h - 1, j - 1)
                pv2(h - 1, 5)
            if h < H2:
                qk2(h, 2)
                qk2(h, 3)
        if not has("gate2"):
            return
        pe.wait_ge(sem("o2_done"), H2)
        panels("gate2")
        if not has("conv_out"):
            return
        pe.wait_ge(bank_free, BASE["conv_out"] + 2)

        def conv_out(i, u, ahead):
            b = 2 * (u % 2)
            panel(i, u, "conv_out", ps[:, b, :], [(k, k) for k in range(4)], yc_hi, yc_lo, last=False)
            panel(i, u, "conv_out", ps[:, b + 1, :], [(4 + k, k) for k in range(4)], yc_hi, yc_lo, first=False)
        loop(pe, "conv_out", conv_out)
        if not has("attn_out"):
            return
        pe.wait_ge(bank_free, BASE["attn_out"] + 2)
        panels("attn_out", None, q2_hi, q2_lo)
        if not has("out2"):
            return
        panels("out2", evacuated("attn_out"))
        if not has("norm_ffn"):
            return
        column_sum("norm_ffn", T)
        if not has("ffn"):
            return
        for c in range(3):
            panels(f"up_{c}", normed("norm_ffn"))
            panels(f"down_{c}", evacuated(f"up_{c}", 2), f_hi, f_lo, [(k, k) for k in range(HID[c])])
        if not has("final2"):
            return
        column_sum("final2", T)

    ctx.close()


def host_layout(i):
    f = np.float32
    g = {k: np.asarray(v) for k, v in i.items()}

    def tiles(w, k=KT):
        n = w.shape[1] // P
        return w.reshape(k, P, n, P).transpose(2, 1, 0, 3)

    def few(w):
        z = np.zeros((D, P), f)
        z[:, :w.shape[1]] = w
        return tiles(z)

    w_in = g["w_in"][0]
    cut = np.cumsum([512, 512, 512, 8, 512, 128, 128, 128, 128, 128, 128, 24, D, D])[:-1]
    fq, fk, fv, fl, nq, kc, vc, ks, vs, kw, vw, ng, ga, gb = np.split(w_in, cut, axis=1)
    nq = nq.reshape(D, 2, 4, 64).transpose(0, 2, 1, 3).reshape(D, 512)
    br_n = g["w_br_nsa"][0].reshape(2, 4, 64, D).transpose(1, 0, 2, 3).reshape(512, D)
    cmp = [g[n][0].reshape(4, 4, P, 2, P).transpose(0, 2, 1, 3, 4).reshape(4, P, 8, P) for n in ("cmp_w1_k", "cmp_w1_v")]
    part = {"fox_qk": tiles(np.concatenate([fq, fk], 1)), "fox_v": tiles(fv),
            "nsa_kv": np.concatenate([few(fl), few(ng), tiles(ks), tiles(kw), tiles(kc), tiles(vc), tiles(vs), tiles(vw)]),
            "nsa_q": tiles(nq), "cmp": np.concatenate(cmp), "gate": tiles(np.concatenate([ga, gb], 1)),
            "branch": np.concatenate([tiles(g["w_br_fox"][0], 4), tiles(br_n, 4)], 2), "out": tiles(g["w_out"][0])}
    for c in range(4):
        part[f"ff1_{c}"] = tiles(g["w_ff1"][0][:, c * D:(c + 1) * D])
        part[f"ff2_{c}"] = tiles(g["w_ff2"][0][c * D:(c + 1) * D])
    w_in2 = g["w_in_2"][0]
    q, k, v, ua, ub, g2 = np.split(w_in2, np.cumsum([D, 256, 256, 512, 512]), axis=1)
    part["kv2"] = tiles(np.concatenate([k, v], 1))
    part["glu"] = np.stack([tiles(ua), tiles(ub)], 1).reshape(8, P, KT, P)
    part["q2"], part["gate2"] = tiles(q), tiles(g2)
    co = tiles(g["w_conv_out_2"][0], 4)
    part["conv_out"] = co.reshape(4, 2, P, 4, P).transpose(0, 2, 1, 3, 4).reshape(4, P, 8, P)
    part["attn_out"], part["out2"] = tiles(g["w_attn_out_2"][0]), tiles(g["w_out_2"][0])
    up, down, at = g["w_up_2"][0], g["w_down_2"][0], 0
    hidden = FFN_T * P
    for c, n in enumerate(HID):
        a_, b_ = (up[:, o + at * P:o + (at + n) * P] for o in (0, hidden))
        part[f"up_{c}"] = np.stack([tiles(a_), tiles(b_)], 1).reshape(2 * n, P, KT, P)
        d = np.zeros((D, D), f)
        d[:n * P] = down[at * P:(at + n) * P]
        part[f"down_{c}"] = tiles(d)
        at += n
    panels = np.concatenate([part[n] for n, _ in GROUPS])
    assert panels.shape == (PANELS, P, 8, P), panels.shape

    consts = np.zeros((P, C_ALL), f)
    consts[:, C_ID:C_ID + P] = np.eye(P)
    consts[:, C_ONE:C_ONE + P] = 1.0
    r = np.arange(0, P, 2)
    consts[r + 1, C_ROT + r] = -1.0
    consts[r, C_ROT + r + 1] = 1.0
    tok, half = np.arange(T), 64
    inv = 10000.0 ** (-np.arange(0, half, 2, dtype=f) / f(half))
    ang = np.concatenate([(tok // 64).astype(f)[:, None] * inv, (tok % 64).astype(f)[:, None] * inv], 1).astype(f)
    consts[:, C_COS:C_COS + T] = np.repeat(np.cos(ang).T, 2, 0)
    consts[:, C_SIN:C_SIN + T] = np.repeat(np.sin(ang).T, 2, 0)
    p = np.arange(P)
    consts[:, C_MASK:C_MASK + P] = np.where(p[None, :] > p[:, None], S8 * NEG, 0.0)
    consts[:, C_ROW] = p >= CMP_BLOCK - 1
    consts[:, C_EPS], consts[:, C_EPS + 1] = EPS, EPS * P
    dist = T - 1 - np.arange(640)
    n = np.maximum(dist, 0)
    nf = np.maximum(n, 16).astype(f)
    log_b = 16 + (np.log(nf / f(16)) / f(np.log(8.0)) * f(16)).astype(np.int32)
    bucket = np.where(n < 16, n, np.minimum(log_b, 31))
    onehot = (bucket[None, :] == np.arange(32)[:, None]).astype(f)
    r_mask = np.broadcast_to(np.where(dist < 0, S8 * NEG, 0.0).astype(f), (8, 640))

    vec = np.zeros((P, V_ALL), f)

    def put(name, v):
        vec[:, V_AT[name]:V_AT[name] + v.shape[1]] = v

    def by_tile(v):
        return v.reshape(-1, P).T
    for name, src in [("g_attn", "g_attn"), ("g_mlp", "g_mlp"), ("g_final", "g_final"), ("norm1", "norm1_g_2"),
                      ("norm2", "norm2_g_2"), ("final2", "final_g_2"), ("ln_g", "conv_ln_g_2"), ("ln_b", "conv_ln_b_2"),
                      ("dw_b", "conv_dw_b_2"), ("ffn_b", "ffn_dw_b_2"), ("q_g", "q_norm_g_2"), ("k_g", "k_norm_g_2"),
                      ("c", "c_2"), ("c_ctx", "c_ctx_2"), ("b_mod", "b_mod_2")]:
        put(name, by_tile(g[src].reshape(-1)))
    put("dw_w", g["conv_dw_w_2"][0].reshape(TAPS, CONV_T, P).transpose(2, 1, 0).reshape(P, -1))
    put("ffn_w", g["ffn_dw_w_2"][0].reshape(3, FFN_T, P).transpose(2, 0, 1).reshape(P, -1))
    put("pe_k", g["cmp_pe_k"][0].reshape(16, P).T)
    put("pe_v", g["cmp_pe_v"][0].reshape(16, P).T)
    w2k = g["cmp_w2_k"][0].reshape(2, P, 64).transpose(1, 0, 2)
    return {
        "panels": panels, "x": g["x"][0].T.reshape(KT, P, T).transpose(1, 0, 2), "consts": consts, "vectors": vec,
        "onehot": onehot, "r_mask": r_mask, "table": g["rel_bias_table"], "b_forget": g["b_forget"].reshape(8, 1),
        "w2k": np.concatenate([w2k, w2k], 2), "w2v": g["cmp_w2_v"][0].reshape(2, P, 64).transpose(1, 0, 2),
        "ctx": g["ctx_2"][0].T.reshape(KT, P, CTX).transpose(1, 0, 2), "w_mod": g["w_mod_2"][0].reshape(KT, P, 6 * D),
    }


def kernel(**inputs):
    import concourse.bacc as bacc
    from concourse.bass_utils import run_bass_kernel_spmd

    nc = bacc.Bacc("TRN2", target_bir_lowering=False, num_devices=1)
    arrays, aps = {}, {}
    for name, v in host_layout(inputs).items():
        v = np.ascontiguousarray(v)
        arrays[f"in_{name}"] = v
        aps[name] = nc.dram_tensor(f"in_{name}", v.shape, mybir.dt.from_np(v.dtype), kind="ExternalInput").ap()
    out = nc.dram_tensor("out_dram", (P, KT, T), F32, kind="ExternalOutput").ap()
    build(nc, aps, out)
    r = run_bass_kernel_spmd(nc, [arrays], core_ids=[0])
    y = r.results[0]["out_dram"]
    return np.ascontiguousarray(np.transpose(y, (2, 1, 0)).reshape(1, T, D))
```

```python
from contextlib import ExitStack

import numpy as np

import concourse.bass as bass
from concourse import mybir

F32 = mybir.dt.float32
F32R = mybir.dt.float32r
ALU = mybir.AluOpType
ACT = mybir.ActivationFunctionType
AX = mybir.AxisListType.X

P = 128
T = 512
D = 1024
KT = D // P
NT = T // P
FOX_PAIRS = 4
NSA_PAIRS = 4
NSA_HEADS = 8
CMP_STRIDE, CMP_BLOCK = 16, 32
NCB = (T - CMP_BLOCK) // CMP_STRIDE + 1
CW = 32
FF = 4 * D
CTX = 256
H2, KV2 = 8, 2
KEYS2 = CTX + T
CONV_T = 4
TAPS = 31
DVE_TAPS = 24
POOL_TAPS = TAPS - DVE_TAPS
FFN_T = 22
EPS = 1e-6
NEG = -1e30
S8 = 8.0
SC2 = 128.0 ** -0.5
RING = 4
AHEAD = 2
REL_W = 639

C_ID, C_ONE, C_ROT, C_COS, C_SIN, C_MASK, C_ROW, C_EPS = 0, 128, 256, 384, 896, 1408, 1536, 1537
C_ALL = 1539
V_SPEC = [("g_attn", 8), ("g_mlp", 8), ("g_final", 8), ("norm1", 8), ("norm2", 8), ("final2", 8), ("ln_g", 4),
          ("ln_b", 4), ("dw_b", 4), ("dw_w", 4 * TAPS), ("ffn_w", FFN_T * 3), ("ffn_b", FFN_T), ("q_g", 1),
          ("k_g", 1), ("c", 8), ("c_ctx", 8), ("b_mod", 48), ("pe_k", 16), ("pe_v", 16)]
V_AT, V_ALL = {}, 0
for _n, _w in V_SPEC:
    V_AT[_n] = V_ALL
    V_ALL += _w

GROUPS = [("fox_qk", 8), ("fox_v", 4), ("nsa_kv", 8), ("nsa_q", 4), ("cmp", 8), ("gate", 16), ("branch", 8),
          ("out", 8)]
for _c in range(4):
    GROUPS += [(f"ff1_{_c}", 8), (f"ff2_{_c}", 8)]
GROUPS += [("glu", 8), ("kv2", 4), ("q2", 8), ("gate2", 16), ("attn_out", 8), ("conv_out", 4), ("out2", 8)]
HID = [8, 8, 6]
for _c in range(3):
    GROUPS += [(f"up_{_c}", 2 * HID[_c]), (f"down_{_c}", 8)]
BASE, PANELS = {}, 0
for _n, _w in GROUPS:
    BASE[_n] = PANELS
    PANELS += _w
COUNT = dict(GROUPS)


def build(nc, a, out):
    ctx = ExitStack()
    base0 = (nc.sbuf_base + 63) // 64 * 64
    room = (nc.sbuf_usable_end - base0) // 4
    mark = {"at": 0}

    def place(name, shape, dt, at=None):
        n = int(np.prod(shape[1:]))
        n = (n + 7) // 8 * 8
        if at is None:
            at = mark["at"]
            mark["at"] += n
        assert at + n <= room, (name, at, n, room)
        return nc.alloc_sbuf_tensor_at(name, list(shape), dt, offset=base0 + 4 * at)

    raw = place("raw", [P, RING, 8, P], F32)
    w_hi = place("w_hi", [P, RING, 8, P], F32R)
    w_lo = place("w_lo", [P, RING, 8, P], F32R)
    h_hi = place("h_hi", [P, KT, T], F32R)
    h_lo = place("h_lo", [P, KT, T], F32R)
    x_at = mark["at"]
    X = place("X", [P, KT, T], F32)
    cst = place("cst", [P, C_ALL], F32)
    vec = place("vec", [P, V_ALL], F32)
    cst_r = place("cst_r", [P, 2 * P], F32R)
    rstd_at = mark["at"]
    rstd = place("rstd", [P, T], F32)
    sq_acc = place("sq_acc", [P, T], F32)
    tmp_at = mark["at"]
    tmp_v = place("tmp_v", [P, 2, T], F32)
    tmp_s = place("tmp_s", [P, 2, T], F32)
    small_at = mark["at"]
    small = place("small", [P, 736], F32)
    pool = mark["at"]

    eps, eps128 = cst[:, C_EPS:C_EPS + 1], cst[:, C_EPS + 1:C_EPS + 2]

    def vcol(name, k=0):
        return vec[:, V_AT[name] + k:V_AT[name] + k + 1]

    q_hi = place("q_hi", [P, 8, T], F32R, pool)
    q_lo = place("q_lo", [P, 8, T], F32R, pool + 4096)
    v_hi = place("v_hi", [P, NT, 512], F32R, pool + 8192)
    v_lo = place("v_lo", [P, NT, 512], F32R, pool + 10240)
    kn_hi = place("kn_hi", [P, 2, T], F32R, pool + 12800)
    kn_lo = place("kn_lo", [P, 2, T], F32R, pool + 13824)
    vn_hi = place("vn_hi", [P, 2, NT, P], F32R, pool + 14848)
    vn_lo = place("vn_lo", [P, 2, NT, P], F32R, pool + 15872)
    cmp_at = pool + 16896
    pt_hi = place("pt_hi", [P, 1280], F32R, cmp_at)
    pt_lo = place("pt_lo", [P, 1280], F32R, cmp_at + 1280)
    bias = place("bias", [P, 2, T], F32, cmp_at + 2560)
    sb = [place(f"sb{n}", [P, 1280], F32, at)
          for n, at in enumerate((rstd_at, rstd_at + 1280, cmp_at + 3584))]
    nq_hi = place("nq_hi", [P, 4, T], F32R, x_at)
    nq_lo = place("nq_lo", [P, 4, T], F32R, x_at + 2048)
    blk_f = place("blk_f", [P, 16, 64], F32, cmp_at)
    blk_hi = [place(f"blk_hi{j}", [P, 16, 64], F32R, cmp_at + 1024 + 2048 * j) for j in range(2)]
    blk_lo = [place(f"blk_lo{j}", [P, 16, 64], F32R, cmp_at + 2048 + 2048 * j) for j in range(2)]
    sig_n = place("sig_n", [24, T], F32, cmp_at + 3072)
    w2k = place("w2k", [P, 2, P], F32, tmp_at)
    w2v = place("w2v", [P, 2, 64], F32, tmp_at + 256)
    lf_a = place("lf_a", [8, T], F32, rstd_at)
    cum = place("cum", [8, T], F32, rstd_at + 512)
    zf = place("zf", [8, T], F32, tmp_at + 512)
    hot = place("hot", [32, 640], F32, pool)
    r8 = place("r8", [8, 640], F32, pool + 640)
    r_mask = place("r_mask", [8, 640], F32, pool + 1280)
    sm = {"at": small_at}

    def sml(name, shape, dt=F32):
        t = place(name, shape, dt, sm["at"])
        sm["at"] += (int(np.prod(shape[1:])) + 7) // 8 * 8
        assert sm["at"] <= small_at + 632, (name, sm["at"] - small_at)
        return t

    vc_hi = place("vc_hi", [CW, P], F32R, cmp_at + 5120)
    vc_lo = place("vc_lo", [CW, P], F32R, cmp_at + 5248)
    kc_hi = sml("kc_hi", [P, CW], F32R)
    kc_lo = sml("kc_lo", [P, CW], F32R)
    gate_t = sml("gate_t", [P, NT, 24])
    c_q8 = sml("c_q8", [P, NT, 8])
    row_max = sml("row_max", [P, 3, 4])
    neg_max = sml("neg_max", [P, 3, 4])
    row_sum = sml("row_sum", [P, 3, 4])
    factor = sml("factor", [P, 3, 4])
    factor2 = sml("factor2", [P, 3, 4])
    p_cmp = [sml("p_cmp0", [P, NT, CW]), sml("p_cmp1", [P, NT, CW]), place("p_cmp2", [P, NT, CW], F32, cmp_at + 5376)]
    hid_c = place("hid_c", [P, 2, 64], F32, cmp_at + 5504)
    tab = sml("tab", [32, 8])
    bf = sml("bf", [8, 1])
    silu_c = place("silu_c", [P, 16], F32, small_at + 632)
    mod = place("mod", [P, 64], F32, small_at + 648)
    gains = place("gains", [P, 24], F32, small_at + 712)
    gates = place("gates", [P, 16, T], F32, pool + 8192)
    f_hi = place("f_hi", [P, 8, T], F32R, pool)
    f_lo = place("f_lo", [P, 8, T], F32R, pool + 4096)
    mod_a = place("mod_a", [P, 6 * D], F32, pool + 8192)
    mod_x = place("mod_x", [P, 2 * D], F32, pool + 14336)
    wm = place("wm", [P, 2, 3 * D], F32, pool + 16384)
    x_ctx = place("x_ctx", [P, KT, CTX], F32, pool)
    q2_hi = place("q2_hi", [P, H2, T], F32R, pool)
    q2_lo = place("q2_lo", [P, H2, T], F32R, pool + 4096)
    k2_hi = place("k2_hi", [P, KV2, KEYS2], F32R, pool + 8192)
    k2_lo = place("k2_lo", [P, KV2, KEYS2], F32R, pool + 9728)
    v2_hi = place("v2_hi", [P, 6, KV2 * P], F32R, pool + 11264)
    v2_lo = place("v2_lo", [P, 6, KV2 * P], F32R, pool + 12800)
    hc_hi = place("hc_hi", [P, KT, CTX], F32R, pool + 14336)
    hc_lo = place("hc_lo", [P, KT, CTX], F32R, pool + 16384)
    VP = T + TAPS - 1
    u_pad = place("u_pad", [P, CONV_T, VP], F32, pool + 18432)
    conv = place("conv", [P, CONV_T, T], F32, pool + 20600)
    conv_p = place("conv_p", [P, T], F32, pool + 17408)
    yc_hi = place("yc_hi", [P, CONV_T, T], F32R, pool + 16384)
    yc_lo = place("yc_lo", [P, CONV_T, T], F32R, pool + 18432)
    kg = place("kg", [P, 2, T], F32, pool + 4096)
    qg = place("qg", [P, 2, T], F32, pool + 14336)
    c_sq = place("c_sq", [P, 2, CTX], F32, pool + 2048)
    c_acc = place("c_acc", [P, CTX], F32, pool + 2560)
    c_rstd = place("c_rstd", [P, CTX], F32, pool + 2816)
    probs = place("probs", [P, 2, 2, KEYS2], F32, pool + 14336)
    pt2_hi = place("pt2_hi", [P, 2, T], F32R, tmp_at)
    pt2_lo = place("pt2_lo", [P, 2, T], F32R, tmp_at + 1024)

    ps = nc.alloc_psum_tensor("ps", [P, 8, T], F32)
    scratch_c = nc.dram_tensor("scratch_c", (8, T), F32).ap()
    scratch_r = nc.dram_tensor("scratch_r", (8, P, 640), F32).ap()

    total = PANELS
    sems = {}

    def sem(name):
        if name not in sems:
            sems[name] = nc.alloc_semaphore(name)
        return sems[name]

    landed = [sem(f"panel_landed_{s}") for s in range(RING)]
    hi_ready = sem("panel_hi_ready")
    lo_ready = sem("panel_lo_ready")
    used = sem("panel_used")
    bank_free = sem("bank_free")
    in_x, in_c, in_v, in_small = sem("x_loaded"), sem("constants_loaded"), sem("vectors_loaded"), sem("small_loaded")
    n_sq, n_acc, n_sum, n_rms = (sem("norm_" + s) for s in ("square", "sum", "column_sum", "rms"))
    n_val, n_hi, n_lo = sem("norm_value"), sem("norm_hi"), sem("norm_lo")
    setup = sem("setup_done")
    x_new = sem("x_updated")
    chain_v, chain_s = sem("vector_step"), sem("scalar_step")

    def done(n):
        return n + 1 + RING

    split_norm = {"norm1": 0, "norm_mlp": 1, "norm2": 2, "norm_ffn": 3}
    NORMS = {"norm1": 0, "norm_mlp": 1, "final1": 2, "norm2": 3, "norm_ffn": 4, "final2": 5}
    X_STEP = {"norm_mlp": 8, "final1": 8 + 32, "norm2": 48, "norm_ffn": 56, "final2": 56 + 24}

    inst = [("fox", p, h, None) for p in range(FOX_PAIRS) for h in range(2)]
    for p in range(NSA_PAIRS):
        for h in range(2):
            inst += [("cmp", p, h, 0), ("slc", p, h, 1), ("win", p, h, 2)]
    NI = len(inst)
    big_of, turn_of, first_turn, n_turn, n_big, n_small = [], [], [], 0, 0, 0
    for k, p, h, b in inst:
        first_turn.append(n_turn)
        n_turn += 1 if k == "cmp" else NT
        big_of.append(n_small % 3 if k == "cmp" else n_big % 3)
        n_small += k == "cmp"
        n_big += k != "cmp"
    PT_AT = [0, 512, 896, 1152]

    def pair_of(s):
        return inst[s][1] + (0 if inst[s][0] == "fox" else FOX_PAIRS)

    def head_of(s):
        return 2 * pair_of(s) + inst[s][2]

    def head_end(s):
        return s + 1 == NI or head_of(s + 1) != head_of(s)

    def head_start(s):
        return s == 0 or head_of(s - 1) != head_of(s)

    def load_of(s):
        return s if s < 8 else 8 + (s - 8) // 3

    def turns(s):
        return [0] if inst[s][0] == "cmp" else list(range(NT))

    def turned(s, j):
        return 0 <= s < NI and j in turns(s)

    SB_AT = [0, P, 3 * P, 6 * P]

    def scores_of(s, t):
        if inst[s][0] == "cmp":
            w = 8 * t + 7
            return p_cmp[big_of[s]][:, t, 0:w], w
        w = (t + 1) * P
        return sb[big_of[s]][:, SB_AT[t]:SB_AT[t] + w], w

    def pt_shape(s, j):
        return (CW, 0, T) if inst[s][0] == "cmp" else (P, PT_AT[j], T - j * P)

    pt_wait, seen = {}, {}
    for s in range(NI):
        for j in turns(s):
            if j in seen:
                pt_wait[first_turn[s] + j] = seen[j] + 1
            seen[j] = first_turn[s] + j

    UNITS, PAIRS = 2 * H2, KEYS2 // (2 * P)

    def s2(e):
        b = 2 * (1 - e)
        return ps[:, b:b + 2, :].rearrange("p b n -> p (b n)")

    block = ctx.enter_context(nc.Block())

    def loop(eng, group, body):
        last = BASE[group] + COUNT[group] == total
        n = COUNT[group] // RING - last
        if n == 1:
            for u in range(RING):
                body(0, u, True)
        elif n > 1:
            with eng.Fori(0, n) as i:
                for u in range(RING):
                    body(i, u, True)
        if last:
            for u in range(RING):
                body(n, u, u + AHEAD < RING)

    @block.sync
    def _(sp):
        for u in range(RING):
            sp.dma_start(raw[:, u], a["panels"][u]).then_inc(landed[u], 16)
            if u == 0:
                sp.dma_start(X[:], a["x"]).then_inc(in_x, 16)
                sp.dma_start(cst[:], a["consts"]).then_inc(in_c, 16)
                sp.dma_start(vec[:], a["vectors"]).then_inc(in_v, 16)
        if total > RING:
            with sp.Fori(1, total // RING) as i:
                for u in range(RING):
                    sp.wait_ge(lo_ready, i * RING + (u - RING + 1))
                    sp.dma_start(raw[:, u], a["panels"][bass.ds(i * RING + u, 1)].rearrange("o p k n -> p (o k) n"))\
                      .then_inc(landed[u], 16)
        for f in range(KT):
            sp.wait_ge(sem("final2_tile"), f + 1)
            sp.dma_start(out[:, f, :], X[:, f, :]).then_inc(sem("out_stored"), 16)
        sp.wait_ge(sem("out_stored"), 16 * KT)

    @block.gpsimd
    def _(gp):
        gp.dma_start(hot[:], a["onehot"]).then_inc(in_small, 16)
        gp.dma_start(tab[:], a["table"]).then_inc(in_small, 16)
        gp.dma_start(bf[:], a["b_forget"]).then_inc(in_small, 16)
        gp.dma_start(r_mask[:], a["r_mask"]).then_inc(in_small, 16)
        gp.wait_ge(sem("rel_rows"), 2)
        gp.dma_start(scratch_r, r8[:].unsqueeze(1).to_broadcast([8, P, 640])).then_inc(sem("rel_stored"), 16)
        gp.wait_ge(sem("v_turned"), 5)
        gp.dma_start(w2k[:], a["w2k"]).then_inc(sem("w2_loaded"), 16)
        gp.dma_start(w2v[:], a["w2v"]).then_inc(sem("w2_loaded"), 16)
        gp.wait_ge(sem("c_summed"), 1)
        gp.dma_start(scratch_c, cum[:]).then_inc(sem("c_stored"), 16)
        gp.wait_ge(sem("c_stored"), 16)
        gp.wait_ge(sem("rel_stored"), 16)
        gp.wait_ge(sem("cmp_v_done"), 1)
        for n in range(16):
            if n >= 2:
                m = n - 2
                if m < 8:
                    gp.wait_ge(sem("fox_bias"), 4 * (m + 1))
                else:
                    gp.wait_ge(sem("scored"), 4 * (8 + 3 * (m - 8) + 3))
            if n < 8:
                src = bass.AP(tensor=scratch_c.tensor, offset=n * T, ap=[[0, P], [1, T]])
            else:
                head = (n - 8) // 2 + 4 * ((n - 8) % 2)
                src = bass.AP(tensor=scratch_r.tensor, offset=head * P * 640 + 127, ap=[[639, P], [1, T]])
            gp.dma_start(bias[:, n % 2, :], src).then_inc(sem(f"bias_loaded_{n % 2}"), 16)
        gp.wait_ge(used, done(BASE["branch"] + 7))
        gp.dma_start(X[:], a["x"]).then_inc(sem("x_reloaded"), 16)
        for n in range(16):
            c, part, i = n // 4, n // 2 % 2, n % 2
            if n == 0:
                gp.wait_ge(used, done(BASE["out"] - 1))
            if i == 1:
                gp.wait_ge(sem("mod_step"), n + 1)
            elif n >= 4:
                gp.wait_ge(sem("mod_step"), n - 1)
            gp.dma_start(wm[:, part], a["w_mod"][2 * c + i, :, part * 3 * D:(part + 1) * 3 * D])\
              .then_inc(sem(f"w_mod_loaded_{part}"), 16)
        gp.wait_ge(used, done(BASE["ff2_3"] + 7))
        gp.dma_start(x_ctx[:], a["ctx"]).then_inc(sem("ctx_loaded"), 16)
        gp.wait_ge(sem("ctx_loaded"), 16)
        for f in range(KT):
            gp.tensor_tensor(c_sq[:, f % 2, :], x_ctx[:, f, :], x_ctx[:, f, :], ALU.mult).then_inc(sem("ctx_sq"), 1)
            gp.wait_ge(sem("ctx_sq"), f + 1)
            if f == 0:
                gp.tensor_copy(c_acc[:], c_sq[:, 0, :]).then_inc(sem("ctx_acc"), 1)
            else:
                gp.wait_ge(sem("ctx_acc"), f)
                gp.tensor_tensor(c_acc[:], c_acc[:], c_sq[:, f % 2, :], ALU.add).then_inc(sem("ctx_acc"), 1)
        gp.wait_ge(sem("ctx_acc"), KT)
        gp.wait_ge(bank_free, BASE["kv2"] + 4 + 2)
        for f in range(CONV_T):
            for n, tap in enumerate(range(DVE_TAPS, TAPS)):
                x, w = u_pad[:, f, tap:tap + T], vcol("dw_w", f * TAPS + tap)
                if n == 0:
                    gp.tensor_scalar(conv[:, f, :], x, w, vcol("dw_b", f), ALU.mult, ALU.add).then_inc(sem("pool_tap"), 1)
                else:
                    gp.wait_ge(sem("pool_tap"), f * POOL_TAPS + n)
                    gp.tensor_scalar(conv_p[:], x, w, None, ALU.mult).then_inc(sem("pool_product"), 1)
                    gp.wait_ge(sem("pool_product"), f * (POOL_TAPS - 1) + n)
                    gp.tensor_tensor(conv[:, f, :], conv[:, f, :], conv_p[:], ALU.add).then_inc(sem("pool_tap"), 1)

    @block.scalar
    def _(act):
        step = {"n": 0}

        def split_hi(i, u, group):
            slot, turn = (u + AHEAD) % RING, (u + AHEAD) // RING
            act.wait_ge(landed[slot], (i + (BASE[group] // RING + turn + 1)) * 16)
            act.wait_ge(used, i * RING + (BASE[group] + u + AHEAD + 1))
            act.activation(w_hi[:, slot], raw[:, slot], ACT.Copy).then_inc(hi_ready, 1)

        def chain(ins):
            ins.then_inc(chain_s, 1)
            step["n"] += 1
            act.wait_ge(chain_s, step["n"])

        def norm(name, src, N, dst_hi, shift):
            k = NORMS[name]
            if name in X_STEP:
                act.wait_ge(x_new, X_STEP[name])
            for f in range(KT):
                act.wait_ge(n_acc, 8 * k + f - 1) if 8 * k + f > 1 else None
                act.activation(tmp_s[:, f % 2, :N], src[:, f, :], ACT.Square).then_inc(n_sq, 1)
            act.wait_ge(n_sum, NORMS[name] + 1)
            act.activation(rstd[:, :N], ps[:, 4, :N], ACT.Sqrt, scale=1.0 / D, bias=eps).then_inc(n_rms, 1)
            if dst_hi is not None:
                for f in range(KT):
                    act.wait_ge(n_val, 8 * split_norm[name] + f + 1)
                    if shift is None:
                        act.activation(dst_hi[:, f, :], tmp_v[:, f % 2, :N], ACT.Copy).then_inc(n_hi, 1)
                    else:
                        act.activation(dst_hi[:, f, :], tmp_v[:, f % 2, :N], ACT.Identity,
                                       bias=mod[:, shift + f:shift + f + 1]).then_inc(n_hi, 1)

        def split_out(group, dst):
            def body(i, u, ahead):
                split_hi(i, u, group) if ahead else None
                act.wait_ge(used, i * RING + done(BASE[group] + u))
                act.activation(dst[:, bass.ds(i * RING + u, 1), :], ps[:, u % 2:u % 2 + 1, :], ACT.Copy)\
                   .then_inc(sem(group + "_hi"), 1)
            loop(act, group, body)

        def only_split(group):
            loop(act, group, lambda i, u, ahead: split_hi(i, u, group) if ahead else None)

        def hi_of_tmp(group, dst, total_f, part="_val"):
            def body(i, u, ahead):
                split_hi(i, u, group) if ahead else None
                act.wait_ge(sem(group + part), i * RING + (u + 1))
                act.activation(dst[:, bass.ds(i * RING + u, 1), :], tmp_v[:, u % 2:u % 2 + 1, :], ACT.Copy)\
                   .then_inc(sem(group + "_hi"), 1)
            loop(act, group, body)

        act.wait_ge(in_c, 16)
        act.activation(cst_r[:, 0:P], cst[:, C_ID:C_ID + P], ACT.Copy).then_inc(setup, 1)
        act.activation(cst_r[:, P:2 * P], cst[:, C_MASK:C_MASK + P], ACT.Copy).then_inc(setup, 1)
        act.wait_ge(in_v, 16)
        act.activation(silu_c[:, :], vec[:, V_AT["c"]:V_AT["c"] + 16], ACT.Silu).then_inc(sem("silu_c_ready"), 1)
        for m in range(AHEAD):
            act.wait_ge(landed[m], 16)
            act.activation(w_hi[:, m], raw[:, m], ACT.Copy).then_inc(hi_ready, 1)
        act.wait_ge(in_x, 16)
        norm("norm1", X, T, h_hi, None)
        act.wait_ge(sem("rel_stored"), 16)
        split_out("fox_qk", q_hi)

        def v_out(t_sem, at, views):
            for j, dst in views:
                act.wait_ge(sem(t_sem), j + 1)
                act.activation(dst, ps[:, 4 + j % 2, :].rearrange("p (t n) -> p t n", n=P), ACT.Copy)\
                   .then_inc(sem("v_hi_done"), 1)

        for u in range(RING):
            split_hi(0, u, "fox_v")
            v_out("v_turned", 0, [(u, v_hi[:, :, u * P:(u + 1) * P])])
        for m in range(8):
            i, u = divmod(m, RING)
            split_hi(i, u, "nsa_kv")
            if m == 0:
                act.wait_ge(sem("forget_z"), 1)
                chain(act.activation(lf_a[:], zf[:], ACT.Abs))
                chain(act.activation(lf_a[:], lf_a[:], ACT.Exp, scale=-1.0))
                act.activation(lf_a[:], lf_a[:], ACT.Ln, bias=cst[0:8, C_ONE:C_ONE + 1]).then_inc(sem("forget_ln"), 1)
            if m == 1:
                act.wait_ge(used, done(BASE["nsa_kv"] + 1))
                act.activation(sig_n[:], ps[0:24, 1, :], ACT.Sigmoid).then_inc(sem("gate_n"), 1)
            if m in (2, 3):
                act.wait_ge(used, done(BASE["nsa_kv"] + m))
                act.activation(kn_hi[:, m - 2, :], ps[:, m % 2, :], ACT.Copy).then_inc(sem("kn_hi_done"), 1)
            if m in (4, 5):
                act.wait_ge(sem("blk_ready"), m - 3)
                act.activation(blk_hi[m - 4][:], blk_f[:], ACT.Copy).then_inc(sem("blk_hi_done"), 1)
            if m in (6, 7):
                v_out("v_turned", 0, [(m - 2, vn_hi[:, m - 6])])
        split_out("nsa_q", nq_hi)
        for m in range(8):
            i, u = divmod(m, RING)
            split_hi(i, u, "cmp")
            if m == 3:
                act.wait_ge(used, done(BASE["cmp"] + 3))
                act.activation(hid_c[:], ps[:, 0, 0:P].rearrange("p (f n) -> p f n", f=2), ACT.Silu)\
                   .then_inc(sem("cmp_hidden"), 1)
                act.wait_ge(sem("cmp_k_out"), 1)
                for g in range(2):
                    act.activation(kc_hi[64 * g:64 * g + 64, :], ps[64 * g:64 * g + 64, 4, CW * g:CW * g + CW], ACT.Copy)\
                       .then_inc(sem("kc_hi_done"), 1)
            if m == 7:
                act.wait_ge(used, done(BASE["cmp"] + 7))
                act.wait_ge(sem("cmp_k_out"), 1)
                act.activation(hid_c[:], ps[:, 1, 0:P].rearrange("p (f n) -> p f n", f=2), ACT.Silu)\
                   .then_inc(sem("cmp_hidden"), 1)
                act.wait_ge(sem("cmp_v_out"), 1)
                act.activation(vc_hi[:], ps[0:CW, 5, 0:P], ACT.Copy).then_inc(sem("vc_hi_done"), 1)

        def fox_bias(s):
            act.wait_ge(sem(f"bias_loaded_{s % 2}"), 16 * (s // 2 + 1))
            if s >= 3:
                act.wait_ge(sem("turned"), first_turn[s - 3] + NT)
            for t in range(NT):
                w = (t + 1) * P
                act.activation(sb[big_of[s]][:, SB_AT[t]:SB_AT[t] + w], bias[:, s % 2, 0:w], ACT.Identity,
                               bias=c_q8[:, t, s:s + 1]).then_inc(sem("fox_bias"), 1)

        def exp(s, t):
            if not 0 <= s < NI:
                return
            if t == 0:
                act.wait_ge(sem("neg_max_ready"), s + 1)
            buf, w = scores_of(s, t)
            act.activation(buf, buf, ACT.Exp, bias=neg_max[:, s % 3, t:t + 1],
                           accum_out=row_sum[:, s % 3, t:t + 1]).then_inc(sem("exp_done"), 1)

        def hi_turn(s, j):
            if not turned(s, j):
                return
            r = first_turn[s] + j
            act.wait_ge(sem("turned"), r + 1)
            if r in pt_wait:
                act.wait_ge(sem("pv_done"), pt_wait[r])
            rows, at, w = pt_shape(s, j)
            act.activation(pt_hi[0:rows, at:at + w], ps[0:rows, 4 + r % 2, 0:w], ACT.Copy).then_inc(sem("pt_hi_done"), 1)

        def o_hi(s):
            p, half = pair_of(s), inst[s][2]
            r = slice(64 * half, 64 * half + 64)
            act.wait_ge(sem("pv_done"), first_turn[s] + len(turns(s)))
            dst = q_hi[r, p, :] if p < FOX_PAIRS else nq_hi[r, p - FOX_PAIRS, :]
            act.activation(dst, ps[r, 6 + half, :], ACT.Copy).then_inc(sem("o_hi_done"), 1)

        act.wait_ge(sem("c_q_ready"), 1)
        act.wait_ge(sem("cmp_v_done"), 1)
        fox_bias(0)
        for s in range(NI + 3):
            exp(s - 1, 0)
            exp(s - 1, 1)
            hi_turn(s - 2, 0)
            exp(s - 1, 2)
            exp(s - 1, 3)
            hi_turn(s - 2, 1)
            hi_turn(s - 2, 2)
            hi_turn(s - 2, 3)
            if s >= 3 and head_end(s - 3):
                o_hi(s - 3)
            if s + 1 < FOX_PAIRS * 2:
                fox_bias(s + 1)

        def sigmoids(group):
            act.wait_ge(bank_free, BASE[group] + 2)
            def body(i, u, ahead):
                split_hi(i, u, group) if ahead else None
                act.wait_ge(used, i * RING + done(BASE[group] + u))
                act.activation(gates[:, bass.ds(i * RING + u, 1), :], ps[:, u % 2:u % 2 + 1, :], ACT.Sigmoid)\
                   .then_inc(bank_free, 1)
            loop(act, group, body)

        sigmoids("gate")
        hi_of_tmp("branch", h_hi, 8)
        only_split("out")
        norm("norm_mlp", X, T, h_hi, None)
        for c in range(4):
            g = f"ff1_{c}"

            def body(i, u, ahead):
                split_hi(i, u, g) if ahead else None
                act.wait_ge(used, i * RING + done(BASE[g] + u))
                act.activation(tmp_s[:, u % 2, :], ps[:, u % 2, :], ACT.Relu).then_inc(sem("relu_done"), 1)
                act.wait_ge(sem("relu_squared"), i * RING + (8 * c + u + 1))
                act.activation(f_hi[:, bass.ds(i * RING + u, 1), :], tmp_v[:, u % 2:u % 2 + 1, :], ACT.Copy)\
                   .then_inc(sem("f_hi_done"), 1)
            loop(act, g, body)
            only_split(f"ff2_{c}")
        norm("final1", X, T, None, None)
        norm("norm2", X, T, h_hi, 0)
        act.wait_ge(sem("ctx_sum"), 1)
        act.activation(c_rstd[:], ps[:, 5, :CTX], ACT.Sqrt, scale=1.0 / D, bias=eps).then_inc(sem("ctx_rms"), 1)

        def glu(i, u, ahead):
            split_hi(i, u, "glu") if ahead else None
            act.wait_ge(used, i * RING + done(BASE["glu"] + u))
            if u % 2:
                act.activation(tmp_s[:, u // 2, :], ps[:, 1, :], ACT.Sigmoid).then_inc(sem("glu_sig"), 1)
            act.wait_ge(sem("ctx_val"), i * RING + (u + 1))
            act.activation(hc_hi[:, bass.ds(i * RING + u, 1), :], tmp_v[:, u % 2:u % 2 + 1, :CTX], ACT.Identity,
                           bias=mod[:, bass.ds(i * RING + (48 + u), 1)]).then_inc(sem("ctx_hi"), 1)
        loop(act, "glu", glu)

        def k_squares(u):
            act.wait_ge(used, done(BASE["kv2"] + u))
            for m, (bank, N) in enumerate([(u, T), (2 + u, CTX)]):
                act.activation(tmp_s[:, m, :N], ps[:, bank, :N], ACT.Square).then_inc(sem("h_sq"), 1)
                act.activation(kg[:, m, :N], ps[:, bank, :N], ACT.Copy, scale=vcol("k_g")).then_inc(sem("h_gained"), 1)
            act.wait_ge(sem("h_gained"), 2 * u + 2)
            act.sem_inc(bank_free, 1)

        def k_tail(u):
            act.wait_ge(sem("h_aux"), u + 1)
            act.activation(rstd[:], ps[:, 4, :], ACT.Sqrt, scale=1.0 / P, bias=eps).then_inc(sem("h_rms"), 1)
            act.activation(sq_acc[:, :CTX], ps[:, 6, :CTX], ACT.Sqrt, scale=1.0 / P, bias=eps).then_inc(sem("h_rms"), 1)
            for m, (dst, N) in enumerate([(k2_hi[:, u, CTX:KEYS2], T), (k2_hi[:, u, 0:CTX], CTX)]):
                act.wait_ge(sem("h_val"), 2 * u + m + 1)
                act.activation(dst, tmp_v[:, m, :N], ACT.Copy).then_inc(sem("h_hi_done"), 1)

        def v_hi2(g):
            act.wait_ge(sem("v2_turned"), 2 * g + 1)
            act.activation(v2_hi[:, 2:6, g * P:(g + 1) * P], ps[:, 4 + 2 * g, :].rearrange("p (t n) -> p t n", n=P),
                           ACT.Copy).then_inc(sem("v2_hi_done"), 1)
            act.wait_ge(sem("v2_turned"), 2 * g + 2)
            act.activation(v2_hi[:, 0:2, g * P:(g + 1) * P], ps[:, 5 + 2 * g, 0:CTX].rearrange("p (t n) -> p t n", n=P),
                           ACT.Copy).then_inc(sem("v2_hi_done"), 1)

        split_hi(0, 0, "kv2")
        k_squares(0)
        split_hi(0, 1, "kv2")
        k_tail(0)
        k_squares(1)
        split_hi(0, 2, "kv2")
        k_tail(1)
        split_hi(0, 3, "kv2")
        v_hi2(0)
        v_hi2(1)

        def q2_squares(m):
            act.wait_ge(used, done(BASE["q2"] + m))
            act.activation(tmp_s[:, m % 2, :], ps[:, m % 2, :], ACT.Square).then_inc(sem("q_sq"), 1)
            act.activation(qg[:, m % 2, :], ps[:, m % 2, :], ACT.Copy, scale=vcol("q_g")).then_inc(sem("q_gained"), 1)
            act.wait_ge(sem("q_gained"), m + 1)
            act.sem_inc(bank_free, 1)

        def q2_tail(m):
            act.wait_ge(sem("q_aux"), m + 1)
            act.activation(rstd[:], ps[:, 4, :], ACT.Sqrt, bias=eps128).then_inc(sem("q_rms"), 1)
            act.wait_ge(sem("q_val"), m + 1)
            act.activation(q2_hi[:, m, :], tmp_v[:, 0, :], ACT.Copy).then_inc(sem("q_hi_done"), 1)

        for m in range(H2 + 1):
            if m < H2:
                split_hi(*divmod(m, RING), "q2")
                q2_squares(m)
            if m:
                q2_tail(m - 1)

        def exp2(w, e):
            if w >= UNITS:
                return
            if w >= 2 and e == 0:
                act.wait_ge(sem("turned2"), PAIRS * (w - 1))
            act.wait_ge(sem("neg_max2"), 2 * w + e + 1)
            act.activation(probs[:, w % 2, e, :], s2(e)[:, 0:KEYS2], ACT.Exp, bias=neg_max[:, w % 2, e:e + 1],
                           accum_out=row_sum[:, w % 2, e:e + 1]).then_inc(sem("exp2_done"), 1)

        def hi_turn2(w, j):
            if 0 <= w < UNITS:
                r = PAIRS * w + j
                act.wait_ge(sem("turned2"), r + 1)
                if r >= 2:
                    act.wait_ge(sem("pv2_done"), r - 1)
                act.activation(pt2_hi[:, r % 2, :], ps[:, 4 + r % 2, :], ACT.Copy).then_inc(sem("pt2_hi_done"), 1)

        def o2_hi(h):
            act.wait_ge(sem("pv2_done"), 2 * PAIRS * (h + 1))
            act.activation(q2_hi[:, h, :], ps[:, 6 + h % 2, :], ACT.Copy).then_inc(sem("o2_hi_done"), 1)

        for w in range(UNITS + 2):
            hi_turn2(w - 1, 0)
            exp2(w, 0)
            hi_turn2(w - 1, 1)
            exp2(w, 1)
            hi_turn2(w - 1, 2)
            if w >= 2 and w % 2:
                o2_hi(w // 2 - 1)
        sigmoids("gate2")
        for m in range(8):
            i, u = divmod(m, RING)
            split_hi(i, u, "attn_out")
            if m == 2:
                for f in range(CONV_T):
                    act.wait_ge(sem("ln_centered"), f + 1)
                    act.wait_ge(sem("ln_sq_summed"), f - 1) if f > 1 else None
                    act.activation(tmp_s[:, f % 2, :], conv[:, f, :], ACT.Square).then_inc(sem("ln_sq"), 1)
            if m == 4:
                act.wait_ge(sem("ln_column"), 2)
                act.activation(rstd[:], ps[:, 4, :], ACT.Sqrt, scale=1.0 / (CONV_T * P), bias=eps).then_inc(sem("ln_rms"), 1)
            if m in (5, 6):
                for f in (2 * m - 10, 2 * m - 9):
                    act.wait_ge(sem("ln_scaled"), f + 1)
                    act.wait_ge(sem("yc_lo_done"), f - 1) if f > 1 else None
                    chain(act.activation(tmp_s[:, f % 2, :], tmp_v[:, f % 2, :], ACT.Silu, scale=vcol("ln_g", f),
                                         bias=vcol("ln_b", f)))
                    act.activation(yc_hi[:, f, :], tmp_s[:, f % 2, :], ACT.Copy).then_inc(sem("yc_hi_done"), 1)
        for u in range(RING):
            split_hi(0, u, "conv_out")
            act.wait_ge(sem("merged"), u + 1)
            act.activation(h_hi[:, 2 * u:2 * u + 2, :], tmp_v[:], ACT.Copy).then_inc(sem("merged_hi"), 1)
        only_split("out2")
        norm("norm_ffn", X, T, h_hi, 24)
        at = 0
        for c in range(3):
            g = f"up_{c}"

            def up(i, u, ahead):
                split_hi(i, u, g) if ahead else None
                act.wait_ge(used, i * RING + done(BASE[g] + u))
                b, f = u // 2, i * 2 + (8 * c + u // 2)
                if u % 2 == 0:
                    act.activation(tmp_s[:, b, :], ps[:, 0, :], ACT.Identity,
                                   scale=vec[:, bass.ds(f + (V_AT["ffn_w"] + FFN_T), 1)],
                                   bias=vec[:, bass.ds(f + V_AT["ffn_b"], 1)]).then_inc(sem("tap_mid"), 1)
                else:
                    act.wait_ge(sem("taps_done"), i * 2 + (8 * c + b + 1))
                    act.activation(tmp_s[:, b, :], tmp_s[:, b, :], ACT.Gelu_apprx_tanh).then_inc(sem("gelu_done"), 1)
                    act.wait_ge(sem("hidden_val"), i * 2 + (8 * c + b + 1))
                    act.activation(f_hi[:, bass.ds(i * 2 + b, 1), :], tmp_v[:, b:b + 1, :], ACT.Copy)\
                       .then_inc(sem("hidden_hi"), 1)
            loop(act, g, up)
            only_split(f"down_{c}")
        norm("final2", X, T, None, None)

    @block.vector
    def _(dve):
        step = {"n": 0}

        def chain(ins):
            ins.then_inc(chain_v, 1)
            step["n"] += 1
            dve.wait_ge(chain_v, step["n"])

        def split_lo(i, u, group):
            slot = (u + AHEAD) % RING
            dve.wait_ge(hi_ready, i * RING + (BASE[group] + u + AHEAD + 1))
            dve.tensor_tensor(w_lo[:, slot], raw[:, slot], w_hi[:, slot].bitcast(F32), ALU.subtract).then_inc(lo_ready, 1)

        def norm(name, src, N, dst_hi, dst_lo, gain, shift):
            k = NORMS[name]
            for f in range(KT):
                dve.wait_ge(n_sq, 8 * k + f + 1)
                if f == 0:
                    dve.tensor_copy(sq_acc[:, :N], tmp_s[:, 0, :N]).then_inc(n_acc, 1)
                else:
                    dve.wait_ge(n_acc, 8 * k + f)
                    dve.tensor_tensor(sq_acc[:, :N], sq_acc[:, :N], tmp_s[:, f % 2, :N], ALU.add).then_inc(n_acc, 1)
            dve.wait_ge(n_rms, NORMS[name] + 1)
            chain(dve.reciprocal(rstd[:, :N], rstd[:, :N]))
            if dst_hi is None:
                for f in range(KT):
                    dve.scalar_tensor_tensor(src[:, f, :], src[:, f, :], gain(f), rstd[:, :N], ALU.mult, ALU.mult)\
                       .then_inc(sem(name + "_tile"), 1)
                dve.wait_ge(sem(name + "_tile"), KT)
                return

            def value(f):
                if f >= 2:
                    dve.wait_ge(n_lo, 8 * split_norm[name] + f - 1)
                dve.scalar_tensor_tensor(tmp_v[:, f % 2, :N], src[:, f, :], gain(f), rstd[:, :N], ALU.mult, ALU.mult)\
                   .then_inc(n_val, 1)

            value(0)
            for f in range(KT):
                if f + 1 < KT:
                    value(f + 1)
                dve.wait_ge(n_hi, 8 * split_norm[name] + f + 1)
                if shift is None:
                    dve.tensor_tensor(dst_lo[:, f, :], tmp_v[:, f % 2, :N], dst_hi[:, f, :].bitcast(F32), ALU.subtract)\
                       .then_inc(n_lo, 1)
                else:
                    dve.scalar_tensor_tensor(dst_lo[:, f, :], tmp_v[:, f % 2, :N], mod[:, shift + f:shift + f + 1],
                                             dst_hi[:, f, :].bitcast(F32), ALU.add, ALU.subtract).then_inc(n_lo, 1)

        def gain_of(name):
            return lambda f: vcol(name, f)

        def split_out(group, hi, lo):
            def body(i, u, ahead):
                split_lo(i, u, group) if ahead else None
                dve.wait_ge(sem(group + "_hi"), i * RING + (u + 1))
                f = bass.ds(i * RING + u, 1)
                dve.tensor_tensor(lo[:, f, :], ps[:, u % 2:u % 2 + 1, :], hi[:, f, :].bitcast(F32), ALU.subtract)\
                   .then_inc(bank_free, 1)
            loop(dve, group, body)

        def only_split(group):
            loop(dve, group, lambda i, u, ahead: split_lo(i, u, group) if ahead else None)

        dve.sem_inc(used, RING)
        dve.sem_inc(bank_free, 2)
        for b in range(3):
            dve.memset(p_cmp[b][:], 0.0)
        dve.memset(blk_f[:].rearrange("p j (g c) -> p (j g) c", c=CW)[:, :, NCB:CW], 0.0).then_inc(setup, 1)
        for m in range(AHEAD):
            dve.wait_ge(hi_ready, m + 1)
            dve.tensor_tensor(w_lo[:, m], raw[:, m], w_hi[:, m].bitcast(F32), ALU.subtract).then_inc(lo_ready, 1)
        dve.wait_ge(in_small, 64)
        dve.wait_ge(sem("rel_out"), 1)
        dve.scalar_tensor_tensor(r8[:, 0:T], ps[0:8, 5, :], S8, r_mask[:, 0:T], ALU.mult, ALU.add).then_inc(sem("rel_rows"), 1)
        dve.scalar_tensor_tensor(r8[:, T:640], ps[0:8, 6, 0:P], S8, r_mask[:, T:640], ALU.mult, ALU.add)\
           .then_inc(sem("rel_rows"), 1)
        norm("norm1", X, T, h_hi, h_lo, gain_of("g_attn"), None)
        dve.wait_ge(sem("rel_stored"), 16)
        split_out("fox_qk", q_hi, q_lo)

        def v_copy(j, group, m):
            dve.wait_ge(used, done(BASE[group] + m))
            if j >= 2:
                dve.wait_ge(sem("v_turned"), j - 1)
            dve.tensor_copy(tmp_v[:, j % 2, :], ps[:, m % 2, :]).then_inc(bank_free, 1)

        def v_out(j, hi, lo):
            dve.wait_ge(sem("v_hi_done"), j + 1)
            dve.tensor_tensor(lo, ps[:, 4 + j % 2, :].rearrange("p (t n) -> p t n", n=P), hi.bitcast(F32), ALU.subtract)\
               .then_inc(sem("v_lo_done"), 1)

        def v_dst(v, j):
            return v[:, :, j * P:(j + 1) * P] if j < 4 else v[:, j - 4]

        for u in range(RING):
            split_lo(0, u, "fox_v")
            v_copy(u, "fox_v", u)
            v_out(u, v_dst(v_hi, u), v_dst(v_lo, u))
        for m in range(8):
            i, u = divmod(m, RING)
            split_lo(i, u, "nsa_kv")
            dve.wait_ge(used, done(BASE["nsa_kv"] + m))
            if m == 0:
                dve.tensor_scalar(zf[:], ps[0:8, 0, :], bf[:, 0:1], None, ALU.add).then_inc(sem("forget_z"), 1)
                dve.wait_ge(sem("forget_z"), 1)
                dve.wait_ge(sem("forget_ln"), 1)
                chain(dve.scalar_tensor_tensor(zf[:], zf[:], 0.0, lf_a[:], ALU.min, ALU.subtract))
                chain(dve.tensor_scalar(zf[:], zf[:], -S8, None, ALU.mult))
                chain(dve.memset(lf_a[:], 1.0))
                dve.tensor_tensor_scan(cum[:], lf_a[:], zf[:], 0.0, ALU.mult, ALU.add).then_inc(sem("c_summed"), 1)
                dve.wait_ge(sem("c_summed"), 1)
                dve.wait_ge(sem("c_turned"), 1)
                dve.tensor_scalar(c_q8[:], ps[:, 4, 0:32].rearrange("p (t h) -> p t h", h=8), -1.0, None, ALU.mult)\
                   .then_inc(sem("c_q_ready"), 1)
                dve.wait_ge(sem("c_q_ready"), 1)
                dve.sem_inc(bank_free, 1)
            if m == 1:
                dve.wait_ge(sem("gate_turned"), 1)
                dve.tensor_copy(gate_t[:], ps[:, 5, 0:96].rearrange("p (t h) -> p t h", h=24)).then_inc(bank_free, 1)
            if m in (2, 3):
                dve.wait_ge(sem("kn_hi_done"), m - 1)
                dve.tensor_tensor(kn_lo[:, m - 2, :], ps[:, m % 2, :], kn_hi[:, m - 2, :].bitcast(F32), ALU.subtract)\
                   .then_inc(bank_free, 1)
            if m in (4, 5):
                pe = vec[:, V_AT["pe_k" if m == 4 else "pe_v"]:V_AT["pe_k" if m == 4 else "pe_v"] + 16]
                for par in range(2):
                    for g in range(2):
                        src = bass.AP(tensor=ps[:].tensor, offset=64 * g * 8 * T + (m % 2) * T + par,
                                      ap=[[8 * T, 64], [2, 16], [CMP_STRIDE, NCB]])
                        dst = blk_f[64 * par:64 * par + 64, :, CW * g:CW * g + NCB]
                        pe_b = pe[64 * par:64 * par + 64, :].unsqueeze(2).to_broadcast([64, 16, NCB])
                        last = dve.tensor_tensor(dst, src, pe_b, ALU.add)
                last.then_inc(sem("blk_ready"), 1)
                dve.wait_ge(sem("blk_ready"), m - 3)
                dve.wait_ge(sem("blk_hi_done"), m - 3)
                dve.tensor_tensor(blk_lo[m - 4][:], blk_f[:], blk_hi[m - 4][:].bitcast(F32), ALU.subtract)\
                   .then_inc(sem("blk_lo_done"), 1)
                dve.wait_ge(sem("blk_lo_done"), m - 3)
                dve.sem_inc(bank_free, 1)
            if m in (6, 7):
                v_copy(m - 2, "nsa_kv", m)
                v_out(m - 2, v_dst(vn_hi, m - 2), v_dst(vn_lo, m - 2))
        split_out("nsa_q", nq_hi, nq_lo)
        for m in range(8):
            i, u = divmod(m, RING)
            split_lo(i, u, "cmp")
            if m == 3:
                dve.wait_ge(sem("kc_hi_done"), 2)
                for g in range(2):
                    last = dve.tensor_tensor(kc_lo[64 * g:64 * g + 64, :], ps[64 * g:64 * g + 64, 4, CW * g:CW * g + CW],
                                             kc_hi[64 * g:64 * g + 64, :].bitcast(F32), ALU.subtract)
                last.then_inc(bank_free, 4)
        dve.wait_ge(sem("vc_hi_done"), 1)
        dve.tensor_tensor(vc_lo[:], ps[0:CW, 5, 0:P], vc_hi[:].bitcast(F32), ALU.subtract)\
           .then_inc(bank_free, 4)
        dve.wait_ge(bank_free, BASE["cmp"] + 8 + 2)
        dve.sem_inc(sem("cmp_v_done"), 1)

        def score_room(s):
            kind = inst[s][0]
            if kind == "fox":
                dve.wait_ge(sem("fox_bias"), NT * (s + 1))
            else:
                n = load_of(s)
                dve.wait_ge(sem(f"bias_loaded_{n % 2}"), 16 * (n // 2 + 1))
                prev = [r for r in range(s) if (inst[r][0] == "cmp") == (kind == "cmp")]
                if len(prev) >= 3:
                    dve.wait_ge(sem("turned"), first_turn[prev[-3]] + len(turns(prev[-3])))

        def score(s, t):
            if s >= NI:
                return
            if t == 0:
                score_room(s)
            kind = inst[s][0]
            buf, w = scores_of(s, t)
            dve.wait_ge(sem("qk_done"), NT * s + t + 1)
            if kind == "fox":
                add = buf
            elif kind == "cmp":
                c0 = T - P - t * P + CMP_BLOCK - 1
                add = bias[:, load_of(s) % 2, c0:c0 + CMP_STRIDE * (w - 1) + 1:CMP_STRIDE]
            else:
                add = bias[:, load_of(s) % 2, T - w:T]
            dve.tensor_tensor_reduce(out=buf, in0=ps[:, t, 0:w], in1=add, scale=1.0 / S8, scalar=-3e38,
                                     op0=ALU.add, op1=ALU.max, accum_out=row_max[:, s % 3, t:t + 1])\
               .then_inc(sem("scored"), 1)
            if t == NT - 1:
                dve.wait_ge(sem("scored"), NT * (s + 1))
                dve.tensor_scalar(neg_max[:, s % 3, :], row_max[:, s % 3, :], -1.0, None, ALU.mult)\
                   .then_inc(sem("neg_max_ready"), 1)

        def normalize(s):
            if not 0 <= s < NI:
                return
            kind, p, half, b = inst[s]
            dve.wait_ge(sem("exp_done"), NT * (s + 1))
            f = factor[:, s % 3, :]
            chain(dve.reciprocal(f, row_sum[:, s % 3, :]))
            if b is not None:
                head = p + NSA_PAIRS * half
                f2 = factor2[:, s % 3, :]
                chain(dve.tensor_tensor(f2, f, gate_t[:, :, 3 * head + b], ALU.mult))
                f = f2
                if kind == "cmp":
                    chain(dve.tensor_tensor(f[:, 0:1], f[:, 0:1], cst[:, C_ROW:C_ROW + 1], ALU.mult))
            for t in range(NT):
                buf, w = scores_of(s, t)
                last = dve.tensor_scalar(buf, buf, f[:, t:t + 1], None, ALU.mult)
            last.then_inc(sem("normed"), 1)

        def lo_turn(s, j):
            if not turned(s, j):
                return
            rows, at, w = pt_shape(s, j)
            r = first_turn[s] + j
            dve.wait_ge(sem("pt_hi_done"), r + 1)
            dve.tensor_tensor(pt_lo[0:rows, at:at + w], ps[0:rows, 4 + r % 2, 0:w],
                              pt_hi[0:rows, at:at + w].bitcast(F32), ALU.subtract).then_inc(sem("pt_lo_done"), 1)

        def o_lo(s):
            p, half = pair_of(s), inst[s][2]
            r = slice(64 * half, 64 * half + 64)
            hi, lo = (q_hi, q_lo) if p < FOX_PAIRS else (nq_hi, nq_lo)
            dve.wait_ge(sem("o_hi_done"), head_of(s) + 1)
            dve.tensor_tensor(lo[r, p % 4, :], ps[r, 6 + half, :], hi[r, p % 4, :].bitcast(F32), ALU.subtract)\
               .then_inc(sem("o_done"), 1)

        for s in range(NI + 3):
            score(s, 0)
            score(s, 1)
            lo_turn(s - 2, 0)
            score(s, 2)
            score(s, 3)
            lo_turn(s - 2, 1)
            lo_turn(s - 2, 2)
            lo_turn(s - 2, 3)
            normalize(s - 1)
            if s >= 3 and head_end(s - 3):
                o_lo(s - 3)
        only_split("gate")
        dve.wait_ge(bank_free, BASE["branch"] + 2)

        def branch(i, u, ahead):
            split_lo(i, u, "branch") if ahead else None
            b = 2 * (u % 2)
            f = i * RING + u
            dve.wait_ge(used, i * RING + done(BASE["branch"] + u))
            dve.tensor_tensor(tmp_s[:, 0:1, :], ps[:, b:b + 1, :], gates[:, bass.ds(f, 1), :], ALU.mult)
            dve.tensor_tensor(tmp_s[:, 1:2, :], ps[:, b + 1:b + 2, :], gates[:, bass.ds(f + 8, 1), :], ALU.mult)\
               .then_inc(sem("branch_gated"), 1)
            dve.wait_ge(sem("branch_gated"), f + 1)
            dve.tensor_tensor(tmp_v[:, u % 2, :], tmp_s[:, 0, :], tmp_s[:, 1, :], ALU.add).then_inc(sem("branch_val"), 1)
            dve.wait_ge(sem("branch_hi"), f + 1)
            dve.tensor_tensor(h_lo[:, bass.ds(f, 1), :], tmp_v[:, u % 2:u % 2 + 1, :], h_hi[:, bass.ds(f, 1), :].bitcast(F32),
                              ALU.subtract).then_inc(bank_free, 1)
        loop(dve, "branch", branch)
        dve.wait_ge(sem("x_reloaded"), 16)

        def add_to_x(group, gain=None):
            def body(i, u, ahead):
                split_lo(i, u, group) if ahead else None
                dve.wait_ge(used, i * RING + done(BASE[group] + u))
                x = X[:, bass.ds(i * RING + u, 1), :]
                if gain is None:
                    dve.tensor_tensor(x, ps[:, u % 2:u % 2 + 1, :], x, ALU.add).then_inc(bank_free, 1)
                else:
                    dve.scalar_tensor_tensor(x, ps[:, u % 2:u % 2 + 1, :], mod[:, bass.ds(i * RING + (gain + u), 1)], x,
                                             ALU.mult, ALU.add).then_inc(bank_free, 1)
            loop(dve, group, body)
            dve.wait_ge(bank_free, BASE[group] + COUNT[group] + 2)
            dve.sem_inc(x_new, 8)

        add_to_x("out")
        norm("norm_mlp", X, T, h_hi, h_lo, gain_of("g_mlp"), None)
        dve.memset(mod_a[:], 0.0)
        dve.memset(mod_x[:], 0.0).then_inc(sem("mod_step"), 1)
        dve.wait_ge(sem("silu_c_ready"), 1)

        def mod_sums(c, part, i, u):
            if u != 1:
                return
            n = 4 * c + 2 * part
            dve.wait_ge(sem(f"w_mod_loaded_{part}"), i * 16 + 16 * (2 * c + 1))
            dve.wait_ge(sem("mod_step"), i + (n + 1))
            k = bass.ds(i + 2 * c, 1)
            acc = mod_a[:, part * 3 * D:(part + 1) * 3 * D]
            ins = dve.scalar_tensor_tensor(acc, wm[:, part], silu_c[:, k], acc, ALU.mult, ALU.add)
            if part == 0:
                ins.then_inc(sem("mod_x_step"), 1)
                ins = dve.scalar_tensor_tensor(mod_x[:], wm[:, 0, 0:2 * D], silu_c[:, bass.ds(i + 2 * c + 8, 1)], mod_x[:],
                                               ALU.mult, ALU.add)
            ins.then_inc(sem("mod_step"), 1)

        for c in range(4):
            g = f"ff1_{c}"

            def ff1(i, u, ahead):
                split_lo(i, u, g) if ahead else None
                mod_sums(c, 0, i, u)
                dve.wait_ge(sem("relu_done"), i * RING + (8 * c + u + 1))
                dve.tensor_tensor(tmp_v[:, u % 2, :], tmp_s[:, u % 2, :], tmp_s[:, u % 2, :], ALU.mult)\
                   .then_inc(sem("relu_squared"), 1)
                dve.wait_ge(sem("f_hi_done"), i * RING + (8 * c + u + 1))
                f = bass.ds(i * RING + u, 1)
                dve.tensor_tensor(f_lo[:, f, :], tmp_v[:, u % 2:u % 2 + 1, :], f_hi[:, f, :].bitcast(F32), ALU.subtract)\
                   .then_inc(bank_free, 1)
            loop(dve, g, ff1)
            g2 = f"ff2_{c}"

            def ff2(i, u, ahead):
                split_lo(i, u, g2) if ahead else None
                mod_sums(c, 1, i, u)
                dve.wait_ge(used, i * RING + done(BASE[g2] + u))
                x = X[:, bass.ds(i * RING + u, 1), :]
                dve.tensor_tensor(x, ps[:, u % 2:u % 2 + 1, :], x, ALU.add).then_inc(bank_free, 1)
            loop(dve, g2, ff2)
            dve.wait_ge(bank_free, BASE[g2] + COUNT[g2] + 2)
            dve.sem_inc(x_new, 8)
        norm("final1", X, T, None, None, gain_of("g_final"), None)
        dve.wait_ge(sem("mod_out"), 1)
        b_mod = vec[:, V_AT["b_mod"]:V_AT["b_mod"] + 48]
        dve.tensor_tensor(mod[:, 0:48], ps[:, 5, 0:48], b_mod, ALU.add)
        chain(dve.tensor_tensor(mod[:, 48:64], ps[:, 5, 48:64], b_mod[:, 0:16], ALU.add))
        chain(dve.tensor_scalar(gains[:, 0:8], mod[:, 8:16], 1.0, None, ALU.add))
        chain(dve.tensor_scalar(gains[:, 8:16], mod[:, 56:64], 1.0, None, ALU.add))
        chain(dve.tensor_scalar(gains[:, 16:24], mod[:, 32:40], 1.0, None, ALU.add))
        for n, name in enumerate(("norm1", "norm1", "norm2")):
            g = gains[:, 8 * n:8 * n + 8]
            chain(dve.tensor_tensor(g, g, vec[:, V_AT[name]:V_AT[name] + 8], ALU.mult))
        dve.sem_inc(sem("mod_summed"), 1)
        dve.sem_inc(x_new, 8)
        norm("norm2", X, T, h_hi, h_lo, lambda f: gains[:, f:f + 1], 0)
        dve.wait_ge(sem("ctx_rms"), 1)
        chain(dve.reciprocal(c_rstd[:], c_rstd[:]))
        for e in (0, VP - TAPS // 2):
            dve.memset(u_pad[:, :, e:e + TAPS // 2], 0.0)

        def glu(i, u, ahead):
            split_lo(i, u, "glu") if ahead else None
            n = i * RING + u
            dve.wait_ge(sem("ctx_lo"), n + 1)
            dve.scalar_tensor_tensor(tmp_v[:, u % 2:u % 2 + 1, :CTX], x_ctx[:, bass.ds(n, 1), :], gains[:, bass.ds(n + 8, 1)],
                                     c_rstd[:].unsqueeze(1), ALU.mult, ALU.mult).then_inc(sem("ctx_val"), 1)
            if u % 2:
                f = i * 2 + u // 2
                dve.wait_ge(sem("glu_sig"), f + 1)
                dve.tensor_tensor(u_pad[:, bass.ds(f, 1), TAPS // 2:TAPS // 2 + T], ps[:, 0:1, :], tmp_s[:, u // 2:u // 2 + 1, :],
                                  ALU.mult).then_inc(bank_free, 2)
            dve.wait_ge(sem("ctx_hi"), n + 1)
            dve.scalar_tensor_tensor(hc_lo[:, bass.ds(n, 1), :], tmp_v[:, u % 2:u % 2 + 1, :CTX], mod[:, bass.ds(n + 48, 1)],
                                     hc_hi[:, bass.ds(n, 1), :].bitcast(F32), ALU.add, ALU.subtract).then_inc(sem("ctx_lo"), 1)
        dve.sem_inc(sem("ctx_lo"), 1)
        loop(dve, "glu", glu)
        dve.wait_ge(bank_free, BASE["glu"] + 8 + 2)

        def k_tail(u):
            dve.wait_ge(sem("h_rms"), 2 * u + 2)
            chain(dve.reciprocal(rstd[:], rstd[:]))
            chain(dve.tensor_tensor(tmp_v[:, 1, :], ps[:, 5, :], cst[:, C_SIN:C_SIN + T], ALU.mult))
            chain(dve.tensor_tensor(tmp_v[:, 0, :], kg[:, 0, :], cst[:, C_COS:C_COS + T], ALU.mult))
            chain(dve.tensor_tensor(tmp_v[:, 0, :], tmp_v[:, 0, :], tmp_v[:, 1, :], ALU.add))
            dve.tensor_tensor(tmp_v[:, 0, :], tmp_v[:, 0, :], rstd[:], ALU.mult).then_inc(sem("h_val"), 1)
            chain(dve.reciprocal(sq_acc[:, :CTX], sq_acc[:, :CTX]))
            dve.tensor_tensor(tmp_v[:, 1, :CTX], kg[:, 1, :CTX], sq_acc[:, :CTX], ALU.mult).then_inc(sem("h_val"), 1)
            dve.wait_ge(sem("h_hi_done"), 2 * u + 1)
            dve.tensor_tensor(k2_lo[:, u, CTX:KEYS2], tmp_v[:, 0, :], k2_hi[:, u, CTX:KEYS2].bitcast(F32), ALU.subtract)\
               .then_inc(sem("h_lo_done"), 1)
            dve.wait_ge(sem("h_hi_done"), 2 * u + 2)
            dve.tensor_tensor(k2_lo[:, u, 0:CTX], tmp_v[:, 1, :CTX], k2_hi[:, u, 0:CTX].bitcast(F32), ALU.subtract)\
               .then_inc(sem("h_lo_done"), 1)
            dve.wait_ge(sem("h_lo_done"), 2 * u + 2)

        def v_copy2(g):
            dve.wait_ge(used, done(BASE["kv2"] + 2 + g))
            if g:
                dve.wait_ge(sem("v2_turned"), 2)
            dve.tensor_copy(tmp_v[:, 0, :], ps[:, g, :])
            dve.tensor_copy(tmp_v[:, 1, 0:CTX], ps[:, 2 + g, 0:CTX]).then_inc(bank_free, 1)

        def v_lo2(g):
            cols = slice(g * P, (g + 1) * P)
            for n, (bank, tiles, N) in enumerate([(4 + 2 * g, slice(2, 6), T), (5 + 2 * g, slice(0, 2), CTX)]):
                dve.wait_ge(sem("v2_hi_done"), 2 * g + n + 1)
                dve.tensor_tensor(v2_lo[:, tiles, cols], ps[:, bank, 0:N].rearrange("p (t n) -> p t n", n=P),
                                  v2_hi[:, tiles, cols].bitcast(F32), ALU.subtract).then_inc(sem("v2_lo_done"), 1)

        split_lo(0, 0, "kv2")
        split_lo(0, 1, "kv2")
        k_tail(0)
        split_lo(0, 2, "kv2")
        k_tail(1)
        split_lo(0, 3, "kv2")
        v_copy2(0)
        v_copy2(1)
        v_lo2(0)
        v_lo2(1)

        def q2_tail(m):
            if m:
                dve.wait_ge(sem("q_lo_done"), m)
            dve.wait_ge(sem("q_aux"), m + 1)
            dve.tensor_tensor(tmp_v[:, 1, :], ps[:, 5, :], cst[:, C_SIN:C_SIN + T], ALU.mult)
            dve.tensor_tensor(tmp_v[:, 0, :], qg[:, m % 2, :], cst[:, C_COS:C_COS + T], ALU.mult).then_inc(sem("q_cos"), 1)
            dve.wait_ge(sem("q_rms"), m + 1)
            dve.reciprocal(rstd[:], rstd[:]).then_inc(sem("q_inv"), 1)
            dve.wait_ge(sem("q_cos"), m + 1)
            dve.tensor_tensor(tmp_v[:, 0, :], tmp_v[:, 0, :], tmp_v[:, 1, :], ALU.add).then_inc(sem("q_turned"), 1)
            dve.wait_ge(sem("q_turned"), m + 1)
            dve.tensor_tensor(tmp_v[:, 0, :], tmp_v[:, 0, :], rstd[:], ALU.mult).then_inc(sem("q_val"), 1)
            dve.wait_ge(sem("q_hi_done"), m + 1)
            dve.tensor_tensor(q2_lo[:, m, :], tmp_v[:, 0, :], q2_hi[:, m, :].bitcast(F32), ALU.subtract)\
               .then_inc(sem("q_lo_done"), 1)

        for m in range(H2 + 1):
            if m < H2:
                split_lo(*divmod(m, RING), "q2")
            if m:
                q2_tail(m - 1)

        def row_max2(w, e):
            if w < UNITS:
                dve.wait_ge(sem("qk2_done"), 2 * w + e + 1)
                dve.tensor_reduce(neg_max[:, w % 2, e:e + 1], s2(e)[:, 0:KEYS2], AX, ALU.max, negate=True)\
                   .then_inc(sem("neg_max2"), 1)

        def lo_turn2(w, j):
            if 0 <= w < UNITS:
                r = PAIRS * w + j
                dve.wait_ge(sem("pt2_hi_done"), r + 1)
                dve.tensor_tensor(pt2_lo[:, r % 2, :], ps[:, 4 + r % 2, :], pt2_hi[:, r % 2, :].bitcast(F32), ALU.subtract)\
                   .then_inc(sem("pt2_lo_done"), 1)

        def normalize2(w):
            if w >= UNITS:
                return
            dve.wait_ge(sem("exp2_done"), 2 * (w + 1))
            chain(dve.reciprocal(factor[:, w % 2, 0:2], row_sum[:, w % 2, 0:2]))
            for e in range(2):
                dve.tensor_scalar(probs[:, w % 2, e, :], probs[:, w % 2, e, :], factor[:, w % 2, e:e + 1], None,
                                  ALU.mult).then_inc(sem("normed2"), 1)

        def o2_lo(h):
            dve.wait_ge(sem("o2_hi_done"), h + 1)
            dve.tensor_tensor(q2_lo[:, h, :], ps[:, 6 + h % 2, :], q2_hi[:, h, :].bitcast(F32), ALU.subtract)\
               .then_inc(sem("o2_done"), 1)

        for w in range(UNITS + 2):
            row_max2(w, 0)
            lo_turn2(w - 1, 0)
            row_max2(w, 1)
            lo_turn2(w - 1, 1)
            lo_turn2(w - 1, 2)
            normalize2(w)
            if w >= 2 and w % 2:
                o2_lo(w // 2 - 1)

        def gate2(i, u, ahead):
            split_lo(i, u, "gate2") if ahead else None
            if u == 0:
                dve.wait_ge(sem("pool_tap"), i * POOL_TAPS + POOL_TAPS)
            x0 = DVE_TAPS // RING * u
            for tap in range(x0, x0 + DVE_TAPS // RING):
                if tap:
                    dve.wait_ge(sem("conv_step"), i * DVE_TAPS + tap)
                dve.scalar_tensor_tensor(conv[:, bass.ds(i, 1), :], u_pad[:, bass.ds(i, 1), tap:tap + T],
                                         vec[:, bass.ds(i * TAPS + (V_AT["dw_w"] + tap), 1)],
                                         conv[:, bass.ds(i, 1), :], ALU.mult, ALU.add).then_inc(sem("conv_step"), 1)
        loop(dve, "gate2", gate2)
        dve.wait_ge(sem("conv_step"), CONV_T * DVE_TAPS)
        dve.wait_ge(bank_free, BASE["attn_out"] + 2)

        def ln_sums():
            chain(dve.tensor_tensor(sq_acc[:], conv[:, 0, :], conv[:, 1, :], ALU.add))
            chain(dve.tensor_tensor(sq_acc[:], sq_acc[:], conv[:, 2, :], ALU.add))
            dve.tensor_tensor(sq_acc[:], sq_acc[:], conv[:, 3, :], ALU.add).then_inc(sem("ln_summed"), 1)

        def ln_center():
            dve.wait_ge(sem("ln_column"), 1)
            chain(dve.tensor_scalar(rstd[:], ps[:, 4, :], 1.0 / (CONV_T * P), None, ALU.mult))
            for f in range(CONV_T):
                dve.tensor_tensor(conv[:, f, :], conv[:, f, :], rstd[:], ALU.subtract).then_inc(sem("ln_centered"), 1)

        def ln_squares():
            for f in range(CONV_T):
                dve.wait_ge(sem("ln_sq"), f + 1)
                if f == 0:
                    dve.tensor_copy(sq_acc[:], tmp_s[:, 0, :]).then_inc(sem("ln_sq_summed"), 1)
                else:
                    dve.wait_ge(sem("ln_sq_summed"), f)
                    dve.tensor_tensor(sq_acc[:], sq_acc[:], tmp_s[:, f % 2, :], ALU.add).then_inc(sem("ln_sq_summed"), 1)

        def ln_scale(f):
            if f > 1:
                dve.wait_ge(sem("yc_hi_done"), f - 1)
            dve.tensor_tensor(tmp_v[:, f % 2, :], conv[:, f, :], rstd[:], ALU.mult).then_inc(sem("ln_scaled"), 1)

        def ln_lo(f):
            dve.wait_ge(sem("yc_hi_done"), f + 1)
            dve.tensor_tensor(yc_lo[:, f, :], tmp_s[:, f % 2, :], yc_hi[:, f, :].bitcast(F32), ALU.subtract)\
               .then_inc(sem("yc_lo_done"), 1)

        for m in range(8):
            i, u = divmod(m, RING)
            split_lo(i, u, "attn_out")
            if m == 0:
                ln_sums()
            if m == 2:
                ln_center()
                ln_squares()
            if m == 5:
                dve.wait_ge(sem("ln_rms"), 1)
                chain(dve.reciprocal(rstd[:], rstd[:]))
                ln_scale(0)
                ln_scale(1)
            if m == 6:
                ln_lo(0)
                ln_lo(1)
                ln_scale(2)
                ln_scale(3)
            if m == 7:
                ln_lo(2)
                ln_lo(3)
            dve.wait_ge(used, done(BASE["attn_out"] + m))
            dve.tensor_tensor(gates[:, m, :], ps[:, m % 2, :], gates[:, m, :], ALU.mult).then_inc(bank_free, 1)
        dve.wait_ge(bank_free, BASE["conv_out"] + 2)
        for u in range(RING):
            split_lo(0, u, "conv_out")
            b, two = 2 * (u % 2), slice(2 * u, 2 * u + 2)
            dve.wait_ge(used, done(BASE["conv_out"] + u))
            chain(dve.tensor_tensor(tmp_s[:], ps[:, b:b + 2, :], gates[:, 8 + 2 * u:10 + 2 * u, :], ALU.mult))
            dve.tensor_tensor(tmp_v[:], tmp_s[:], gates[:, two, :], ALU.add).then_inc(sem("merged"), 1)
            dve.wait_ge(sem("merged_hi"), u + 1)
            dve.tensor_tensor(h_lo[:, two, :], tmp_v[:], h_hi[:, two, :].bitcast(F32), ALU.subtract).then_inc(bank_free, 1)
        add_to_x("out2", gain=16)
        norm("norm_ffn", X, T, h_hi, h_lo, lambda f: gains[:, 16 + f:17 + f], 24)
        for c in range(3):
            g = f"up_{c}"

            def up(i, u, ahead):
                split_lo(i, u, g) if ahead else None
                b, n, F = u // 2, i * 2 + (8 * c + u // 2), FFN_T
                if u % 2 == 0:
                    dve.wait_ge(sem("tap_mid"), n + 1)
                    dve.scalar_tensor_tensor(tmp_s[:, b, 1:T], ps[:, 0, 0:T - 1], vec[:, bass.ds(n + V_AT["ffn_w"], 1)],
                                             tmp_s[:, b, 1:T], ALU.mult, ALU.add).then_inc(sem("tap_left"), 1)
                    dve.wait_ge(sem("tap_left"), n + 1)
                    dve.scalar_tensor_tensor(tmp_s[:, b, 0:T - 1], ps[:, 0, 1:T],
                                             vec[:, bass.ds(n + (V_AT["ffn_w"] + 2 * F), 1)],
                                             tmp_s[:, b, 0:T - 1], ALU.mult, ALU.add).then_inc(sem("taps_done"), 1)
                    dve.wait_ge(sem("taps_done"), n + 1)
                    dve.sem_inc(bank_free, 1)
                else:
                    dve.wait_ge(sem("gelu_done"), n + 1)
                    dve.tensor_tensor(tmp_v[:, b, :], ps[:, 1, :], tmp_s[:, b, :], ALU.mult).then_inc(sem("hidden_val"), 1)
                    dve.wait_ge(sem("hidden_hi"), n + 1)
                    f = bass.ds(i * 2 + b, 1)
                    dve.tensor_tensor(f_lo[:, f, :], tmp_v[:, b:b + 1, :], f_hi[:, f, :].bitcast(F32), ALU.subtract)\
                       .then_inc(bank_free, 1)
            loop(dve, g, up)
            add_to_x(f"down_{c}", gain=40)
        norm("final2", X, T, None, None, gain_of("final2"), None)

    @block.tensor
    def _(pe):
        ident, ones = cst[:, C_ID:C_ID + P], cst[:, C_ONE:C_ONE + P]

        def panel(i, u, group, out, blocks, hi, lo, N=T, ready=None, last=True, first=True):
            if first:
                pe.wait_ge(lo_ready, i * RING + (BASE[group] + u + 1))
                pe.wait_ge(bank_free, i * RING + (BASE[group] + u + 1))
            for b, k in blocks:
                if ready is not None and u == 0:
                    pe.wait_ge(*ready(k))
                start, stop = (b, k) == blocks[0], (b, k) == blocks[-1]
                pe.matmul(out, w_hi[:, u, b, :], hi[:, k, :N], start=start, stop=False)
                pe.matmul(out, w_hi[:, u, b, :], lo[:, k, :N], start=False, stop=False)
                ins = pe.matmul(out, w_lo[:, u, b, :], hi[:, k, :N], start=False, stop=stop)
            if last:
                ins.then_inc(used, 1)

        ALL = [(k, k) for k in range(KT)]

        def panels(group, ready=None, hi=h_hi, lo=h_lo, blocks=ALL):
            loop(pe, group, lambda i, u, ahead: panel(i, u, group, ps[:, u % 2, :], blocks, hi, lo, ready=ready))

        def column_sum(name, N):
            pe.wait_ge(n_acc, 8 * (NORMS[name] + 1))
            pe.matmul(ps[:, 4, :N], ones, sq_acc[:, :N], start=True, stop=True).then_inc(n_sum, 1)

        def normed(name):
            return lambda k: (n_lo, 8 * split_norm[name] + k + 1)

        def evacuated(group, per=1):
            return lambda k: (bank_free, BASE[group] + per * (k + 1) + 2)

        pe.wait_ge(in_c, 16)
        pe.wait_ge(in_small, 64)
        pe.matmul(ps[0:8, 5, :], tab[:], hot[:, 0:T], start=True, stop=True)
        pe.matmul(ps[0:8, 6, 0:P], tab[:], hot[:, T:640], start=True, stop=True).then_inc(sem("rel_out"), 1)
        column_sum("norm1", T)
        panels("fox_qk", normed("norm1"))

        def turn_v(j, group, m):
            pe.wait_ge(bank_free, BASE[group] + m + 1 + 2)
            if j >= 2:
                pe.wait_ge(sem("v_lo_done"), j - 1)
            for t in range(NT):
                ins = pe.transpose(ps[:, 4 + j % 2, t * P:(t + 1) * P], tmp_v[:, j % 2, t * P:(t + 1) * P], ident)
            ins.then_inc(sem("v_turned"), 1)

        for u in range(RING):
            panel(0, u, "fox_v", ps[:, u % 2, :], ALL, h_hi, h_lo)
            if u:
                turn_v(u - 1, "fox_v", u - 1)
        turn_v(3, "fox_v", 3)
        for m in range(8):
            i, u = divmod(m, RING)
            panel(i, u, "nsa_kv", ps[:, m % 2, :], ALL, h_hi, h_lo)
            if m == 0:
                pe.wait_ge(sem("v_lo_done"), 4)
                pe.wait_ge(sem("c_summed"), 1)
                for t in range(NT):
                    ins = pe.transpose(ps[:, 4, 8 * t:8 * t + 8], cum[:, t * P:(t + 1) * P], ident[0:8, 0:8])
                ins.then_inc(sem("c_turned"), 1)
            if m == 1:
                pe.wait_ge(sem("gate_n"), 1)
                for t in range(NT):
                    ins = pe.transpose(ps[:, 5, 24 * t:24 * t + 24], sig_n[:, t * P:(t + 1) * P], ident[0:24, 0:24])
                ins.then_inc(sem("gate_turned"), 1)
            if m == 7:
                turn_v(4, "nsa_kv", 6)
        turn_v(5, "nsa_kv", 7)
        panels("nsa_q")
        pe.wait_ge(bank_free, BASE["cmp"] + 2)
        pe.wait_ge(sem("blk_lo_done"), 2)
        pe.wait_ge(sem("v_lo_done"), 6)
        for m in range(8):
            i, u = divmod(m, RING)
            kv = m // 4
            pe.wait_ge(lo_ready, BASE["cmp"] + m + 1)
            for b in range(8):
                jp, f = 4 * u + b // 2, b % 2
                out = ps[:, kv, 64 * f:64 * f + 64]
                x_hi, x_lo = blk_hi[kv][:, jp, :], blk_lo[kv][:, jp, :]
                end = u == 3 and b >= 6
                pe.matmul(out, w_hi[:, u, b, :], x_hi, start=(u == 0 and b == 0), stop=False, skip_group_check=True)
                pe.matmul(out, w_hi[:, u, b, :], x_lo, start=False, stop=False, skip_group_check=True)
                ins = pe.matmul(out, w_lo[:, u, b, :], x_hi, start=False, stop=end, skip_group_check=True)
            ins.then_inc(used, 1)
            if m == 3:
                pe.wait_ge(sem("w2_loaded"), 32)
                pe.wait_ge(sem("cmp_hidden"), 1)
                for f in range(2):
                    ins = pe.matmul(ps[:, 4, 0:64], w2k[:, f, :], hid_c[:, f, :], start=f == 0, stop=f == 1)
                ins.then_inc(sem("cmp_k_out"), 1)
        pe.wait_ge(sem("cmp_hidden"), 2)
        for g in range(2):
            for f in range(2):
                ins = pe.matmul(ps[0:CW, 5, 64 * g:64 * g + 64], hid_c[:, f, CW * g:CW * g + CW], w2v[:, f, :],
                                start=f == 0, stop=f == 1)
        ins.then_inc(sem("cmp_v_out"), 1)

        def keys_of(s):
            kind, p, half, b = inst[s]
            r = slice(64 * half, 64 * half + 64)
            if kind == "fox":
                return q_hi[r, p, :], q_lo[r, p, :], q_hi[r, 4 + p, :], q_lo[r, 4 + p, :]
            if kind == "cmp":
                return nq_hi[r, p, :], nq_lo[r, p, :], kc_hi[r, :], kc_lo[r, :]
            n = 0 if kind == "slc" else 1
            return nq_hi[r, p, :], nq_lo[r, p, :], kn_hi[r, n, :], kn_lo[r, n, :]

        def qk(s, t):
            if s >= NI:
                return
            qh, ql, kh, kl = keys_of(s)
            fox = inst[s][0] == "fox"
            if s:
                pe.wait_ge(sem("scored"), NT * (s - 1) + t + 1)
            w = 8 * t + 8 if inst[s][0] == "cmp" else (t + 1) * P
            out = ps[:, t, 0:w]
            c = slice(t * P, (t + 1) * P)
            pe.matmul(out, qh[:, c], kh[:, 0:w], start=True, stop=False, skip_group_check=True)
            pe.matmul(out, qh[:, c], kl[:, 0:w], start=False, stop=False, skip_group_check=True)
            ins = pe.matmul(out, ql[:, c], kh[:, 0:w], start=False, stop=not fox, skip_group_check=True)
            if fox:
                ins = pe.matmul(ps[:, t, w - P:w], cst_r[:, 0:P], cst_r[:, P:2 * P], start=False, stop=True,
                                skip_group_check=True)
            ins.then_inc(sem("qk_done"), 1)

        def turn_p(s, j):
            if not turned(s, j):
                return
            if j == 0:
                pe.wait_ge(sem("normed"), s + 1)
            r = first_turn[s] + j
            if r >= 2:
                pe.wait_ge(sem("pt_lo_done"), r - 1)
            if inst[s][0] == "cmp":
                for t in range(NT):
                    ins = pe.transpose(ps[0:CW, 4 + r % 2, t * P:(t + 1) * P], p_cmp[big_of[s]][:, t, :], ident)
            else:
                for t in range(j, NT):
                    ins = pe.transpose(ps[:, 4 + r % 2, (t - j) * P:(t - j + 1) * P],
                                       sb[big_of[s]][:, SB_AT[t] + j * P:SB_AT[t] + (j + 1) * P], ident)
            ins.then_inc(sem("turned"), 1)

        def pv(s, j):
            if not turned(s, j):
                return
            kind, p, half, b = inst[s]
            r = first_turn[s] + j
            rows, at, w = pt_shape(s, j)
            if kind == "fox":
                vh, vl = v_hi[:, j, p * P:(p + 1) * P], v_lo[:, j, p * P:(p + 1) * P]
            elif kind == "cmp":
                vh, vl = vc_hi[:], vc_lo[:]
            else:
                n = 0 if kind == "slc" else 1
                vh, vl = vn_hi[:, n, j], vn_lo[:, n, j]
            out = ps[:, 6 + half, T - w:T]
            begin = head_start(s) and j == 0
            end = head_end(s) and j == turns(s)[-1]
            if begin and head_of(s) >= 2:
                pe.wait_ge(sem("o_done"), head_of(s) - 1)
            pe.wait_ge(sem("pt_lo_done"), r + 1)
            pe.matmul(out, vh, pt_hi[0:rows, at:at + w], start=begin, stop=False, skip_group_check=True)
            pe.matmul(out, vh, pt_lo[0:rows, at:at + w], start=False, stop=False, skip_group_check=True)
            pe.matmul(out, vl, pt_hi[0:rows, at:at + w], start=False, stop=end, skip_group_check=True)\
              .then_inc(sem("pv_done"), 1)

        pe.wait_ge(sem("cmp_v_done"), 1)
        pe.wait_ge(setup, 3)
        for s in range(NI + 2):
            qk(s, 0)
            qk(s, 1)
            turn_p(s - 2, 0)
            qk(s, 2)
            qk(s, 3)
            turn_p(s - 2, 1)
            pv(s - 2, 0)
            turn_p(s - 2, 2)
            pv(s - 2, 1)
            turn_p(s - 2, 3)
            pv(s - 2, 2)
            pv(s - 2, 3)
        pe.wait_ge(sem("o_done"), 16)
        panels("gate")
        pe.wait_ge(bank_free, BASE["branch"] + 2)

        def branch(i, u, ahead):
            b = 2 * (u % 2)
            panel(i, u, "branch", ps[:, b, :], [(k, k) for k in range(4)], q_hi, q_lo, last=False)
            panel(i, u, "branch", ps[:, b + 1, :], [(4 + k, k) for k in range(4)], nq_hi, nq_lo, first=False)
        loop(pe, "branch", branch)
        panels("out", evacuated("branch"))
        column_sum("norm_mlp", T)
        for c in range(4):
            panels(f"ff1_{c}", normed("norm_mlp"))
            panels(f"ff2_{c}", evacuated(f"ff1_{c}"), f_hi, f_lo)
        column_sum("final1", T)
        pe.wait_ge(sem("mod_step"), 17)
        for f in range(64):
            src = mod_a[:, f * P:(f + 1) * P] if f < 48 else mod_x[:, (f - 48) * P:(f - 47) * P]
            ins = pe.matmul(ps[:, 5, f:f + 1], src, ones[:, 0:1], start=True, stop=True)
        ins.then_inc(sem("mod_out"), 1)
        pe.wait_ge(sem("ctx_acc"), KT)
        pe.wait_ge(sem("mod_summed"), 1)
        pe.matmul(ps[:, 5, :CTX], ones, c_acc[:], start=True, stop=True).then_inc(sem("ctx_sum"), 1)
        column_sum("norm2", T)
        panels("glu", normed("norm2"))
        pe.wait_ge(bank_free, BASE["kv2"] + 2)
        pe.wait_ge(sem("ctx_lo"), KT + 1)
        rot = cst[:, C_ROT:C_ROT + P]

        def kv_panel(u):
            panel(0, u, "kv2", ps[:, u % 2, :], ALL, h_hi, h_lo, last=False)
            panel(0, u, "kv2", ps[:, 2 + u % 2, 0:CTX], ALL, hc_hi, hc_lo, N=CTX, first=False)

        def k_aux(u):
            pe.wait_ge(sem("h_gained"), 2 * u + 2)
            if u:
                pe.wait_ge(sem("h_lo_done"), 2)
            pe.matmul(ps[:, 4, :], ones, tmp_s[:, 0, :], start=True, stop=True)
            pe.matmul(ps[:, 6, :CTX], ones, tmp_s[:, 1, :CTX], start=True, stop=True)
            pe.matmul(ps[:, 5, :], rot, kg[:, 0, :], start=True, stop=True).then_inc(sem("h_aux"), 1)

        def turn_v2(g):
            pe.wait_ge(bank_free, BASE["kv2"] + 2 + g + 1 + 2)
            for n, (bank, tiles) in enumerate([(4 + 2 * g, T // P), (5 + 2 * g, CTX // P)]):
                for t in range(tiles):
                    ins = pe.transpose(ps[:, bank, t * P:(t + 1) * P], tmp_v[:, n, t * P:(t + 1) * P], ident)
                ins.then_inc(sem("v2_turned"), 1)

        kv_panel(0)
        kv_panel(1)
        k_aux(0)
        kv_panel(2)
        k_aux(1)
        kv_panel(3)
        pe.wait_ge(sem("h_lo_done"), 4)
        turn_v2(0)
        turn_v2(1)
        pe.wait_ge(bank_free, BASE["q2"] + 2)
        pe.wait_ge(sem("v2_lo_done"), 4)

        def q_aux(m):
            pe.wait_ge(sem("q_gained"), m + 1)
            if m:
                pe.wait_ge(sem("q_val"), m)
            pe.matmul(ps[:, 4, :], ones, tmp_s[:, m % 2, :], start=True, stop=True)
            pe.matmul(ps[:, 5, :], rot, qg[:, m % 2, :], start=True, stop=True).then_inc(sem("q_aux"), 1)

        for m in range(H2 + 1):
            if m < H2:
                i, u = divmod(m, RING)
                panel(i, u, "q2", ps[:, u % 2, :], ALL, h_hi, h_lo)
            if m:
                q_aux(m - 1)

        def qk2(w, e):
            if w >= UNITS:
                return
            if w:
                pe.wait_ge(sem("exp2_done"), 2 * (w - 1) + e + 1)
            h = w // 2
            g, t = h // (H2 // KV2), 2 * (w % 2) + e
            c = slice(t * P, (t + 1) * P)
            for k0, n in ((0, T), (T, KEYS2 - T)):
                out = s2(e)[:, k0:k0 + n]
                pe.matmul(out, q2_hi[:, h, c], k2_hi[:, g, k0:k0 + n], start=True, stop=False)
                pe.matmul(out, q2_hi[:, h, c], k2_lo[:, g, k0:k0 + n], start=False, stop=False)
                ins = pe.matmul(out, q2_lo[:, h, c], k2_hi[:, g, k0:k0 + n], start=False, stop=True)
            ins.then_inc(sem("qk2_done"), 1)

        def turn_p2(w, j):
            if w < 0:
                return
            if j == 0:
                pe.wait_ge(sem("normed2"), 2 * (w + 1))
            r = PAIRS * w + j
            if r >= 2:
                pe.wait_ge(sem("pt2_lo_done"), r - 1)
            for n in range(4):
                k, e = 2 * j + n // 2, n % 2
                ins = pe.transpose(ps[:, 4 + r % 2, n * P:(n + 1) * P], probs[:, w % 2, e, k * P:(k + 1) * P], ident)
            ins.then_inc(sem("turned2"), 1)

        def pv2(w, j):
            if w < 0:
                return
            r, h = PAIRS * w + j, w // 2
            if h >= 2 and j == 0:
                pe.wait_ge(sem("o2_done"), h - 1)
            g = h // (H2 // KV2)
            out = ps[:, 6 + h % 2, 2 * P * (w % 2):2 * P * (w % 2 + 1)]
            c = slice(g * P, (g + 1) * P)
            pe.wait_ge(sem("pt2_lo_done"), r + 1)
            for n in range(2):
                k, q = 2 * j + n, slice(2 * P * n, 2 * P * (n + 1))
                pe.matmul(out, v2_hi[:, k, c], pt2_hi[:, r % 2, q], start=k == 0, stop=False, skip_group_check=True)
                pe.matmul(out, v2_hi[:, k, c], pt2_lo[:, r % 2, q], start=False, stop=False, skip_group_check=True)
                ins = pe.matmul(out, v2_lo[:, k, c], pt2_hi[:, r % 2, q], start=False, stop=k == 5, skip_group_check=True)
            ins.then_inc(sem("pv2_done"), 1)

        pe.wait_ge(sem("q_lo_done"), H2)
        for w in range(UNITS + 1):
            qk2(w, 0)
            turn_p2(w - 1, 0)
            qk2(w, 1)
            turn_p2(w - 1, 1)
            pv2(w - 1, 0)
            turn_p2(w - 1, 2)
            pv2(w - 1, 1)
            pv2(w - 1, 2)
        pe.wait_ge(sem("o2_done"), H2)
        panels("gate2")
        pe.wait_ge(bank_free, BASE["attn_out"] + 2)
        for m in range(8):
            i, u = divmod(m, RING)
            panel(i, u, "attn_out", ps[:, u % 2, :], ALL, q2_hi, q2_lo)
            if m == 1:
                pe.wait_ge(sem("ln_summed"), 1)
                pe.matmul(ps[:, 4, :], ones, sq_acc[:], start=True, stop=True).then_inc(sem("ln_column"), 1)
            if m == 4:
                pe.wait_ge(sem("ln_sq_summed"), CONV_T)
                pe.matmul(ps[:, 4, :], ones, sq_acc[:], start=True, stop=True).then_inc(sem("ln_column"), 1)
        pe.wait_ge(bank_free, BASE["conv_out"] + 2)
        pe.wait_ge(sem("yc_lo_done"), CONV_T)
        for u in range(RING):
            b = 2 * (u % 2)
            panel(0, u, "conv_out", ps[:, b, :], [(k, k) for k in range(4)], yc_hi, yc_lo, last=False)
            panel(0, u, "conv_out", ps[:, b + 1, :], [(4 + k, k) for k in range(4)], yc_hi, yc_lo, first=False)
        panels("out2", lambda k: (bank_free, BASE["conv_out"] + k // 2 + 1 + 2))
        column_sum("norm_ffn", T)
        for c in range(3):
            panels(f"up_{c}", normed("norm_ffn"))
            panels(f"down_{c}", evacuated(f"up_{c}", 2), f_hi, f_lo, [(k, k) for k in range(HID[c])])
        column_sum("final2", T)

    ctx.close()


def host_layout(i):
    f = np.float32
    g = {k: np.asarray(v) for k, v in i.items()}

    def tiles(w, k=KT):
        n = w.shape[1] // P
        return w.reshape(k, P, n, P).transpose(2, 1, 0, 3)

    def few(w):
        z = np.zeros((D, P), f)
        z[:, :w.shape[1]] = w
        return tiles(z)

    w_in = g["w_in"][0]
    cut = np.cumsum([512, 512, 512, 8, 512, 128, 128, 128, 128, 128, 128, 24, D, D])[:-1]
    fq, fk, fv, fl, nq, kc, vc, ks, vs, kw, vw, ng, ga, gb = np.split(w_in, cut, axis=1)
    nq = nq.reshape(D, 2, 4, 64).transpose(0, 2, 1, 3).reshape(D, 512)
    br_n = g["w_br_nsa"][0].reshape(2, 4, 64, D).transpose(1, 0, 2, 3).reshape(512, D)
    cmp = [g[n][0].reshape(4, 4, P, 2, P).transpose(0, 2, 1, 3, 4).reshape(4, P, 8, P) for n in ("cmp_w1_k", "cmp_w1_v")]
    part = {"fox_qk": tiles(np.concatenate([fq, fk], 1)), "fox_v": tiles(fv),
            "nsa_kv": np.concatenate([few(fl), few(ng), tiles(ks), tiles(kw), tiles(kc), tiles(vc), tiles(vs), tiles(vw)]),
            "nsa_q": tiles(nq), "cmp": np.concatenate(cmp), "gate": tiles(np.concatenate([ga, gb], 1)),
            "branch": np.concatenate([tiles(g["w_br_fox"][0], 4), tiles(br_n, 4)], 2), "out": tiles(g["w_out"][0])}
    for c in range(4):
        part[f"ff1_{c}"] = tiles(g["w_ff1"][0][:, c * D:(c + 1) * D])
        part[f"ff2_{c}"] = tiles(g["w_ff2"][0][c * D:(c + 1) * D])
    w_in2 = g["w_in_2"][0]
    q, k, v, ua, ub, g2 = np.split(w_in2, np.cumsum([D, 256, 256, 512, 512]), axis=1)
    part["kv2"] = tiles(np.concatenate([k, v], 1))
    part["glu"] = np.stack([tiles(ua), tiles(ub)], 1).reshape(8, P, KT, P)
    part["q2"], part["gate2"] = tiles(q), tiles(g2)
    co = tiles(g["w_conv_out_2"][0], 4)
    part["conv_out"] = co.reshape(4, 2, P, 4, P).transpose(0, 2, 1, 3, 4).reshape(4, P, 8, P)
    part["attn_out"], part["out2"] = tiles(g["w_attn_out_2"][0]), tiles(g["w_out_2"][0])
    up, down, at = g["w_up_2"][0], g["w_down_2"][0], 0
    hidden = FFN_T * P
    for c, n in enumerate(HID):
        a_, b_ = (up[:, o + at * P:o + (at + n) * P] for o in (0, hidden))
        part[f"up_{c}"] = np.stack([tiles(a_), tiles(b_)], 1).reshape(2 * n, P, KT, P)
        d = np.zeros((D, D), f)
        d[:n * P] = down[at * P:(at + n) * P]
        part[f"down_{c}"] = tiles(d)
        at += n
    panels = np.concatenate([part[n] for n, _ in GROUPS])
    assert panels.shape == (PANELS, P, 8, P), panels.shape

    consts = np.zeros((P, C_ALL), f)
    consts[:, C_ID:C_ID + P] = np.eye(P)
    consts[:, C_ONE:C_ONE + P] = 1.0
    r = np.arange(0, P, 2)
    consts[r + 1, C_ROT + r] = -1.0
    consts[r, C_ROT + r + 1] = 1.0
    tok, half = np.arange(T), 64
    inv = 10000.0 ** (-np.arange(0, half, 2, dtype=f) / f(half))
    ang = np.concatenate([(tok // 64).astype(f)[:, None] * inv, (tok % 64).astype(f)[:, None] * inv], 1).astype(f)
    consts[:, C_COS:C_COS + T] = np.repeat(np.cos(ang).T, 2, 0)
    consts[:, C_SIN:C_SIN + T] = np.repeat(np.sin(ang).T, 2, 0)
    p = np.arange(P)
    consts[:, C_MASK:C_MASK + P] = np.where(p[None, :] > p[:, None], S8 * NEG, 0.0)
    consts[:, C_ROW] = p >= CMP_BLOCK - 1
    consts[:, C_EPS], consts[:, C_EPS + 1] = EPS, EPS * P
    dist = T - 1 - np.arange(640)
    n = np.maximum(dist, 0)
    nf = np.maximum(n, 16).astype(f)
    log_b = 16 + (np.log(nf / f(16)) / f(np.log(8.0)) * f(16)).astype(np.int32)
    bucket = np.where(n < 16, n, np.minimum(log_b, 31))
    onehot = (bucket[None, :] == np.arange(32)[:, None]).astype(f)
    r_mask = np.broadcast_to(np.where(dist < 0, S8 * NEG, 0.0).astype(f), (8, 640))

    vec = np.zeros((P, V_ALL), f)

    def put(name, v):
        vec[:, V_AT[name]:V_AT[name] + v.shape[1]] = v

    def by_tile(v):
        return v.reshape(-1, P).T
    for name, src in [("g_attn", "g_attn"), ("g_mlp", "g_mlp"), ("g_final", "g_final"), ("norm1", "norm1_g_2"),
                      ("norm2", "norm2_g_2"), ("final2", "final_g_2"), ("ln_g", "conv_ln_g_2"), ("ln_b", "conv_ln_b_2"),
                      ("dw_b", "conv_dw_b_2"), ("ffn_b", "ffn_dw_b_2"), ("q_g", "q_norm_g_2"), ("k_g", "k_norm_g_2"),
                      ("c", "c_2"), ("c_ctx", "c_ctx_2"), ("b_mod", "b_mod_2")]:
        put(name, by_tile(g[src].reshape(-1)))
    put("dw_w", g["conv_dw_w_2"][0].reshape(TAPS, CONV_T, P).transpose(2, 1, 0).reshape(P, -1))
    put("ffn_w", g["ffn_dw_w_2"][0].reshape(3, FFN_T, P).transpose(2, 0, 1).reshape(P, -1))
    put("pe_k", g["cmp_pe_k"][0].reshape(16, P).T)
    put("pe_v", g["cmp_pe_v"][0].reshape(16, P).T)
    w2k = g["cmp_w2_k"][0].reshape(2, P, 64).transpose(1, 0, 2)
    return {
        "panels": panels, "x": g["x"][0].T.reshape(KT, P, T).transpose(1, 0, 2), "consts": consts, "vectors": vec,
        "onehot": onehot, "r_mask": r_mask, "table": g["rel_bias_table"], "b_forget": g["b_forget"].reshape(8, 1),
        "w2k": np.concatenate([w2k, w2k], 2), "w2v": g["cmp_w2_v"][0].reshape(2, P, 64).transpose(1, 0, 2),
        "ctx": g["ctx_2"][0].T.reshape(KT, P, CTX).transpose(1, 0, 2), "w_mod": g["w_mod_2"][0].reshape(KT, P, 6 * D),
    }


def kernel(**inputs):
    import concourse.bacc as bacc
    from concourse.bass_utils import run_bass_kernel_spmd

    nc = bacc.Bacc("TRN2", target_bir_lowering=False, num_devices=1)
    arrays, aps = {}, {}
    for name, v in host_layout(inputs).items():
        v = np.ascontiguousarray(v)
        arrays[f"in_{name}"] = v
        aps[name] = nc.dram_tensor(f"in_{name}", v.shape, mybir.dt.from_np(v.dtype), kind="ExternalInput").ap()
    out = nc.dram_tensor("out_dram", (P, KT, T), F32, kind="ExternalOutput").ap()
    build(nc, aps, out)
    r = run_bass_kernel_spmd(nc, [arrays], core_ids=[0])
    y = r.results[0]["out_dram"]
    return np.ascontiguousarray(np.transpose(y, (2, 1, 0)).reshape(1, T, D))
```
